# Optimizing a Trainium2 kernel written in Bass

```python
import math
import jax, jax.numpy as jnp
from jax import lax
import numpy as np

D_MODEL = 2048
BATCH = 1
SEQ = 256
DEPTH = 1

MEM_LEN = 256
LRU_WIDTH = 2048
LRU_BLOCKS = 16
LRU_BLOCK_DIM = LRU_WIDTH // LRU_BLOCKS
CONV_WIDTH = 4
LRU_C = 8.0
DIFF_HEADS = 8
DIFF_HEAD_DIM = 128
DIFF_V_DIM = 2 * DIFF_HEAD_DIM
DIFF_QK_WIDTH = DIFF_HEADS * 2 * DIFF_HEAD_DIM
DIFF_WIDTH = DIFF_HEADS * DIFF_V_DIM
ROT_DIM = DIFF_HEAD_DIM // 4
ROPE_THETA = 500000.0
Q_BLOCK = 128
MEM_HEADS = 4
MEM_HEAD_DIM = 384
MEM_WIDTH = MEM_HEADS * MEM_HEAD_DIM
N_BRANCHES = 3
PEER_HEADS = 8
N_KEYS = 128
N_EXPERTS = N_KEYS * N_KEYS
PEER_TOPK = 16
PEER_KEY_DIM = 256
PEER_SUBKEY_DIM = PEER_KEY_DIM // 2
PEER_TOKEN_BLOCK = 128
DEEPNORM_ALPHA = (2 * DEPTH) ** 0.25
DEEPNORM_BETA = (8 * DEPTH) ** -0.25
LN_EPS = 1e-5
IN_SPLITS = (LRU_WIDTH, LRU_WIDTH, DIFF_QK_WIDTH, DIFF_QK_WIDTH, DIFF_WIDTH, MEM_WIDTH, N_BRANCHES * D_MODEL)
IN_WIDTH = sum(IN_SPLITS)

kernel_name = "hybrid_rglru_diffattn_memxattn_peer"

def split_columns(z, sizes):
    out, start = [], 0
    for s in sizes:
        out.append(z[..., start:start + s])
        start += s
    return out

def layer_norm(x, g, b):
    xf = x.astype(jnp.float32)
    mu = jnp.mean(xf, axis=-1, keepdims=True)
    var = jnp.mean(jnp.square(xf - mu), axis=-1, keepdims=True)
    return ((xf - mu) * lax.rsqrt(var + LN_EPS) * g.astype(jnp.float32) + b.astype(jnp.float32)).astype(x.dtype)

def rms_norm(x, g):
    xf = x.astype(jnp.float32)
    ms = jnp.mean(jnp.square(xf), axis=-1, keepdims=True)
    return (xf * lax.rsqrt(ms + LN_EPS) * g.astype(jnp.float32)).astype(x.dtype)

def partial_rotary(t, positions):
    half = ROT_DIM // 2
    inv_freq = ROPE_THETA ** (-jnp.arange(half, dtype=jnp.float32) / half)
    ang = positions.astype(jnp.float32)[..., None] * inv_freq
    cos = jnp.cos(ang)[:, :, None, None, :]
    sin = jnp.sin(ang)[:, :, None, None, :]
    t1 = t[..., :half].astype(jnp.float32)
    t2 = t[..., half:ROT_DIM].astype(jnp.float32)
    rot = jnp.concatenate([t1 * cos - t2 * sin, t2 * cos + t1 * sin], axis=-1).astype(t.dtype)
    return jnp.concatenate([rot, t[..., ROT_DIM:]], axis=-1)

def centred_depthwise_conv(x, w, b):
    y = lax.conv_general_dilated(
        x, w[:, None, :], window_strides=(1,), padding=[(1, 2)],
        dimension_numbers=("NWC", "WIO", "NWC"), feature_group_count=LRU_WIDTH)
    return y + b

def _linear_combine(e1, e2):
    a1, b1 = e1
    a2, b2 = e2
    return a1 * a2, a2 * b1 + b2

def rg_lru_direction(xc, w_a, b_a, w_i, b_i, lam, reverse):
    B, S, _ = xc.shape
    xb = xc.reshape(B, S, LRU_BLOCKS, LRU_BLOCK_DIM)
    r = jax.nn.sigmoid(jnp.einsum("bsni,nij->bsnj", xb, w_a).reshape(B, S, LRU_WIDTH) + b_a)
    i = jax.nn.sigmoid(jnp.einsum("bsni,nij->bsnj", xb, w_i).reshape(B, S, LRU_WIDTH) + b_i)
    log_a = -LRU_C * r.astype(jnp.float32) * jax.nn.softplus(-lam.astype(jnp.float32))
    a = jnp.exp(log_a)
    u = jnp.sqrt(-jnp.expm1(2.0 * log_a)) * (i * xc).astype(jnp.float32)
    if reverse:
        a, u = jnp.flip(a, axis=1), jnp.flip(u, axis=1)
    _, h = lax.associative_scan(_linear_combine, (a, u), axis=1)
    if reverse:
        h = jnp.flip(h, axis=1)
    return h.astype(xc.dtype)

def diff_attention(q, k, v, lam, lam_init, subln_w):
    B, S = q.shape[0], q.shape[1]
    nb = S // Q_BLOCK
    scale = DIFF_HEAD_DIM ** -0.5
    qb = q.reshape(B, nb, Q_BLOCK, DIFF_HEADS, 2, DIFF_HEAD_DIM).transpose(1, 0, 2, 3, 4, 5)

    def one_block(qblk):
        s = jnp.einsum("bqhjd,bkhjd->bhjqk", qblk, k).astype(jnp.float32) * scale
        p = jax.nn.softmax(s, axis=-1)
        attn = (p[:, :, 0] - lam * p[:, :, 1]).astype(v.dtype)
        return jnp.einsum("bhqk,bkhd->bqhd", attn, v)

    o = lax.map(one_block, qb)
    o = o.transpose(1, 0, 2, 3, 4).reshape(B, S, DIFF_HEADS, DIFF_V_DIM)
    o = rms_norm(o, subln_w) * (1.0 - lam_init)
    return o.reshape(B, S, DIFF_WIDTH)

def memory_attention(q, mk, mv):
    B, S = q.shape[0], q.shape[1]
    s = jnp.einsum("bshd,bmhd->bhsm", q, mk).astype(jnp.float32) * (MEM_HEAD_DIM ** -0.5)
    p = jax.nn.softmax(s, axis=-1).astype(q.dtype)
    return jnp.einsum("bhsm,bmhd->bshd", p, mv).reshape(B, S, MEM_WIDTH)

def peer_ffn(x, w_q, sub_keys, u_table, v_table):
    B, S, D = x.shape
    T = B * S
    xt = x.reshape(T, D)
    q = (xt @ w_q).reshape(T, PEER_HEADS, 2, PEER_SUBKEY_DIM)
    s = jnp.einsum("thjc,hjnc->thjn", q, sub_keys).astype(jnp.float32)
    s_top, i_top = lax.top_k(s, PEER_TOPK)
    cand = s_top[:, :, 0, :, None] + s_top[:, :, 1, None, :]
    cand = cand.reshape(T, PEER_HEADS, PEER_TOPK * PEER_TOPK)
    best, c = lax.top_k(cand, PEER_TOPK)
    i1 = jnp.take_along_axis(i_top[:, :, 0], c // PEER_TOPK, axis=-1)
    i2 = jnp.take_along_axis(i_top[:, :, 1], c % PEER_TOPK, axis=-1)
    experts = (i1 * N_KEYS + i2).reshape(T, PEER_HEADS * PEER_TOPK)
    gates = jax.nn.softmax(best, axis=-1).reshape(T, PEER_HEADS * PEER_TOPK)
    nb = T // PEER_TOKEN_BLOCK

    def one_block(args):
        xb, eb, gb = args
        u = u_table[eb]
        h = jnp.einsum("td,tkd->tk", xb, u).astype(jnp.float32)
        w = (gb * jax.nn.gelu(h, approximate=False)).astype(xb.dtype)
        return jnp.einsum("tk,tkd->td", w, v_table[eb])

    out = lax.map(one_block, (xt.reshape(nb, PEER_TOKEN_BLOCK, D),
                              experts.reshape(nb, PEER_TOKEN_BLOCK, -1),
                              gates.reshape(nb, PEER_TOKEN_BLOCK, -1)))
    return out.reshape(B, S, D)

def setup_inputs(seed: int = 0) -> dict:
    key = jax.random.key(seed)
    ks = jax.random.split(key, 32)
    f32 = jnp.float32
    nrm = lambda k, shape, s: jax.random.normal(k, shape, f32) * s
    L = DEPTH
    x = nrm(ks[0], (BATCH, SEQ, D_MODEL), 1.0)
    mem = nrm(ks[1], (BATCH, MEM_LEN, D_MODEL), 1.0)
    positions = jnp.broadcast_to(jnp.arange(SEQ, dtype=jnp.int32), (BATCH, SEQ))
    col_scale = jnp.concatenate([
        jnp.ones((2 * LRU_WIDTH + 2 * DIFF_QK_WIDTH,), f32),
        jnp.full((DIFF_WIDTH,), DEEPNORM_BETA, f32),
        jnp.ones((MEM_WIDTH + N_BRANCHES * D_MODEL,), f32)])
    w_in = nrm(ks[2], (L, D_MODEL, IN_WIDTH), D_MODEL ** -0.5) * col_scale
    b_gate = nrm(ks[3], (L, N_BRANCHES * D_MODEL), 0.01)
    conv_w = nrm(ks[4], (L, CONV_WIDTH, LRU_WIDTH), CONV_WIDTH ** -0.5)
    conv_b = nrm(ks[5], (L, LRU_WIDTH), 0.01)
    lru_w_a = nrm(ks[6], (L, 2, LRU_BLOCKS, LRU_BLOCK_DIM, LRU_BLOCK_DIM), LRU_BLOCK_DIM ** -0.5)
    lru_b_a = nrm(ks[7], (L, 2, LRU_WIDTH), 0.01)
    lru_w_i = nrm(ks[8], (L, 2, LRU_BLOCKS, LRU_BLOCK_DIM, LRU_BLOCK_DIM), LRU_BLOCK_DIM ** -0.5)
    lru_b_i = nrm(ks[9], (L, 2, LRU_WIDTH), 0.01)
    a_c = jax.random.uniform(ks[10], (L, 2, LRU_WIDTH), f32, 0.9, 0.999)
    a0 = a_c ** (1.0 / LRU_C)
    lru_lambda = jnp.log(a0) - jnp.log1p(-a0)
    diff_lambda = nrm(ks[11], (L, 4, DIFF_HEAD_DIM), 0.1)
    diff_subln = 1.0 + nrm(ks[12], (L, DIFF_V_DIM), 0.01)
    kv_scale = jnp.concatenate([jnp.ones((MEM_WIDTH,), f32), jnp.full((MEM_WIDTH,), DEEPNORM_BETA, f32)])
    w_mem_kv = nrm(ks[13], (L, D_MODEL, 2 * MEM_WIDTH), D_MODEL ** -0.5) * kv_scale
    w_branch_lru = nrm(ks[14], (L, LRU_WIDTH, D_MODEL), DEEPNORM_BETA * LRU_WIDTH ** -0.5)
    w_branch_diff = nrm(ks[15], (L, DIFF_WIDTH, D_MODEL), DEEPNORM_BETA * DIFF_WIDTH ** -0.5)
    w_branch_mem = nrm(ks[16], (L, MEM_WIDTH, D_MODEL), DEEPNORM_BETA * MEM_WIDTH ** -0.5)
    w_out = nrm(ks[17], (L, D_MODEL, D_MODEL), DEEPNORM_BETA * D_MODEL ** -0.5)
    ln1_g = 1.0 + nrm(ks[18], (L, D_MODEL), 0.01)
    ln1_b = nrm(ks[19], (L, D_MODEL), 0.01)
    peer_w_q = nrm(ks[20], (L, D_MODEL, PEER_HEADS * PEER_KEY_DIM), D_MODEL ** -0.5)
    peer_sub_keys = nrm(ks[21], (L, PEER_HEADS, 2, N_KEYS, PEER_SUBKEY_DIM), PEER_SUBKEY_DIM ** -0.5)
    peer_u = nrm(ks[22], (L, N_EXPERTS, D_MODEL), D_MODEL ** -0.5)
    peer_v = nrm(ks[23], (L, N_EXPERTS, D_MODEL), DEEPNORM_BETA)
    ln2_g = 1.0 + nrm(ks[24], (L, D_MODEL), 0.01)
    ln2_b = nrm(ks[25], (L, D_MODEL), 0.01)
    return {"x": x, "mem": mem, "positions": positions, "w_in": w_in, "b_gate": b_gate,
            "conv_w": conv_w, "conv_b": conv_b, "lru_w_a": lru_w_a, "lru_b_a": lru_b_a,
            "lru_w_i": lru_w_i, "lru_b_i": lru_b_i, "lru_lambda": lru_lambda,
            "diff_lambda": diff_lambda, "diff_subln": diff_subln, "w_mem_kv": w_mem_kv,
            "w_branch_lru": w_branch_lru, "w_branch_diff": w_branch_diff, "w_branch_mem": w_branch_mem,
            "w_out": w_out, "ln1_g": ln1_g, "ln1_b": ln1_b, "peer_w_q": peer_w_q,
            "peer_sub_keys": peer_sub_keys, "peer_u": peer_u, "peer_v": peer_v,
            "ln2_g": ln2_g, "ln2_b": ln2_b}

def reference(x, mem, positions, w_in, b_gate, conv_w, conv_b, lru_w_a, lru_b_a, lru_w_i, lru_b_i,
              lru_lambda, diff_lambda, diff_subln, w_mem_kv, w_branch_lru, w_branch_diff, w_branch_mem,
              w_out, ln1_g, ln1_b, peer_w_q, peer_sub_keys, peer_u, peer_v, ln2_g, ln2_b):
    B, S, D = x.shape
    M = mem.shape[1]
    for l in range(DEPTH):
        lam_init = 0.8 - 0.6 * math.exp(-0.3 * l)
        z = x @ w_in[l]
        a_gate_in, a_x, d_q, d_k, d_v, m_q, g = split_columns(z, IN_SPLITS)
        xc = centred_depthwise_conv(a_x, conv_w[l], conv_b[l])
        h = (rg_lru_direction(xc, lru_w_a[l, 0], lru_b_a[l, 0], lru_w_i[l, 0], lru_b_i[l, 0], lru_lambda[l, 0], False)
             + rg_lru_direction(xc, lru_w_a[l, 1], lru_b_a[l, 1], lru_w_i[l, 1], lru_b_i[l, 1], lru_lambda[l, 1], True))
        br_a = jax.nn.gelu(a_gate_in, approximate=False) * h
        q = partial_rotary(d_q.reshape(B, S, DIFF_HEADS, 2, DIFF_HEAD_DIM), positions)
        k = partial_rotary(d_k.reshape(B, S, DIFF_HEADS, 2, DIFF_HEAD_DIM), positions)
        v = d_v.reshape(B, S, DIFF_HEADS, DIFF_V_DIM)
        lp = diff_lambda[l].astype(jnp.float32)
        lam = jnp.exp(jnp.sum(lp[0] * lp[1])) - jnp.exp(jnp.sum(lp[2] * lp[3])) + lam_init
        br_d = diff_attention(q, k, v, lam, lam_init, diff_subln[l])
        mkv = mem @ w_mem_kv[l]
        mk = mkv[..., :MEM_WIDTH].reshape(B, M, MEM_HEADS, MEM_HEAD_DIM)
        mv = mkv[..., MEM_WIDTH:].reshape(B, M, MEM_HEADS, MEM_HEAD_DIM)
        br_m = memory_attention(m_q.reshape(B, S, MEM_HEADS, MEM_HEAD_DIM), mk, mv)
        gates = jax.nn.sigmoid(g + b_gate[l]).reshape(B, S, N_BRANCHES, D)
        merged = (gates[:, :, 0] * (br_a @ w_branch_lru[l])
                  + gates[:, :, 1] * (br_d @ w_branch_diff[l])
                  + gates[:, :, 2] * (br_m @ w_branch_mem[l]))
        x = layer_norm(DEEPNORM_ALPHA * x + merged @ w_out[l], ln1_g[l], ln1_b[l])
        y = peer_ffn(x, peer_w_q[l], peer_sub_keys[l], peer_u[l], peer_v[l])
        x = layer_norm(DEEPNORM_ALPHA * x + y, ln2_g[l], ln2_b[l])
    return x


_drawn_inputs = setup_inputs


def setup_inputs(seed=0):
    import zlib

    import numpy as np

    out = dict(_drawn_inputs(seed))
    spreads = {}
    factors = {'b_gate': 8.0,
     'lru_b_a': 45.781,
     'lru_b_i': 43.099,
     'diff_subln': 6.827,
     'ln2_g': 32.19,
     'ln2_b': 30.971,
     'conv_b': 2.799}
    for name, (base, spread) in spreads.items():
        noise = np.random.default_rng([zlib.crc32(name.encode()), seed]).standard_normal(out[name].shape)
        drawn = base * np.exp(spread * noise) if base else spread * noise
        out[name] = __import__('jax').numpy.asarray(drawn.astype(out[name].dtype))
    for name, factor in factors.items():
        out[name] = (out[name] * factor).astype(out[name].dtype)
    return out
```

```python
import math
from contextlib import ExitStack

import concourse.bass as bass
from concourse import mybir

f32, f32r, i32, u32 = mybir.dt.float32, mybir.dt.float32r, mybir.dt.int32, mybir.dt.uint32
ALU = mybir.AluOpType
ACT = mybir.ActivationFunctionType
AX = mybir.AxisListType
ds = bass.ds

P = 128
D = 2048
TOK = 256
NT = TOK // P
KT = D // P
BLK = 128
WIDE = 512
KQ = 4
UNIT = KT * BLK
HALF = UNIT // 2
MEM = 256
MEM_HEADS, MEM_DIM = 4, 384
MEM_W = MEM_HEADS * MEM_DIM
MB = MEM_W // P
MC = MEM_DIM // P
HEADS, HD = 8, 128
VD = 2 * HD
ROT, HALF_ROT, THETA = 32, 16, 500000.0
QSCALE, MSCALE = HD ** -0.5, MEM_DIM ** -0.5
LAM_INIT = 0.8 - 0.6 * math.exp(0.0)
ALPHA = 2.0 ** 0.25
EPS = 1e-5
PH, NK, TOPK = 8, 128, 16
GROUPS, GC = 4, 32
GT = 8
LOWEST = -3.0e38

COL_GATE, COL_AX, COL_Q, COL_K, COL_V = 0, 2048, 4096, 6144, 8192
COL_MQ, COL_G = 10240, 11776
PRE = 4
M_LRU = 0
M_MK = M_LRU + 2 * KT
M_MV = M_MK + MB
M_MQ = M_MV + MEM_W // WIDE * 4
M_MA = M_MQ + MB
M_D = M_MA + 2 * KT
M_MM = M_D + HEADS // 2 * 12
M_MD = M_MM + 2 * KT
M_OUT = M_MD + 2 * KT
M_WQ = M_OUT + D // WIDE * 4
M_EXP = M_WQ + 2 * PH
PAIRS = KT + MB + 2 * HEADS + PH


def layer(nc, x, mem, pos, w_in, b_gate, conv_w, conv_b, lru_w_a, lru_b_a, lru_w_i, lru_b_i, lru_lambda,
          diff_lambda, diff_subln, w_mem_kv, w_lru, w_diff, w_mem, w_out, ln1_g, ln1_b, w_q, sub_keys,
          u_tab, v_tab, ln2_g, ln2_b, out):
    ctx = ExitStack()
    with ctx:
        def sb(name, shape, dt=f32, stack=ctx):
            return stack.enter_context(nc.sbuf_tensor(name, shape, dt))

        def sem(name):
            return ctx.enter_context(nc.semaphore(name))

        raw = [sb(f"raw{s}", [P, UNIT]) for s in range(2)]
        hi = [sb(f"hi{s}", [P, UNIT], f32r) for s in range(2)]
        lo = [sb(f"lo{s}", [P, UNIT], f32r) for s in range(2)]
        ident = sb("ident", [P, P])
        ones1 = sb("ones1", [1, 1])
        vrow = sb("vrow", [P, 2, P])
        vec = sb("vec", [P, 2, P])
        mom = sb("mom", [P, 4, 2])
        nmom = sb("nmom", [P, 2])
        base = ExitStack()

        A = ExitStack()
        brh = sb("brh", [P, KT, TOK], f32r, A)
        brl = sb("brl", [P, KT, TOK], f32r, A)
        S0 = ExitStack()
        rtmp = sb("rtmp", [ROT, 4, TOK], f32, S0)
        posi = sb("posi", [ROT, TOK], i32, S0)
        lp = sb("lp", [P, 4, P], f32, S0)
        S0.close()
        merged = sb("merged", [P, KT, TOK], f32, A)
        mq = sb("mq", [P, MB, TOK], f32, A)
        L = ExitStack()
        axp = sb("axp", [P, TOK + 3], f32, L)
        xc = sb("xc", [P, TOK], f32, L)
        gelu_gate = sb("gelu_gate", [P, TOK], f32, L)
        lru_w = sb("lru_w", [P, 2, 2, P], f32, L)
        t_r = sb("t_r", [P, 2, TOK], f32, L)
        t_i = sb("t_i", [P, 2, TOK], f32, L)
        dec = sb("dec", [P, 2, TOK], f32, L)
        th = sb("th", [P, 2, TOK], f32, L)
        wsq = sb("wsq", [P, 2, TOK], f32, L)
        sq = sb("sq", [P, 2, TOK], f32, L)
        uin = sb("uin", [P, 2, TOK], f32, L)
        hst = sb("hst", [P, 2, TOK], f32, L)
        L.close()
        M = ExitStack()
        mk = sb("mk", [P, MB, MEM], f32, M)
        mv = sb("mv", [P, 2, MEM_W], f32, M)
        M.close()
        S = ExitStack()
        qk = sb("qk", [P, 8, TOK], f32, S)
        vv = sb("vv", [P, 2, WIDE], f32, S)
        ex = sb("ex", [P, 2, 2, 2, TOK], f32, S)
        at = sb("at", [P, 2, 2, TOK], f32, S)
        S.close()
        pad = sb("pad", [P, 24 * 256], f32, A)
        xh = sb("xh", [P, KT, TOK], f32r, A)
        xl = sb("xl", [P, KT, TOK], f32r, A)
        Z1 = ExitStack()
        memh = sb("memh", [P, KT, MEM], f32r, Z1)
        meml = sb("meml", [P, KT, MEM], f32r, Z1)
        Z1.close()
        Z2 = ExitStack()
        brmh = sb("brmh", [P, MB, TOK], f32r, Z2)
        brml = sb("brml", [P, MB, TOK], f32r, Z2)
        Z4 = ExitStack()
        mqs = sb("mqs", [P, MC, TOK], f32, Z4)
        mvs = sb("mvs", [P, 2, MEM_DIM], f32, Z4)
        pm = sb("pm", [P, 2, MEM], f32, Z4)
        Z4.close()
        rsh = sb("rsh", [ROT, 4, TOK], f32, Z2)
        Z2.close()
        Z3 = ExitStack()
        mh = sb("mh", [P, KT, TOK], f32r, Z3)
        ml = sb("ml", [P, KT, TOK], f32r, Z3)
        Z3.close()
        padz = sb("padz", [P, 32 * 256], f32, A)
        gt = sb("gt", [P, TOK], f32, A)
        pt = sb("pt", [P, TOK], f32, A)
        pmT = sb("pmT", [P, 2, TOK], f32, A)
        cosT = sb("cosT", [ROT, TOK], f32, A)
        sinT = sb("sinT", [ROT, TOK], f32, A)
        ifr = sb("ifr", [1, ROT], f32, A)
        ifc = sb("ifc", [ROT, 1], f32, A)
        sgn = sb("sgn", [ROT, 1], f32, A)
        lsum = sb("lsum", [P, 2], f32, A)
        lame = sb("lame", [P, 2], f32, A)
        nlam = sb("nlam", [P, 1], f32, A)
        hb = sb("hb", [P, 64], f32, A)
        sp = sb("sp", [P, 32], f32, A)
        nsp = sb("nsp", [P, 32], f32, A)
        spt = sb("spt", [P, 4, 32], f32, A)
        mx = sb("mx", [P, 8], f32, A)
        nmx = sb("nmx", [P, 8], f32, A)
        zs = sb("zs", [P, 8], f32, A)
        rz = sb("rz", [P, 8], f32, A)
        ssq = sb("ssq", [P, 4], f32, A)
        rstd = sb("rstd", [P, 4], f32, A)
        A.close()

        B = ExitStack()
        hbuf = sb("hbuf", [P, GC, TOK], f32, B)
        gbuf = sb("gbuf", [P, GC, TOK], f32, B)
        acc = sb("acc", [P, NT, D], f32, B)
        res = sb("res", [P, NT, D], f32, B)
        x1h = sb("x1h", [P, KT, TOK], f32r, B)
        x1l = sb("x1l", [P, KT, TOK], f32r, B)
        top_v = sb("top_v", [P, PH, 2, NT, TOPK], f32, B)
        top_i = sb("top_i", [P, PH, 2, NT, TOPK], f32, B)
        cand = sb("cand", [P, TOPK, TOPK], f32, B)
        cand2 = sb("cand2", [P, TOPK * TOPK], f32, B)
        best = sb("best", [P, TOPK], f32, B)
        nbest = sb("nbest", [P, 1], f32, B)
        zb = sb("zb", [P, 1], f32, B)
        rzb = sb("rzb", [P, 1], f32, B)
        eb = sb("eb", [P, TOPK], f32, B)
        ci = sb("ci", [P, TOPK], u32, B)
        ca = sb("ca", [P, TOPK], u32, B)
        cb = sb("cb", [P, TOPK], u32, B)
        caf = sb("caf", [P, 2, TOPK], f32, B)
        hit = sb("hit", [P, TOPK, TOPK], f32, B)
        iota16 = sb("iota16", [P, TOPK], f32, B)
        iota = sb("iota", [P, P], f32, B)
        pick = sb("pick", [P, 3, NT, PH * TOPK], f32, B)
        pickT = sb("pickT", [P, 3, TOK], f32, B)
        gh = sb("gh", [P, TOK], f32r, B)
        gl = sb("gl", [P, TOK], f32, B)
        i2s = sb("i2s", [P, GT], f32, B)
        B1 = ExitStack()
        skT = sb("skT", [P, 2 * PH, NK], f32, B1)
        qT = sb("qT", [P, 2, TOK], f32, B1)
        stv = sb("stv", [P, 2, NT, TOPK], f32, B1)
        sti = sb("sti", [P, 2, NT, TOPK], u32, B1)
        left = sb("left", [P, 2, NT, NK], f32, B1)
        B1.close()
        B2 = ExitStack()
        one2 = sb("one2", [P, GT, P], f32r, B2)
        mask = sb("mask", [P, GT, GC], f32, B2)
        one1 = sb("one1", [P, 2, GT, GC], f32r, B2)
        wt = sb("wt", [P, TOK], f32, B2)
        wh = [sb(f"wh{s}", [P, TOK], f32r, B2) for s in range(2)]
        wl = [sb(f"wl{s}", [P, TOK], f32r, B2) for s in range(2)]
        B2.close()
        B.close()

        ps = [ctx.enter_context(nc.psum_tensor(f"ps{b}", [P, 512], f32)) for b in range(8)]
        psU, psT, psS = ps[0:2], ps[2:6], ps[6:8]

        raw_in = [sem("raw_in0"), sem("raw_in1")]
        hi_made = sem("hi_made")
        lo_made = sem("lo_made")
        units_done = sem("units_done")
        turned = sem("turned")
        bank_read = [sem("bank_read0"), sem("bank_read1")]
        tok_read = sem("tok_read")
        consts = sem("consts")
        small_in = sem("small_in")
        vec_turned, vec_ready, set_dve, set_act = sem("vec_turned"), sem("vec_ready"), sem("set_dve"), sem("set_act")
        lru_in, lru_mm, gates_read = sem("lru_in"), sem("lru_mm"), sem("gates_read")
        xc_made, decays, w_made, root_made = sem("xc_made"), sem("decays"), sem("w_made"), sem("root_made")
        br_made, br_hi, br_lo = sem("br_made"), sem("br_hi"), sem("br_lo")
        lru_gelu = sem("lru_gelu")
        kv_made = sem("kv_made")
        staged = sem("staged")
        mscore, mmax, mexp, mprob, mturned, mpT, mpv, mhi, mlo = (sem("mem_" + n) for n in (
            "score", "max", "exp", "prob", "turned", "probT", "pv", "hi", "lo"))
        gate_made, merge_made, mg_hi, mg_lo = sem("gate_made"), sem("merge_made"), sem("mg_hi"), sem("mg_lo")
        qk_made, rotated, score, smax, sexp, attn, aturned, atT, pv, sqsum, onorm, oturned, ohi, olo, srt = (
            sem("d_" + n) for n in ("qk", "rotated", "score", "max", "exp", "attn", "turned", "attnT", "pv",
                                    "sqsum", "onorm", "oturned", "hi", "lo", "root"))
        res_in, sub_in, ln_in = sem("res_in"), sem("sub_in"), sem("ln_in")
        ln_dve, ln_act, ln_done = sem("ln_dve"), sem("ln_act"), sem("ln_done")
        x1_hi, x1_lo, sub_turned, sk_made = sem("x1_hi"), sem("x1_lo"), sem("sub_turned"), sem("sk_made")
        x1_turned = sem("x1_turned")
        q_made, key_score, top_done = sem("q_made"), sem("key_score"), sem("top_done")
        best_made, best_exp, pick_made, pick_turned, pickT_made, split_gate = (
            sem(n) for n in ("best_made", "best_exp", "pick_made", "pick_turned", "pickT_made", "split_gate"))
        i2_staged, one2_made, one1_made, gate_mm, gate_read = (
            sem(n) for n in ("i2_staged", "one2_made", "one1_made", "gate_mm", "gate_read"))
        h_made, w_ready, w_hi, w_lo, acc_read = sem("h_made"), sem("w_ready"), sem("w_hi"), sem("w_lo"), sem("acc_read")
        out_done = sem("out_done")
        passed = sem("passed")
        dve_link, act_link = sem("dve_link"), sem("act_link")

        def settle(eng):
            eng.sem_inc(passed, 1)

        class Link:

            def __init__(self, eng, s):
                self.eng, self.sem, self.n, self.off = eng, s, 0, 0

            def __call__(self, ins):
                ins.then_inc(self.sem, 1)
                self.n += 1
                self.eng.wait_ge(self.sem, self.off + self.n)

            def loop(self, count, per):
                return _Loop(self, count, per)

        class _Loop:

            def __init__(self, link, count, per):
                self.link, self.count, self.per = link, count, per

            def __enter__(self):
                self.fori = self.link.eng.Fori(0, self.count)
                i = self.fori.__enter__()
                self.start = self.link.n
                self.link.off = i * self.per if self.per else 0
                return i

            def __exit__(self, *e):
                got = self.link.n - self.start
                assert e[0] or got == self.per, f"{got} steps, not {self.per}"
                self.link.off = 0
                self.link.n = self.start + self.count * self.per
                return self.fori.__exit__(*e)

        def rows(w):
            return w.rearrange("(k p) c -> p k c", p=P)

        win_v, kv_v = rows(w_in[0]), rows(w_mem_kv[0])
        lru_v, diff_v, mem_v, out_v, wq_v = (rows(w[0]) for w in (w_lru, w_diff, w_mem, w_out, w_q))
        u_v = u_tab[0].rearrange("(c p) d -> p c d", p=P)
        v_v = v_tab[0].rearrange("(c p) d -> p c d", p=P)
        k3 = lambda t: t[:, :].rearrange("p (k c) -> p k c", c=BLK)
        w3 = lambda t: t[:, :].rearrange("p (k c) -> p k c", c=WIDE)

        block = ctx.enter_context(nc.Block())

        @block.sync
        def _(sp_):
            def load(m, s, dst, src, first=False):
                if not first:
                    sp_.wait_ge(lo_made, (m + (PRE - 1)) * 4)
                    settle(sp_)
                sp_.dma_start(dst, src).then_inc(raw_in[s], 16)

            for r, (src, t) in enumerate(((x, 0), (x, 1), (mem, 0), (mem, 1))):
                load(r - PRE, r % 2, raw[r % 2][:, :], src[0, t * P:(t + 1) * P, :], first=r < 2)

            def col(m, s, view, c):
                load(m, s, k3(raw[s]), view[:, :, ds(c, BLK)])

            with sp_.Fori(0, KT) as i:
                col(M_LRU + 2 * i, 0, win_v, COL_AX + i * BLK)
                col(M_LRU + 2 * i + 1, 1, win_v, COL_GATE + i * BLK)
            with sp_.Fori(0, MB // 2) as i:
                for s in range(2):
                    col(M_MK + 2 * i + s, s, kv_v, i * (2 * BLK) + s * BLK)
            with sp_.Fori(0, MEM_W // WIDE) as g:
                for j in range(4):
                    load(M_MV + 4 * g + j, j % 2, w3(raw[j % 2]), kv_v[:, j * KQ:(j + 1) * KQ, ds(MEM_W + g * WIDE, WIDE)])
            with sp_.Fori(0, MB // 2) as i:
                for s in range(2):
                    col(M_MQ + 2 * i + s, s, win_v, COL_MQ + i * (2 * BLK) + s * BLK)
            with sp_.Fori(0, KT) as i:
                col(M_MA + 2 * i, 0, win_v, COL_G + i * BLK)
                col(M_MA + 2 * i + 1, 1, lru_v, i * BLK)
            with sp_.Fori(0, HEADS // 2) as p:
                for j in range(8):
                    c = (COL_Q if j < 4 else COL_K) + (j % 4) * BLK
                    col(M_D + 12 * p + j, j % 2, win_v, c + p * (4 * BLK))
                for j in range(4):
                    load(M_D + 12 * p + 8 + j, j % 2, w3(raw[j % 2]),
                         win_v[:, j * KQ:(j + 1) * KQ, ds(COL_V + p * WIDE, WIDE)])
            with sp_.Fori(0, KT) as i:
                col(M_MM + 2 * i, 0, win_v, COL_G + 2 * D + i * BLK)
                load(M_MM + 2 * i + 1, 1, k3(raw[1])[:, 0:MB, :], mem_v[:, :, ds(i * BLK, BLK)])
            with sp_.Fori(0, KT) as i:
                col(M_MD + 2 * i, 0, win_v, COL_G + D + i * BLK)
                col(M_MD + 2 * i + 1, 1, diff_v, i * BLK)
            sp_.wait_ge(units_done, M_OUT)
            for t in range(NT):
                sp_.dma_start(res[:, t, :], x[0, t * P:(t + 1) * P, :]).then_inc(res_in, 16)
            for n, (v, dst) in enumerate(((ln1_g, 0), (ln1_b, 8))):
                sp_.dma_start(hbuf[:, dst:dst + 8, :].rearrange("p a b -> p (a b)"),
                              v[0].partition_broadcast(P)).then_inc(ln_in, 16)
            sp_.dma_start(gbuf[:, 0:8, :].rearrange("p a b -> p (a b)").rearrange("p (a b) -> p a b", b=P),
                          sub_keys[0].rearrange("h j n c -> n (h j) c")).then_inc(sub_in, 16)
            with sp_.Fori(0, D // WIDE) as g:
                for j in range(4):
                    load(M_OUT + 4 * g + j, j % 2, w3(raw[j % 2]), out_v[:, j * KQ:(j + 1) * KQ, ds(g * WIDE, WIDE)])
            with sp_.Fori(0, PH) as h:
                for s in range(2):
                    col(M_WQ + 2 * h + s, s, wq_v, h * (2 * BLK) + s * BLK)
            for g in range(GROUPS):
                for n, tab in enumerate((u_v, v_v)):
                    m0 = M_EXP + (2 * g + n) * GC
                    with sp_.Fori(0, GC // 2) as i:
                        for s in range(2):
                            load(m0 + 2 * i + s, s, raw[s][:, :],
                                 tab[:, ds(g * GC + 2 * i + s, 1), :].rearrange("p a d -> p (a d)"))
            sp_.wait_ge(w_ready, GROUPS * GC)
            for n, v in enumerate((ln2_g, ln2_b)):
                sp_.dma_start(gbuf[:, 8 * n:8 * n + 8, :].rearrange("p a b -> p (a b)"),
                              v[0].partition_broadcast(P)).then_inc(ln_in, 16)
            for t in range(NT):
                sp_.wait_ge(ln_done, NT + t + 1)
                sp_.dma_start(out[0, t * P:(t + 1) * P, :], res[:, t, :]).then_inc(out_done, 16)
            sp_.wait_ge(out_done, 16 * NT)

        @block.gpsimd
        def _(pool):
            pool.memset(ident[:, :], 0.0).then_inc(consts, 1)
            pool.memset(ones1[:, :], 1.0).then_inc(consts, 1)
            pool.memset(axp[:, :], 0.0).then_inc(consts, 1)
            pool.memset(sgn[:, :], 1.0).then_inc(consts, 1)
            for j in range(HALF_ROT):
                pool.memset(ifr[0:1, j:ROT:HALF_ROT], float(THETA ** (-j / HALF_ROT))).then_inc(consts, 1)
            n = 4 + HALF_ROT
            pool.wait_ge(consts, n)
            pool.affine_select(out=ident[:, :], in_=ident[:, :], compare_op=ALU.not_equal, fill=1.0, base=0,
                               pattern=[[-1, P]], channel_multiplier=1).then_inc(consts, 1)
            pool.memset(sgn[0:HALF_ROT, :], -1.0).then_inc(consts, 1)
            v1 = ((conv_w[0].rearrange("j (n p) -> (j n) p", p=P), 0, 64), (conv_b.rearrange("a (n p) -> (a n) p", p=P), 64, 16),
                  (b_gate.rearrange("a (n p) -> (a n) p", p=P), 80, 48))
            v2 = ((lru_b_a[0].rearrange("d (n p) -> (d n) p", p=P), 0, 32), (lru_b_i[0].rearrange("d (n p) -> (d n) p", p=P), 32, 32),
                  (lru_lambda[0].rearrange("d (n p) -> (d n) p", p=P), 64, 32),
                  (diff_subln.rearrange("a (n p) -> (a n) p", p=P), 96, 2))
            for k, vs in enumerate((v1, v2)):
                for src, at0, cnt in vs:
                    pool.dma_start(vrow[at0:at0 + cnt, k, :], src).then_inc(small_in, 16)
            pool.dma_start(lp[:, :, :].rearrange("p a b -> p (a b)"),
                           diff_lambda[0].rearrange("a b -> (a b)").partition_broadcast(P)).then_inc(small_in, 16)
            pool.dma_start(posi[:, :], pos[0].partition_broadcast(ROT)).then_inc(small_in, 16)
            with pool.Fori(0, KT) as i:
                pool.wait_ge(lru_mm, i)
                for k, w in enumerate((lru_w_a, lru_w_i)):
                    pool.dma_start(lru_w[:, k, :, :], w[0].rearrange("d n i j -> i n d j")[:, ds(i, 1), :, :]
                                   .rearrange("i a d j -> i (a d) j")).then_inc(lru_in, 16)
            with pool.Fori(0, MEM_HEADS) as h:
                pool.wait_ge(kv_made, MB + MEM_W // WIDE + MB)
                pool.wait_ge(mpv, h)
                pool.tensor_copy(mqs[:, :, :], mq[:, ds(h * MC, MC), :]).then_inc(staged, 1)
                pool.tensor_copy(mvs[:, :, :], mv[:, :, ds(h * MEM_DIM, MEM_DIM)]).then_inc(staged, 1)
            pool.wait_ge(ln_done, NT)
            pool.iota(iota[:, :], [[1, P]], base=0, channel_multiplier=0,
                      allow_small_or_imprecise_dtypes=True).then_inc(consts, 1)
            pool.iota(iota16[:, :], [[1, TOPK]], base=0, channel_multiplier=0,
                      allow_small_or_imprecise_dtypes=True).then_inc(consts, 1)
            pool.wait_ge(consts, n + 4)
            for g in range(GROUPS):
                with pool.Fori(0, TOK // GT) as b:
                    step = g * (TOK // GT) + b
                    pool.wait_ge(i2_staged, step + 1)
                    pool.wait_ge(gate_mm, step)
                    settle(pool)
                    for k in range(GT):
                        last = pool.tensor_scalar(one2[:, k, :], iota[:, :], i2s[:, k:k + 1], None, ALU.is_equal)
                    last.then_inc(one2_made, 1)

        @block.scalar
        def _(act):
            link = Link(act, act_link)

            def split(m, s, free=True):
                act.wait_ge(raw_in[s], (m + PRE - s) * 8 + 16)
                if free:
                    act.wait_ge(units_done, m - 1)
                for q in range(2):
                    act.activation(hi[s][:, q * HALF:(q + 1) * HALF], raw[s][:, q * HALF:(q + 1) * HALF],
                                   ACT.Copy).then_inc(hi_made, 2)

            def split_turned(m, s, j):
                act.wait_ge(units_done, m - 1)
                for b in range(4):
                    act.wait_ge(turned, j * 4 + (b + 1))
                    act.activation(hi[s][:, b * 512:(b + 1) * 512], psT[b][:, :], ACT.Copy).then_inc(hi_made, 1)

            def result(m, b):
                act.wait_ge(units_done, m + 1)

            act.wait_ge(vec_turned, 1)
            act.activation(vec[:, :, :].rearrange("p a b -> p (a b)")[:, 0:P + 98], psS[0][:, 0:P + 98], ACT.Copy).then_inc(set_act, 1)
            act.activation(ifc[:, :], psS[1][0:ROT, 0:1], ACT.Copy).then_inc(set_act, 1)
            for r in range(PRE):
                dst, t = (xh, r) if r < 2 else (memh, r - 2)
                for b in range(4):
                    act.wait_ge(turned, 4 * r + b + 1)
                    act.activation(dst[:, 4 * b:4 * b + 4, t * P:(t + 1) * P],
                                   psT[b][:, :].rearrange("p (k c) -> p k c", c=P), ACT.Copy).then_inc(hi_made, 1)
            split(0, 0, free=False)
            act.wait_ge(set_dve, 1)
            act.activation(spt[:, 1, :], spt[:, 0, :], ACT.Exp, scale=-1.0).then_inc(set_act, 1)
            act.activation(lame[:, :], lsum[:, :], ACT.Exp).then_inc(set_act, 1)
            act.wait_ge(set_dve, 2)
            act.activation(sinT[:, :], rtmp[:, 2, :], ACT.Sin).then_inc(set_act, 1)
            act.activation(cosT[:, :], rtmp[:, 3, :], ACT.Sin).then_inc(set_act, 1)
            act.wait_ge(set_dve, 3)

            with act.Fori(0, KT) as i:
                m = M_LRU + 2 * i
                split(m + 1, 1)
                split(m + 2, 0)
                result(m + 1, 1)
                act.activation(gelu_gate[:, :], psU[1][:, 0:TOK], ACT.Gelu).then_inc(bank_read[1], 1)
                act.wait_ge(lru_mm, i + 1)
                for d in range(2):
                    act.activation(t_i[:, d, :], psT[d][:, TOK:2 * TOK], ACT.Tanh, bias=hb[:, ds(i + 32 + 16 * d, 1)], scale=0.5)
                    last = act.activation(t_r[:, d, :], psT[d][:, 0:TOK], ACT.Tanh, bias=hb[:, ds(i + 16 * d, 1)], scale=0.5)
                last.then_inc(gates_read, 1)
                act.wait_ge(gates_read, i + 1)
                for d in range(2):
                    act.activation(dec[:, d, :], t_r[:, d, :], ACT.Exp, bias=nsp[:, ds(i + 16 * d, 1)], scale=nsp[:, ds(i + 16 * d, 1)])
                    last = act.activation(th[:, d, :], t_r[:, d, :], ACT.Tanh, bias=sp[:, ds(i + 16 * d, 1)], scale=sp[:, ds(i + 16 * d, 1)])
                last.then_inc(decays, 1)
                act.wait_ge(w_made, i + 1)
                act.activation(sq[:, :, :], wsq[:, :, :], ACT.Sqrt).then_inc(root_made, 1)
                act.wait_ge(br_made, i + 1)
                act.activation(brh[:, ds(i, 1), :].rearrange("p a t -> p (a t)"), uin[:, 0, :], ACT.Copy).then_inc(br_hi, 1)

            with act.Fori(0, MB // 2) as i:
                m = M_MK + 2 * i
                for s in range(2):
                    split(m + 1 + s, 1 - s)
                    result(m + s, s)
                    act.activation(mk[:, ds(2 * i + s, 1), :].rearrange("p a t -> p (a t)"), psU[s][:, 0:MEM],
                                   ACT.Copy).then_inc(bank_read[s], 1)
            with act.Fori(0, MEM_W // WIDE) as g:
                for j in range(4):
                    split(M_MV + 4 * g + j + 1, (j + 1) % 2)
            with act.Fori(0, MB // 2) as i:
                m = M_MQ + 2 * i
                for s in range(2):
                    split(m + 1 + s, 1 - s)
                    result(m + s, s)
                    act.activation(mq[:, ds(2 * i + s, 1), :].rearrange("p a t -> p (a t)"), psU[s][:, 0:TOK],
                                   ACT.Copy).then_inc(bank_read[s], 1)

            def gate(m, col):
                result(m, 0)
                act.activation(gt[:, :], psU[0][:, 0:TOK], ACT.Sigmoid, bias=vec[:, 0, ds(col + 80, 1)]).then_inc(bank_read[0], 1)

            with act.Fori(0, MEM_HEADS) as h:
                for k in range(4):
                    m = M_MA + 8 * h + 2 * k
                    split(m + 1, 1)
                    act.wait_ge(merge_made, 4 * h + k)
                    gate(m, 4 * h + k)
                    split(m + 2, 0)
                    if k == 0:
                        act.wait_ge(mmax, h + 1)
                        for t in range(NT):
                            last = act.activation(pm[:, t, :], psS[t][:, 0:MEM], ACT.Exp, bias=nmx[:, t:t + 1],
                                                  scale=MSCALE, accum_out=zs[:, t:t + 1])
                        last.then_inc(mexp, 1)
                    if k == 2:
                        act.wait_ge(mturned, h + 1)
                        act.activation(pmT[:, :, :].rearrange("p a t -> p (a t)"), psT[2][:, :], ACT.Copy).then_inc(mpT, 1)
                    if k == 3:
                        act.wait_ge(mpv, h + 1)
                        for c in range(MC):
                            act.activation(brmh[:, ds(h * MC + c, 1), :].rearrange("p a t -> p (a t)"),
                                           psT[(0, 1, 3)[c]][:, 0:TOK], ACT.Copy).then_inc(mhi, 1)

            with act.Fori(0, HEADS // 2) as p:
                m = M_D + 12 * p
                for j in range(8):
                    split(m + j + 1, (j + 1) % 2)
                    result(m + j, j % 2)
                    if j == 0:
                        act.wait_ge(score, 2 * p)
                    act.activation(qk[:, j, :], psU[j % 2][:, 0:TOK], ACT.Copy).then_inc(bank_read[j % 2], 1)
                split(m + 9, 1)
                split(m + 10, 0)
                for hh in range(2):
                    act.wait_ge(smax, 2 * p + hh + 1)
                    for t in range(NT):
                        for j in range(2):
                            c = 4 * hh + 2 * t + j
                            last = act.activation(ex[:, hh, t, j, :], (psS, psT[2:4])[hh][t][:, j * TOK:(j + 1) * TOK], ACT.Exp,
                                                  bias=nmx[:, c:c + 1], scale=QSCALE, accum_out=zs[:, c:c + 1])
                    last.then_inc(sexp, 1)
                split(m + 11, 1)
                split(m + 12, 0)
                for hh in range(2):
                    act.wait_ge(aturned, 2 * p + hh + 1)
                    act.activation(at[:, hh, :, :].rearrange("p a t -> p (a t)"), psS[hh][:, :], ACT.Copy).then_inc(atT, 1)
                for hh in range(2):
                    act.wait_ge(pv, 2 * p + hh + 1)
                    for t in range(NT):
                        last = act.activation(ex[:, hh, t, 1, :], psT[2 + hh][:, t * VD:(t + 1) * VD], ACT.Square,
                                              accum_out=ssq[:, 2 * hh + t:2 * hh + t + 1])
                last.then_inc(sqsum, 1)
                act.wait_ge(srt, 2 * p + 1)
                act.activation(rstd[:, :], ssq[:, :], ACT.Sqrt).then_inc(sqsum, 1)
                for hh in range(2):
                    act.wait_ge(oturned, 2 * p + hh + 1)
                    for c in range(2):
                        act.activation(brh[:, ds(4 * p + 2 * hh + c, 1), :].rearrange("p a t -> p (a t)"),
                                       psS[hh][:, c * TOK:(c + 1) * TOK], ACT.Copy, scale=vec[:, 1, 98 + c:99 + c]).then_inc(ohi, 1)

            for base_m, col, n0 in ((M_MM, 32, 1), (M_MD, 16, 2)):
                with act.Fori(0, KT) as i:
                    m = base_m + 2 * i
                    split(m + 1, 1)
                    act.wait_ge(merge_made, n0 * KT + i)
                    gate(m, i + col)
                    split(m + 2, 0)
                    if n0 == 2:
                        act.wait_ge(merge_made, n0 * KT + i + 1)
                        act.activation(mh[:, ds(i, 1), :].rearrange("p a t -> p (a t)"),
                                       merged[:, ds(i, 1), :].rearrange("p a t -> p (a t)"), ACT.Copy).then_inc(mg_hi, 1)

            with act.Fori(0, D // WIDE) as g:
                for j in range(4):
                    split(M_OUT + 4 * g + j + 1, (j + 1) % 2)

            def norm_act(k):
                for t in range(NT):
                    act.wait_ge(ln_dve, (k * NT + t) * 2 + 1)
                    act.activation(acc[:, t, :], res[:, t, :], ACT.Square, bias=nmom[:, t:t + 1],
                                   accum_out=mom[:, 1, t:t + 1]).then_inc(ln_act, 1)
                    act.wait_ge(ln_dve, (k * NT + t) * 2 + 2)
                    act.activation(mom[:, 2, t:t + 1], mom[:, 1, t:t + 1], ACT.Sqrt).then_inc(ln_act, 1)

            norm_act(0)
            for b in range(4):
                act.wait_ge(sub_turned, b + 1)
                act.activation(skT[:, 4 * b:4 * b + 4, :].rearrange("p a n -> p (a n)"), psT[b][:, :], ACT.Copy).then_inc(sk_made, 1)
            for t in range(NT):
                for b in range(4):
                    act.wait_ge(x1_turned, 4 * t + b + 1)
                    act.activation(x1h[:, 4 * b:4 * b + 4, t * P:(t + 1) * P],
                                   psT[b][:, :].rearrange("p (k c) -> p k c", c=P), ACT.Copy).then_inc(x1_hi, 1)

            def queries(h, m, after):
                split(m + 1, 1)
                act.wait_ge(key_score, 2 * h)
                result(m, 0)
                act.activation(qT[:, 0, :], psU[0][:, 0:TOK], ACT.Copy).then_inc(bank_read[0], 1)
                after()
                result(m + 1, 1)
                act.activation(qT[:, 1, :], psU[1][:, 0:TOK], ACT.Copy).then_inc(bank_read[1], 1)

            with act.Fori(0, PH - 1) as h:
                queries(h, M_WQ + 2 * h, lambda: split(M_WQ + 2 * h + 2, 0))
            queries(PH - 1, M_WQ + 2 * PH - 2, lambda: split_turned(M_EXP, 0, PRE))

            def take_h(m, s, c):
                result(m, s)
                act.activation(hbuf[:, ds(c, 1), :].rearrange("p a t -> p (a t)"), psU[s][:, 0:TOK],
                               ACT.Gelu).then_inc(bank_read[s], 1)

            def split_w(m, s, n):
                act.wait_ge(w_ready, n + 1)
                act.wait_ge(units_done, m - 1)
                act.activation(wh[s][:, :], wt[:, :], ACT.Copy).then_inc(w_hi, 1)

            def best_gates(n):
                act.wait_ge(best_made, n + 1)
                act.activation(eb[:, :], best[:, :], ACT.Exp, bias=nbest[:, 0:1], accum_out=zb[:, 0:1]).then_inc(best_exp, 1)

            def take_gates(step, b):
                act.wait_ge(gate_mm, step + 1)
                act.activation(gbuf[:, :, ds(b * GT, GT)], psS[0][:, 0:GT * GC].rearrange("p (k c) -> p c k", c=GC),
                               ACT.Copy).then_inc(gate_read, 1)

            for g in range(GROUPS):
                mu, mv_ = M_EXP + 2 * g * GC, M_EXP + (2 * g + 1) * GC
                ju = PRE + g * GC

                def pair(i, last=False):
                    m = mu + 2 * i
                    split_turned(m + 1, 1, ju + 2 * i + 1)
                    take_h(m, 0, 2 * i)
                    if last:
                        split(m + 2, 0)
                    else:
                        split_turned(m + 2, 0, ju + 2 * i + 2)
                    take_h(m + 1, 1, 2 * i + 1)
                    if g == 0:
                        best_gates(i)

                if g > 0:
                    act.wait_ge(w_ready, g * GC)
                with act.Fori(0, GC // 2 - 1) as i:
                    pair(i)
                pair(GC // 2 - 1, last=True)
                if g == 0:
                    act.wait_ge(pick_turned, 1)
                    act.activation(pickT[:, 0:2, :].rearrange("p a t -> p (a t)"), psS[1][:, :], ACT.Copy).then_inc(pickT_made, 1)
                    act.activation(pickT[:, 2, :], psS[0][:, 0:TOK], ACT.Copy).then_inc(pickT_made, 1)
                    act.wait_ge(pickT_made, 2)
                    act.activation(gh[:, :], pickT[:, 2, :], ACT.Copy).then_inc(split_gate, 1)
                with act.Fori(0, TOK // GT) as b:
                    take_gates(g * (TOK // GT) + b, b)
                split_w(mv_, 0, g * GC)

                def vpair(i, last=False):
                    m = mv_ + 2 * i
                    split(m + 1, 1)
                    split_w(m + 1, 1, g * GC + 2 * i + 1)
                    if not last:
                        split(m + 2, 0)
                        split_w(m + 2, 0, g * GC + 2 * i + 2)
                    elif g + 1 < GROUPS:
                        split_turned(m + 2, 0, ju + GC)

                with act.Fori(0, GC // 2 - 1) as i:
                    vpair(i)
                vpair(GC // 2 - 1, last=True)
            norm_act(1)

        @block.vector
        def _(dve):
            link = Link(dve, dve_link)

            def split(m, s):
                for q in range(2):
                    dve.wait_ge(hi_made, (m + PRE) * 4 + 2 * (q + 1))
                    h = slice(q * HALF, (q + 1) * HALF)
                    dve.tensor_tensor(lo[s][:, h], raw[s][:, h], hi[s][:, h].bitcast(f32), ALU.subtract).then_inc(lo_made, 2)

            def split_turned(m, s):
                for b in range(4):
                    dve.wait_ge(hi_made, (m + PRE) * 4 + (b + 1))
                    h = slice(b * 512, (b + 1) * 512)
                    dve.tensor_tensor(lo[s][:, h], psT[b][:, :], hi[s][:, h].bitcast(f32), ALU.subtract).then_inc(lo_made, 1)

            for r in range(PRE):
                src, dst, t = (xh, xl, r) if r < 2 else (memh, meml, r - 2)
                for b in range(4):
                    dve.wait_ge(hi_made, 4 * r + b + 1)
                    w = (slice(None), slice(4 * b, 4 * b + 4), slice(t * P, (t + 1) * P))
                    dve.tensor_tensor(dst[w], psT[b][:, :].rearrange("p (k c) -> p k c", c=P), src[w].bitcast(f32),
                                      ALU.subtract).then_inc(lo_made, 1)
            split(0, 0)
            dve.wait_ge(set_act, 2)
            dve.wait_ge(small_in, 9 * 16)
            dve.tensor_scalar(hb[:, :], vec[:, 1, 0:64], 0.5, None, ALU.mult)
            dve.scalar_tensor_tensor(spt[:, 0, :], vec[:, 1, 64:96], -1.0, vec[:, 1, 64:96], ALU.mult, ALU.max)
            link(dve.tensor_tensor(lp[:, 0:4:2, :], lp[:, 0:4:2, :], lp[:, 1:4:2, :], ALU.mult))
            dve.tensor_reduce(lsum[:, :], lp[:, 0:4:2, :], AX.X, ALU.add).then_inc(set_dve, 1)
            ang, turns, red, cang = (rtmp[:, k, :] for k in range(4))
            link(dve.tensor_copy(turns, posi[:, :]))
            link(dve.tensor_scalar(ang, turns, ifc[:, 0:1], None, ALU.mult))
            magic = 1.5 * 2.0 ** 23
            link(dve.tensor_scalar(turns, ang, 1.0 / (2 * math.pi), magic, ALU.mult, ALU.add))
            link(dve.tensor_scalar(turns, turns, -magic, None, ALU.add))
            c1 = 6.28125
            c2 = math.floor((2 * math.pi - c1) * 2.0 ** 20) / 2.0 ** 20
            c3 = 2 * math.pi - c1 - c2
            link(dve.scalar_tensor_tensor(red, turns, -c1, ang, ALU.mult, ALU.add))
            link(dve.scalar_tensor_tensor(red, turns, -c2, red, ALU.mult, ALU.add))
            link(dve.scalar_tensor_tensor(red, turns, -c3, red, ALU.mult, ALU.add))
            link(dve.tensor_scalar(red, red, 3.1415925, -3.1415925, ALU.min, ALU.max))
            link(dve.scalar_tensor_tensor(cang, red, -1.0, red, ALU.mult, ALU.min))
            dve.tensor_scalar(cang, cang, math.pi / 2, None, ALU.add).then_inc(set_dve, 1)
            dve.wait_ge(set_act, 4)
            s0, e_, r_, s2 = (spt[:, k, :] for k in range(4))
            link(dve.tensor_scalar(r_, e_, 2.0, None, ALU.add))
            link(dve.reciprocal(r_, r_))
            link(dve.tensor_tensor(r_, r_, e_, ALU.mult))
            link(dve.tensor_tensor(s2, r_, r_, ALU.mult))
            link(dve.tensor_scalar(s0, s2, 1.0 / 17, None, ALU.mult))
            for k in (15, 13, 11, 9, 7, 5, 3):
                link(dve.scalar_tensor_tensor(s0, s0, 1.0 / k, s2, ALU.add, ALU.mult))
            link(dve.scalar_tensor_tensor(s0, s0, 1.0, r_, ALU.add, ALU.mult))
            link(dve.tensor_scalar(e_, vec[:, 1, 64:96], -1.0, 0.0, ALU.mult, ALU.max))
            link(dve.scalar_tensor_tensor(s0, s0, 2.0, e_, ALU.mult, ALU.add))
            link(dve.tensor_scalar(sp[:, :], s0, 4.0, None, ALU.mult))
            link(dve.tensor_scalar(nsp[:, :], sp[:, :], -1.0, None, ALU.mult))
            link(dve.tensor_tensor(nlam[:, :], lame[:, 1:2], lame[:, 0:1], ALU.subtract))
            link(dve.tensor_scalar(nlam[:, :], nlam[:, :], -LAM_INIT, None, ALU.add))
            link(dve.tensor_scalar(vec[:, 1, 98:100], vec[:, 1, 96:98], 1.0 - LAM_INIT, None, ALU.mult))
            dve.wait_ge(set_act, 6)
            dve.tensor_scalar(sinT[:, :], sinT[:, :], sgn[:, 0:1], None, ALU.mult).then_inc(set_dve, 1)

            with link.loop(KT, 10) as i:
                m = M_LRU + 2 * i
                split(m + 1, 1)
                dve.wait_ge(units_done, m + 1)
                dve.tensor_copy(axp[:, 1:TOK + 1], psU[0][:, 0:TOK]).then_inc(bank_read[0], 1)
                dve.wait_ge(bank_read[0], i + 1)
                link(dve.tensor_scalar(xc[:, :], axp[:, 0:TOK], vec[:, 0, ds(i, 1)], vec[:, 0, ds(i + 64, 1)], ALU.mult, ALU.add))
                for j in (1, 2):
                    link(dve.scalar_tensor_tensor(xc[:, :], axp[:, j:TOK + j], vec[:, 0, ds(i + 16 * j, 1)], xc[:, :], ALU.mult, ALU.add))
                dve.scalar_tensor_tensor(xc[:, :], axp[:, 3:TOK + 3], vec[:, 0, ds(i + 48, 1)], xc[:, :], ALU.mult, ALU.add).then_inc(xc_made, 1)
                split(m + 2, 0)
                dve.wait_ge(decays, i + 1)
                link(dve.tensor_tensor(wsq[:, :, :], dec[:, :, :], dec[:, :, :], ALU.mult))
                dve.scalar_tensor_tensor(wsq[:, :, :], wsq[:, :, :], 1.0, th[:, :, :], ALU.add, ALU.mult).then_inc(w_made, 1)
                link(dve.scalar_tensor_tensor(uin[:, :, :], t_i[:, :, :], 1.0,
                                              xc[:, :].unsqueeze(1).broadcast_to([P, 2, TOK]), ALU.add, ALU.mult))
                dve.wait_ge(root_made, i + 1)
                link(dve.scalar_tensor_tensor(uin[:, :, :], sq[:, :, :], 0.5, uin[:, :, :], ALU.mult, ALU.mult))
                link(dve.tensor_tensor_scan(hst[:, 0, :], dec[:, 0, :], uin[:, 0, :], 0.0, ALU.mult, ALU.add))
                link(dve.tensor_tensor_scan(hst[:, 1, ::-1], dec[:, 1, ::-1], uin[:, 1, ::-1], 0.0, ALU.mult, ALU.add))
                link(dve.tensor_tensor(hst[:, 0, :], hst[:, 0, :], hst[:, 1, :], ALU.add))
                dve.tensor_tensor(uin[:, 0, :], hst[:, 0, :], gelu_gate[:, :], ALU.mult).then_inc(br_made, 1)
                dve.wait_ge(br_hi, i + 1)
                link(dve.tensor_tensor(brl[:, ds(i, 1), :].rearrange("p a t -> p (a t)"), uin[:, 0, :],
                                       brh[:, ds(i, 1), :].rearrange("p a t -> p (a t)").bitcast(f32), ALU.subtract))
            br0 = link.n

            def wide(m, split_, n, take):
                for j in range(4):
                    split_(m + j + 1, (j + 1) % 2)
                dve.wait_ge(units_done, m + 4)
                take()

            with dve.Fori(0, MB // 2) as i:
                for s in range(2):
                    split(M_MK + 2 * i + s + 1, 1 - s)
            with dve.Fori(0, MEM_W // WIDE) as g:
                def take():
                    for t in range(2):
                        last = dve.tensor_copy(mv[:, t, ds(g * WIDE, WIDE)], psT[t][:, :])
                    last.then_inc(tok_read, 1)
                wide(M_MV + 4 * g, split, g, take)
            with dve.Fori(0, MB // 2) as i:
                for s in range(2):
                    split(M_MQ + 2 * i + s + 1, 1 - s)
            dve.wait_ge(bank_read[1], KT + MB)
            dve.wait_ge(bank_read[0], KT + MB)
            dve.tensor_copy(mx[:, 0:1], nsp[:, 0:1]).then_inc(kv_made, MB + MEM_W // WIDE + MB)

            with link.loop(MEM_HEADS, 1) as h:
                for k in range(4):
                    m = M_MA + 8 * h + 2 * k
                    split(m + 1, 1)
                    if k == 0:
                        dve.wait_ge(mscore, h + 1)
                        for t in range(NT):
                            last = dve.tensor_reduce(mx[:, t:t + 1], psS[t][:, 0:MEM], AX.X, ALU.max)
                        link(last)
                        dve.tensor_scalar(nmx[:, 0:2], mx[:, 0:2], -MSCALE, None, ALU.mult).then_inc(mmax, 1)
                    split(m + 2, 0)
                    if k == 1:
                        dve.wait_ge(mexp, h + 1)
                        dve.reciprocal(rz[:, 0:2], zs[:, 0:2]).then_inc(mprob, 1)
                        dve.wait_ge(mprob, 2 * h + 1)
                        for t in range(NT):
                            last = dve.tensor_scalar(pm[:, t, :], pm[:, t, :], rz[:, t:t + 1], None, ALU.mult)
                        last.then_inc(mprob, 1)
                    dve.wait_ge(units_done, m + 2)
                    dve.wait_ge(bank_read[0], KT + MB + 4 * h + k + 1)
                    dve.tensor_tensor(merged[:, ds(4 * h + k, 1), :].rearrange("p a t -> p (a t)"), psU[1][:, 0:TOK],
                                      gt[:, :], ALU.mult).then_inc(merge_made, 1)
                    if k == 3:
                        for c in range(MC):
                            dve.wait_ge(mhi, MC * h + c + 1)
                            w = (slice(None), ds(h * MC + c, 1), slice(None))
                            dve.tensor_tensor(brml[w].rearrange("p a t -> p (a t)"), psT[(0, 1, 3)[c]][:, 0:TOK],
                                              brmh[w].rearrange("p a t -> p (a t)").bitcast(f32), ALU.subtract).then_inc(mlo, 1)

            with link.loop(HEADS // 2, 14) as p:
                m = M_D + 12 * p
                for j in range(8):
                    split(m + j + 1, (j + 1) % 2)
                    if j in (4, 7):
                        b = 0 if j == 4 else 4
                        dve.wait_ge(bank_read[1], KT + MB + 4 * p + (2 if j == 4 else 4))
                        dve.wait_ge(bank_read[0], KT + MB + KT + 4 * p + (2 if j == 4 else 4))
                        q4 = qk[0:ROT, b:b + 4, :]
                        cos4 = cosT[:, :].unsqueeze(1).broadcast_to([ROT, 4, TOK])
                        sin4 = sinT[:, :].unsqueeze(1).broadcast_to([ROT, 4, TOK])
                        swap = [(k + HALF_ROT) % ROT for k in range(ROT)]
                        settle(dve)
                        link(dve.stream_shuffle(rsh[:, :, :], q4, swap))
                        link(dve.tensor_tensor(rsh[:, :, :], rsh[:, :, :], sin4, ALU.mult))
                        link(dve.tensor_tensor(q4, q4, cos4, ALU.mult))
                        dve.tensor_tensor(q4, q4, rsh[:, :, :], ALU.add).then_inc(rotated, 1)
                split(m + 9, 1)
                split(m + 10, 0)
                for hh in range(2):
                    dve.wait_ge(score, 2 * p + hh + 1)
                    for t in range(NT):
                        c = 4 * hh + 2 * t
                        last = dve.tensor_reduce(mx[:, c:c + 2], (psS, psT[2:4])[hh][t][:, :].rearrange("p (j k) -> p j k", j=2), AX.X, ALU.max)
                    link(last)
                    dve.tensor_scalar(nmx[:, 4 * hh:4 * hh + 4], mx[:, 4 * hh:4 * hh + 4], -QSCALE, None, ALU.mult).then_inc(smax, 1)
                split(m + 11, 1)
                split(m + 12, 0)
                for hh in range(2):
                    dve.wait_ge(sexp, 2 * p + hh + 1)
                    z = slice(4 * hh, 4 * hh + 4)
                    zo = slice(4 * hh + 1, 4 * hh + 4, 2)
                    link(dve.reciprocal(rz[:, z], zs[:, z]))
                    link(dve.tensor_scalar(rz[:, zo], rz[:, zo], nlam[:, 0:1], None, ALU.mult))
                    for t in range(NT):
                        c = 4 * hh + 2 * t
                        last = dve.tensor_scalar(ex[:, hh, t, 1, :], ex[:, hh, t, 1, :], rz[:, c + 1:c + 2], None, ALU.mult)
                    link(last)
                    for t in range(NT):
                        c = 4 * hh + 2 * t
                        last = dve.scalar_tensor_tensor(ex[:, hh, t, 0, :], ex[:, hh, t, 0, :], rz[:, c:c + 1],
                                                        ex[:, hh, t, 1, :], ALU.mult, ALU.add)
                    last.then_inc(attn, 1)
                dve.wait_ge(units_done, m + 12)
                for t in range(2):
                    last = dve.tensor_copy(vv[:, t, :], psT[t][:, :])
                last.then_inc(tok_read, 1)
                dve.wait_ge(sqsum, 2 * p + 1)
                dve.tensor_scalar(ssq[:, :], ssq[:, :], 1.0 / VD, EPS, ALU.mult, ALU.add).then_inc(srt, 1)
                dve.wait_ge(sqsum, 2 * p + 2)
                dve.reciprocal(rstd[:, :], rstd[:, :]).then_inc(srt, 1)
                dve.wait_ge(srt, 2 * p + 2)
                for hh in range(2):
                    for t in range(NT):
                        last = dve.tensor_scalar(ex[:, hh, t, 0, :], psT[2 + hh][:, t * VD:(t + 1) * VD],
                                                 rstd[:, 2 * hh + t:2 * hh + t + 1], None, ALU.mult)
                    last.then_inc(onorm, 1)
                for hh in range(2):
                    dve.wait_ge(ohi, 4 * p + 2 * hh + 2)
                    for c in range(2):
                        w = (slice(None), ds(4 * p + 2 * hh + c, 1), slice(None))
                        dve.scalar_tensor_tensor(brl[w].rearrange("p a t -> p (a t)"), psS[hh][:, c * TOK:(c + 1) * TOK],
                                                 vec[:, 1, 98 + c:99 + c], brh[w].rearrange("p a t -> p (a t)").bitcast(f32),
                                                 ALU.mult, ALU.subtract).then_inc(olo, 1)

            for base_m, n0, reads in ((M_MM, 1, KT + MB + KT + 4 * 4), (M_MD, 2, KT + MB + 2 * KT + 4 * 4)):
                with link.loop(KT, 1) as i:
                    m = base_m + 2 * i
                    split(m + 1, 1)
                    split(m + 2, 0)
                    dve.wait_ge(units_done, m + 2)
                    dve.wait_ge(bank_read[0], reads + i + 1)
                    link(dve.tensor_tensor(pt[:, :], psU[1][:, 0:TOK], gt[:, :], ALU.mult))
                    mg = merged[:, ds(i, 1), :].rearrange("p a t -> p (a t)")
                    dve.tensor_tensor(mg, mg, pt[:, :], ALU.add).then_inc(merge_made, 1)
                    if n0 == 2:
                        dve.wait_ge(mg_hi, i + 1)
                        w = (slice(None), ds(i, 1), slice(None))
                        dve.tensor_tensor(ml[w].rearrange("p a t -> p (a t)"), mg,
                                          mh[w].rearrange("p a t -> p (a t)").bitcast(f32), ALU.subtract).then_inc(mg_lo, 1)

            dve.wait_ge(res_in, 16 * NT)
            with dve.Fori(0, D // WIDE) as g:
                def take():
                    for t in range(2):
                        r = res[:, t, ds(g * WIDE, WIDE)]
                        last = dve.scalar_tensor_tensor(r, r, ALPHA, psT[t][:, :], ALU.mult, ALU.add)
                    last.then_inc(tok_read, 1)
                wide(M_OUT + 4 * g, split, g, take)

            def norm(k, gain, bias):
                dve.wait_ge(ln_in, 32 * (k + 1))
                for t in range(NT):
                    link(dve.tensor_reduce(mom[:, 0, t:t + 1], res[:, t, :], AX.X, ALU.add))
                    dve.tensor_scalar(nmom[:, t:t + 1], mom[:, 0, t:t + 1], -1.0 / D, None, ALU.mult).then_inc(ln_dve, 1)
                    dve.wait_ge(ln_act, (k * NT + t) * 2 + 1)
                    dve.tensor_scalar(mom[:, 1, t:t + 1], mom[:, 1, t:t + 1], 1.0 / D, EPS, ALU.mult, ALU.add).then_inc(ln_dve, 1)
                    dve.wait_ge(ln_act, (k * NT + t) * 2 + 2)
                    link(dve.reciprocal(mom[:, 2, t:t + 1], mom[:, 2, t:t + 1]))
                    link(dve.tensor_scalar(res[:, t, :], res[:, t, :], nmom[:, t:t + 1], mom[:, 2, t:t + 1], ALU.add, ALU.mult))
                    link(dve.tensor_tensor(res[:, t, :], res[:, t, :], gain, ALU.mult))
                    dve.tensor_tensor(res[:, t, :], res[:, t, :], bias, ALU.add).then_inc(ln_done, 1)

            dve.wait_ge(tok_read, MEM_W // WIDE + HEADS // 2 + D // WIDE)
            norm(0, hbuf[:, 0:8, :].rearrange("p a b -> p (a b)"), hbuf[:, 8:16, :].rearrange("p a b -> p (a b)"))
            for t in range(NT):
                for b in range(4):
                    dve.wait_ge(x1_hi, 4 * t + b + 1)
                    w = (slice(None), slice(4 * b, 4 * b + 4), slice(t * P, (t + 1) * P))
                    dve.tensor_tensor(x1l[w], psT[b][:, :].rearrange("p (k c) -> p k c", c=P), x1h[w].bitcast(f32),
                                      ALU.subtract).then_inc(x1_lo, 1)

            def top16(src, v, i, rest):
                settle(dve)
                link(dve.max(v[:, 0:8], src))
                settle(dve)
                link(dve.match_replace(rest, v[:, 0:8], src, LOWEST))
                settle(dve)
                link(dve.max(v[:, 8:16], rest))
                settle(dve)
                dve.max_index(i[:, 0:8], v[:, 0:8], src)
                link(dve.max_index(i[:, 8:16], v[:, 8:16], rest))

            def keys(h, m, after):
                split(m + 1, 1)
                after()
                for j in range(2):
                    dve.wait_ge(key_score, 2 * h + j + 1)
                    for t in range(NT):
                        top16(psS[j][:, t * NK:(t + 1) * NK], stv[:, j, t, :], sti[:, j, t, :], left[:, j, t, :])
                dve.tensor_copy(top_v[:, ds(h, 1), :, :, :].rearrange("p a j t r -> p (a j t r)"),
                                stv[:, :, :, :].rearrange("p j t r -> p (j t r)"))
                dve.tensor_copy(top_i[:, ds(h, 1), :, :, :].rearrange("p a j t r -> p (a j t r)"),
                                sti[:, :, :, :].rearrange("p j t r -> p (j t r)")).then_inc(top_done, 1)
                dve.wait_ge(top_done, h + 1)

            with link.loop(PH - 1, 16) as h:
                keys(h, M_WQ + 2 * h, lambda: split(M_WQ + 2 * h + 2, 0))
            keys(PH - 1, M_WQ + 2 * PH - 2, lambda: split_turned(M_EXP, 0))
            dve.wait_ge(consts, 4 + HALF_ROT + 4)

            def choose(h, t, n):
                a_ = top_v[:, ds(h, 1), 0, t, :].rearrange("p a r -> p (a r)")
                b_ = top_v[:, ds(h, 1), 1, t, :].rearrange("p a r -> p (a r)")
                link(dve.tensor_tensor(cand[:, :, :], a_.unsqueeze(2).broadcast_to([P, TOPK, TOPK]),
                                       b_.unsqueeze(1).broadcast_to([P, TOPK, TOPK]), ALU.add))
                flat = cand[:, :, :].rearrange("p a b -> p (a b)")
                dve.wait_ge(best_exp, n)
                top16(flat, best[:, :], ci[:, :], cand2[:, :])
                dve.tensor_scalar(nbest[:, :], best[:, 0:1], -1.0, None, ALU.mult).then_inc(best_made, 1)
                dve.tensor_single_scalar(ca[:, :], ci[:, :], 4, ALU.logical_shift_right)
                link(dve.tensor_single_scalar(cb[:, :], ci[:, :], TOPK - 1, ALU.bitwise_and))
                dve.tensor_copy(caf[:, 0, :], ca[:, :])
                link(dve.tensor_copy(caf[:, 1, :], cb[:, :]))
                for j in range(2):
                    src = top_i[:, ds(h, 1), j, t, :].rearrange("p a r -> p (a r)")
                    link(dve.tensor_tensor(hit[:, :, :], caf[:, j, :].unsqueeze(2).broadcast_to([P, TOPK, TOPK]),
                                           iota16[:, :].unsqueeze(1).broadcast_to([P, TOPK, TOPK]), ALU.is_equal))
                    link(dve.tensor_tensor(hit[:, :, :], hit[:, :, :], src.unsqueeze(1).broadcast_to([P, TOPK, TOPK]), ALU.mult))
                    link(dve.tensor_reduce(pick[:, j, t, ds(h * TOPK, TOPK)], hit[:, :, :], AX.X, ALU.add))
                dve.wait_ge(best_exp, n + 1)
                link(dve.reciprocal(rzb[:, :], zb[:, :]))
                link(dve.tensor_scalar(pick[:, 2, t, ds(h * TOPK, TOPK)], eb[:, :], rzb[:, 0:1], None, ALU.mult))

            def one_hots(step, b):
                tok = ds(b * GT, GT)
                dve.wait_ge(gate_mm, step)
                dve.tensor_copy(i2s[:, :], pickT[:, 1, tok]).then_inc(i2_staged, 1)
                link(dve.tensor_tensor(mask[:, :, :], pickT[:, 0, tok].unsqueeze(2).broadcast_to([P, GT, GC]),
                                       iota[:, 0:GC].unsqueeze(1).broadcast_to([P, GT, GC]), ALU.is_equal))
                dve.tensor_tensor(one1[:, 0, :, :], mask[:, :, :],
                                  gh[:, tok].bitcast(f32).unsqueeze(2).broadcast_to([P, GT, GC]), ALU.mult)
                dve.tensor_tensor(one1[:, 1, :, :], mask[:, :, :],
                                  gl[:, tok].unsqueeze(2).broadcast_to([P, GT, GC]), ALU.mult).then_inc(one1_made, 1)

            def weigh(m, s, c, n):
                dve.wait_ge(w_lo, n)
                cc = (slice(None), ds(c, 1), slice(None))
                dve.tensor_tensor(wt[:, :], hbuf[cc].rearrange("p a t -> p (a t)"), gbuf[cc].rearrange("p a t -> p (a t)"),
                                  ALU.mult).then_inc(w_ready, 1)

            def split_w(s, n):
                dve.wait_ge(w_hi, n + 1)
                dve.tensor_tensor(wl[s][:, :], wt[:, :], wh[s][:, :].bitcast(f32), ALU.subtract).then_inc(w_lo, 1)

            for g in range(GROUPS):
                mu, mv_ = M_EXP + 2 * g * GC, M_EXP + (2 * g + 1) * GC
                if g == 0:
                    with link.loop(PH - 1, 30) as h:
                        for t in range(NT):
                            split_turned(mu + 4 * h + 2 * t + 1, 1)
                            split_turned(mu + 4 * h + 2 * t + 2, 0)
                            choose(h, t, 2 * h + t)
                    for t in range(NT):
                        m = mu + GC - 4 + 2 * t
                        split_turned(m + 1, 1)
                        if t == 0:
                            split_turned(m + 2, 0)
                        else:
                            split(m + 2, 0)
                        choose(PH - 1, t, 2 * PH - 2 + t)
                    dve.tensor_copy(best[:, 0:1], zb[:, 0:1]).then_inc(pick_made, 1)
                    dve.wait_ge(split_gate, 1)
                    dve.tensor_tensor(gl[:, :], pickT[:, 2, :], gh[:, :].bitcast(f32), ALU.subtract).then_inc(split_gate, 1)
                    dve.wait_ge(split_gate, 2)
                else:
                    with dve.Fori(0, GC // 2 - 1) as i:
                        split_turned(mu + 2 * i + 1, 1)
                        split_turned(mu + 2 * i + 2, 0)
                    split_turned(mu + GC - 1, 1)
                    split(mv_, 0)
                    link(dve.tensor_scalar(pickT[:, 0, :], pickT[:, 0, :], float(-GC), None, ALU.add))
                with link.loop(TOK // GT, 1) as b:
                    one_hots(g * (TOK // GT) + b, b)
                dve.wait_ge(bank_read[1], PAIRS + (g + 1) * (GC // 2))
                dve.wait_ge(gate_read, (g + 1) * (TOK // GT))
                weigh(mv_, 0, 0, g * GC)
                split_w(0, g * GC)

                def vpair(i, last=False):
                    m, n = mv_ + 2 * i, g * GC + 2 * i
                    weigh(m + 1, 1, 2 * i + 1, n + 1)
                    split(m + 1, 1)
                    split_w(1, n + 1)
                    if not last:
                        weigh(m + 2, 0, 2 * i + 2, n + 2)
                        split(m + 2, 0)
                        split_w(0, n + 2)

                with dve.Fori(0, GC // 2 - 1) as i:
                    vpair(i)
                vpair(GC // 2 - 1, last=True)
                dve.wait_ge(units_done, mv_ + GC)
                for t in range(NT):
                    for n in range(4):
                        w = acc[:, t, n * 512:(n + 1) * 512]
                        if g == 0:
                            dve.tensor_copy(w, ps[4 * t + n][:, :]).then_inc(acc_read, 1)
                        else:
                            dve.tensor_tensor(w, w, ps[4 * t + n][:, :], ALU.add).then_inc(acc_read, 1)
                dve.wait_ge(acc_read, 8 * (g + 1))
                if g + 1 < GROUPS:
                    split_turned(mv_ + GC, 0)
            for t in range(NT):
                last = dve.scalar_tensor_tensor(res[:, t, :], res[:, t, :], ALPHA, acc[:, t, :], ALU.mult, ALU.add)
            link(last)
            norm(1, gbuf[:, 0:8, :].rearrange("p a b -> p (a b)"), gbuf[:, 8:16, :].rearrange("p a b -> p (a b)"))

        @block.tensor
        def _(pe):
            def turn(src, bank, q, identity=ident):
                return pe.transpose(psT[bank][:, q * P:(q + 1) * P], src, identity[:, :])

            def unit(m, s, b, ah, al, kt, reads, taken=None):
                pe.wait_ge(lo_made, (m + PRE) * 4 + 4)
                pe.wait_ge(taken or bank_read[b], reads)
                w_h, w_l = k3(hi[s]), k3(lo[s])
                for k in range(kt):
                    o = psU[b][:, 0:TOK]
                    pe.matmul(o, w_h[:, k, :], ah[:, k, :], start=k == 0, stop=False)
                    pe.matmul(o, w_h[:, k, :], al[:, k, :], start=False, stop=False)
                    last = pe.matmul(o, w_l[:, k, :], ah[:, k, :], start=False, stop=k == kt - 1)
                last.then_inc(units_done, 1)

            def wide(m, ah, al, reads):
                for j in range(4):
                    s = j % 2
                    pe.wait_ge(lo_made, (m + j + PRE) * 4 + 4)
                    if j == 0:
                        pe.wait_ge(tok_read, reads)
                    w_h, w_l = w3(hi[s]), w3(lo[s])
                    for t in range(2):
                        for k in range(KQ):
                            a_h = ah[:, KQ * j + k, t * P:(t + 1) * P]
                            a_l = al[:, KQ * j + k, t * P:(t + 1) * P]
                            o = psT[t][:, :]
                            pe.matmul(o, a_h, w_h[:, k, :], start=j == 0 and k == 0, stop=False)
                            pe.matmul(o, a_h, w_l[:, k, :], start=False, stop=False)
                            last = pe.matmul(o, a_l, w_h[:, k, :], start=False, stop=j == 3 and k == KQ - 1)
                    last.then_inc(units_done, 1)

            pe.wait_ge(consts, 6 + HALF_ROT)
            pe.wait_ge(small_in, 9 * 16)
            pe.transpose(psS[0][:, 0:P], vrow[:, 0, :], ident[:, :])
            pe.transpose(psS[0][:, P:P + 98], vrow[0:98, 1, :], ident[0:98, 0:98])
            pe.matmul(psS[1][0:ROT, 0:1], ifr[0:1, :], ones1[0:1, 0:1], start=True, stop=True).then_inc(vec_turned, 1)
            for r in range(PRE):
                pe.wait_ge(raw_in[r % 2], 16 * (r // 2 + 1))
                for b in range(4):
                    if r:
                        pe.wait_ge(lo_made, 4 * (r - 1) + b + 1)
                    for q in range(4):
                        last = turn(raw[r % 2][:, (4 * b + q) * P:(4 * b + q + 1) * P], b, q)
                    last.then_inc(turned, 1)

            with pe.Fori(0, KT) as i:
                m = M_LRU + 2 * i
                unit(m, 0, 0, xh, xl, KT, i)
                unit(m + 1, 1, 1, xh, xl, KT, i)
                pe.wait_ge(xc_made, i + 1)
                pe.wait_ge(lru_in, (i + 1) * 32)
                pe.wait_ge(gates_read, i)
                for d in range(2):
                    for k in range(2):
                        last = pe.matmul(psT[d][:, k * TOK:(k + 1) * TOK], lru_w[:, k, d, :], xc[:, :], start=True, stop=True)
                last.then_inc(lru_mm, 1)
            with pe.Fori(0, MB // 2) as i:
                for s in range(2):
                    unit(M_MK + 2 * i + s, s, s, memh, meml, KT, KT + i)
            pe.wait_ge(gates_read, KT)
            with pe.Fori(0, MEM_W // WIDE) as g:
                wide(M_MV + 4 * g, memh, meml, g)
            with pe.Fori(0, MB // 2) as i:
                for s in range(2):
                    unit(M_MQ + 2 * i + s, s, s, xh, xl, KT, KT + MB // 2 + i)
            rd = KT + MB
            pe.wait_ge(kv_made, 1)
            pe.wait_ge(bank_read[1], rd)
            with pe.Fori(0, MEM_HEADS) as h:
                for k in range(4):
                    m = M_MA + 8 * h + 2 * k
                    unit(m, 0, 0, xh, xl, KT, rd + 4 * h + k)
                    if k == 0:
                        pe.wait_ge(staged, 2 * h + 2)
                        for t in range(NT):
                            for c in range(MC):
                                last = pe.matmul(psS[t][:, 0:MEM], mqs[:, c, t * P:(t + 1) * P],
                                                 mk[:, ds(h * MC + c, 1), :].rearrange("p a m -> p (a m)"),
                                                 start=c == 0, stop=c == MC - 1)
                        last.then_inc(mscore, 1)
                    if k == 2:
                        pe.wait_ge(mprob, 2 * h + 2)
                        for b in range(2):
                            for t in range(NT):
                                last = pe.transpose(psT[2][:, (2 * b + t) * P:(2 * b + t + 1) * P], pm[:, t, b * P:(b + 1) * P], ident[:, :])
                        last.then_inc(mturned, 1)
                    if k == 3:
                        pe.wait_ge(mpT, h + 1)
                        pe.wait_ge(mlo, MC * h)
                        for c in range(MC):
                            for b in range(2):
                                last = pe.matmul(psT[(0, 1, 3)[c]][:, 0:TOK], mvs[:, b, c * P:(c + 1) * P], pmT[:, b, :],
                                                 start=b == 0, stop=b == 1)
                        last.then_inc(mpv, 1)
                    unit(m + 1, 1, 1, brh, brl, KT, 4 * h + k, merge_made)
            merges = KT
            rd += KT
            pe.wait_ge(merge_made, KT)
            pe.wait_ge(mlo, MC * MEM_HEADS)
            with pe.Fori(0, HEADS // 2) as p:
                m = M_D + 12 * p
                for j in range(8):
                    unit(m + j, j % 2, j % 2, xh, xl, KT, rd - merges * (j % 2) + 4 * p + j // 2)
                pe.wait_ge(olo, 4 * p)
                for hh in range(2):
                    if hh == 0:
                        pe.wait_ge(rotated, 2 * p + 2)
                    for t in range(NT):
                        for j in range(2):
                            last = pe.matmul((psS, psT[2:4])[hh][t][:, j * TOK:(j + 1) * TOK], qk[:, 2 * hh + j, t * P:(t + 1) * P],
                                             qk[:, 4 + 2 * hh + j, :], start=True, stop=True)
                    last.then_inc(score, 1)
                wide(m + 8, xh, xl, MEM_W // WIDE + p)
                for hh in range(2):
                    pe.wait_ge(attn, 2 * p + hh + 1)
                    for b in range(2):
                        for t in range(NT):
                            last = pe.transpose(psS[hh][:, (2 * b + t) * P:(2 * b + t + 1) * P], ex[:, hh, t, 0, b * P:(b + 1) * P], ident[:, :])
                    last.then_inc(aturned, 1)
                pe.wait_ge(tok_read, MEM_W // WIDE + p + 1)
                for hh in range(2):
                    pe.wait_ge(atT, 2 * p + hh + 1)
                    for t in range(NT):
                        for b in range(2):
                            last = pe.matmul(psT[2 + hh][:, t * VD:(t + 1) * VD], at[:, hh, b, t * P:(t + 1) * P],
                                             vv[:, b, hh * VD:(hh + 1) * VD], start=b == 0, stop=b == 1)
                    last.then_inc(pv, 1)
                for hh in range(2):
                    pe.wait_ge(onorm, 2 * p + hh + 1)
                    for c in range(2):
                        for t in range(NT):
                            last = pe.transpose(psS[hh][:, (2 * c + t) * P:(2 * c + t + 1) * P], ex[:, hh, t, 0, c * P:(c + 1) * P], ident[:, :])
                    last.then_inc(oturned, 1)
            rd += 4 * (HEADS // 2)
            pe.wait_ge(bank_read[1], rd - merges)
            with pe.Fori(0, KT) as i:
                unit(M_MM + 2 * i, 0, 0, xh, xl, KT, rd + i)
                unit(M_MM + 2 * i + 1, 1, 1, brmh, brml, MB, KT + i, merge_made)
            rd += KT
            pe.wait_ge(olo, 2 * HEADS)
            with pe.Fori(0, KT) as i:
                unit(M_MD + 2 * i, 0, 0, xh, xl, KT, rd + i)
                unit(M_MD + 2 * i + 1, 1, 1, brh, brl, KT, 2 * KT + i, merge_made)
            rd += KT
            merges = 3 * KT
            pe.wait_ge(merge_made, merges)
            pe.wait_ge(mg_lo, KT)
            with pe.Fori(0, D // WIDE) as g:
                wide(M_OUT + 4 * g, mh, ml, MEM_W // WIDE + HEADS // 2 + g)
            pe.wait_ge(sub_in, 16)
            pe.wait_ge(tok_read, MEM_W // WIDE + HEADS // 2 + D // WIDE)
            keys_raw = gbuf[:, 0:8, :].rearrange("p a b -> p (a b)")
            for b in range(4):
                for q in range(4):
                    last = turn(keys_raw[:, (4 * b + q) * P:(4 * b + q + 1) * P], b, q)
                last.then_inc(sub_turned, 1)
            for t in range(NT):
                pe.wait_ge(ln_done, t + 1)
                for b in range(4):
                    if t == 0:
                        pe.wait_ge(sk_made, b + 1)
                    else:
                        pe.wait_ge(x1_lo, b + 1)
                    for q in range(4):
                        last = turn(res[:, t, (4 * b + q) * P:(4 * b + q + 1) * P], b, q)
                    last.then_inc(x1_turned, 1)
            pe.wait_ge(x1_lo, 4 * NT)

            def turn_unit(m, s, first=False):
                pe.wait_ge(raw_in[s], (m + PRE - s) * 8 + 16)
                for b in range(4):
                    if not first:
                        pe.wait_ge(lo_made, (m + PRE - 1) * 4 + (b + 1))
                    for q in range(4):
                        last = turn(raw[s][:, (4 * b + q) * P:(4 * b + q + 1) * P], b, q)
                    last.then_inc(turned, 1)

            def queries(h, m, after):
                unit(m, 0, 0, x1h, x1l, KT, rd + h)
                after()
                unit(m + 1, 1, 1, x1h, x1l, KT, rd - merges + h)
                pe.wait_ge(top_done, h)
                for j in range(2):
                    pe.wait_ge(bank_read[j], rd - merges * j + h + 1)
                    for t in range(NT):
                        last = pe.matmul(psS[j][:, t * NK:(t + 1) * NK], qT[:, j, t * P:(t + 1) * P],
                                         skT[:, ds(2 * h + j, 1), :].rearrange("p a n -> p (a n)"), start=True, stop=True)
                    last.then_inc(key_score, 1)

            with pe.Fori(0, PH - 1) as h:
                queries(h, M_WQ + 2 * h, lambda: None)
            queries(PH - 1, M_WQ + 2 * PH - 2, lambda: turn_unit(M_EXP, 0, first=True))
            rd += PH

            for g in range(GROUPS):
                mu, mv_ = M_EXP + 2 * g * GC, M_EXP + (2 * g + 1) * GC
                r0 = rd + g * (GC // 2)

                def pair(i, last=False):
                    m = mu + 2 * i
                    turn_unit(m + 1, 1)
                    unit(m, 0, 0, x1h, x1l, KT, r0 + i)
                    if not last:
                        turn_unit(m + 2, 0)
                    unit(m + 1, 1, 1, x1h, x1l, KT, r0 - merges + i)

                with pe.Fori(0, GC // 2 - 1) as i:
                    pair(i)
                pair(GC // 2 - 1, last=True)
                if g == 0:
                    pe.wait_ge(pick_made, 1)
                    for k in range(3):
                        dst = psS[1] if k < 2 else psS[0]
                        for t in range(NT):
                            c = ((k % 2) * NT + t) * P
                            last = pe.transpose(dst[:, c:c + P], pick[:, k, t, :], ident[:, :])
                    last.then_inc(pick_turned, 1)
                with pe.Fori(0, TOK // GT) as b:
                    step = g * (TOK // GT) + b
                    pe.wait_ge(one2_made, step + 1)
                    pe.wait_ge(one1_made, step + 1)
                    pe.wait_ge(gate_read, step)
                    for k in range(GT):
                        o = psS[0][:, k * GC:(k + 1) * GC]
                        pe.matmul(o, one2[:, k, :], one1[:, 0, k, :], start=True, stop=False)
                        last = pe.matmul(o, one2[:, k, :], one1[:, 1, k, :], start=False, stop=True)
                    last.then_inc(gate_mm, 1)

                def v_unit(m, s, n, first=False, final=False):
                    pe.wait_ge(lo_made, (m + PRE) * 4 + 4)
                    pe.wait_ge(w_lo, n + 1)
                    for t in range(NT):
                        for part, (w, v) in enumerate(((wh[s], hi[s]), (wh[s], lo[s]), (wl[s], hi[s]))):
                            for c in range(4):
                                last = pe.matmul(ps[4 * t + c][:, :], w[:, t * P:(t + 1) * P], v[:, c * 512:(c + 1) * 512],
                                                 start=first and part == 0, stop=final and part == 2)
                    last.then_inc(units_done, 1)

                pe.wait_ge(gate_read, (g + 1) * (TOK // GT))
                pe.wait_ge(bank_read[0], r0 + GC // 2)
                pe.wait_ge(bank_read[1], r0 - merges + GC // 2)
                v_unit(mv_, 0, g * GC, first=True)
                v_unit(mv_ + 1, 1, g * GC + 1)
                with pe.Fori(1, GC // 2 - 1) as i:
                    for s in range(2):
                        v_unit(mv_ + 2 * i + s, s, g * GC + 2 * i + s)
                v_unit(mv_ + GC - 2, 0, g * GC + GC - 2)
                v_unit(mv_ + GC - 1, 1, g * GC + GC - 1, final=True)
                if g + 1 < GROUPS:
                    pe.wait_ge(acc_read, 8 * (g + 1))
                    turn_unit(mv_ + GC, 0, first=True)


_INS = ['x', 'mem', 'positions', 'w_in', 'b_gate', 'conv_w', 'conv_b', 'lru_w_a', 'lru_b_a', 'lru_w_i', 'lru_b_i',
        'lru_lambda', 'diff_lambda', 'diff_subln', 'w_mem_kv', 'w_branch_lru', 'w_branch_diff', 'w_branch_mem',
        'w_out', 'ln1_g', 'ln1_b', 'peer_w_q', 'peer_sub_keys', 'peer_u', 'peer_v', 'ln2_g', 'ln2_b']


def kernel(**inputs):
    import numpy as _np
    import concourse.bacc as _bacc
    from concourse import mybir as _mybir
    from concourse.bass_utils import run_bass_kernel_spmd as _run

    nc = _bacc.Bacc("TRN2", target_bir_lowering=False, num_devices=1)
    arrays, args = {}, []
    for name in _INS:
        a = _np.ascontiguousarray(inputs[name])
        arrays[f"in_{name}"] = a
        args.append(nc.dram_tensor(f"in_{name}", a.shape, _mybir.dt.from_np(a.dtype), kind="ExternalInput").ap())
    o = nc.dram_tensor("out_x", (1, TOK, D), _mybir.dt.float32, kind="ExternalOutput").ap()
    layer(nc, *args, o)
    r = _run(nc, [arrays], core_ids=[0])
    return r.results[0]["out_x"]
```

```python
import math
from contextlib import ExitStack

import concourse.bass as bass
from concourse import mybir

f32, f32r, i32, u32 = mybir.dt.float32, mybir.dt.float32r, mybir.dt.int32, mybir.dt.uint32
ALU = mybir.AluOpType
ACT = mybir.ActivationFunctionType
AX = mybir.AxisListType
ds = bass.ds

P = 128
D = 2048
TOK = 256
NT = TOK // P
KT = D // P
BLK = 128
WIDE = 512
KQ = 4
UNIT = KT * BLK
HALF = UNIT // 2
MEM = 256
MEM_HEADS, MEM_DIM = 4, 384
MEM_W = MEM_HEADS * MEM_DIM
MB = MEM_W // P
MC = MEM_DIM // P
HEADS, HD = 8, 128
VD = 2 * HD
ROT, HALF_ROT, THETA = 32, 16, 500000.0
QSCALE, MSCALE = HD ** -0.5, MEM_DIM ** -0.5
LAM_INIT = 0.8 - 0.6 * math.exp(0.0)
ALPHA = 2.0 ** 0.25
EPS = 1e-5
PH, NK, TOPK = 8, 128, 16
GROUPS, GC = 4, 32
GT = 4
STEPS = TOK // GT
HALF0 = GC // 4
LOWEST = -3.0e38
FREE, FREE2 = 1, 2

COL_GATE, COL_AX, COL_Q, COL_K, COL_V = 0, 2048, 4096, 6144, 8192
COL_MQ, COL_G = 10240, 11776
PRE = 4
M_LRU = 0
M_MK = M_LRU + 2 * KT
M_MV = M_MK + MB
M_MQ = M_MV + MEM_W // WIDE * 4
M_MA = M_MQ + MB
M_D = M_MA + 2 * KT
M_MM = M_D + HEADS // 2 * 12
M_MD = M_MM + 2 * KT
M_OUT = M_MD + 2 * KT
M_WQ = M_OUT + D // WIDE * 4
M_EXP = M_WQ + 2 * PH
PAIRS = KT + MB + 2 * HEADS + PH


def layer(nc, x, mem, pos, w_in, b_gate, conv_w, conv_b, lru_w_a, lru_b_a, lru_w_i, lru_b_i, lru_lambda,
          diff_lambda, diff_subln, w_mem_kv, w_lru, w_diff, w_mem, w_out, ln1_g, ln1_b, w_q, sub_keys,
          u_tab, v_tab, ln2_g, ln2_b, out):
    ctx = ExitStack()
    with ctx:
        def sb(name, shape, dt=f32, stack=ctx):
            return stack.enter_context(nc.sbuf_tensor(name, shape, dt))

        def sem(name):
            return ctx.enter_context(nc.semaphore(name))

        raw = [sb(f"raw{s}", [P, UNIT]) for s in range(2)]
        hi = [sb(f"hi{s}", [P, UNIT], f32r) for s in range(2)]
        lo = [sb(f"lo{s}", [P, UNIT], f32r) for s in range(2)]
        ident = sb("ident", [P, P])
        ones1 = sb("ones1", [1, 1])
        vrow = sb("vrow", [P, 2, P])
        vec = sb("vec", [P, 2, P])
        mom = sb("mom", [P, 4, 2])
        nmom = sb("nmom", [P, 2])
        base = ExitStack()

        A = ExitStack()
        brh = sb("brh", [P, KT, TOK], f32r, A)
        brl = sb("brl", [P, KT, TOK], f32r, A)
        S0 = ExitStack()
        rtmp = sb("rtmp", [ROT, 4, TOK], f32, S0)
        posi = sb("posi", [ROT, TOK], i32, S0)
        lp = sb("lp", [P, 4, P], f32, S0)
        S0.close()
        merged = sb("merged", [P, KT, TOK], f32, A)
        mq = sb("mq", [P, MB, TOK], f32, A)
        L = ExitStack()
        axp = sb("axp", [P, TOK + 3], f32, L)
        xc = sb("xc", [P, TOK], f32, L)
        gelu_gate = sb("gelu_gate", [P, TOK], f32, L)
        lru_w = sb("lru_w", [P, 2, 2, P], f32, L)
        t_r = sb("t_r", [P, 2, TOK], f32, L)
        t_i = sb("t_i", [P, 2, TOK], f32, L)
        dec = sb("dec", [P, 2, TOK], f32, L)
        th = sb("th", [P, 2, TOK], f32, L)
        wsq = sb("wsq", [P, 2, TOK], f32, L)
        sq = sb("sq", [P, 2, TOK], f32, L)
        uin = sb("uin", [P, 2, TOK], f32, L)
        hst = sb("hst", [P, 2, TOK], f32, L)
        L.close()
        M = ExitStack()
        mk = sb("mk", [P, MB, MEM], f32, M)
        mv = sb("mv", [P, 2, MEM_W], f32, M)
        M.close()
        S = ExitStack()
        qk = sb("qk", [P, 8, TOK], f32, S)
        vv = sb("vv", [P, 2, WIDE], f32, S)
        ex = sb("ex", [P, 2, 2, 2, TOK], f32, S)
        at = sb("at", [P, 2, 2, TOK], f32, S)
        S.close()
        pad = sb("pad", [P, 24 * 256], f32, A)
        xh = sb("xh", [P, KT, TOK], f32r, A)
        xl = sb("xl", [P, KT, TOK], f32r, A)
        Z1 = ExitStack()
        memh = sb("memh", [P, KT, MEM], f32r, Z1)
        meml = sb("meml", [P, KT, MEM], f32r, Z1)
        Z1.close()
        Z2 = ExitStack()
        brmh = sb("brmh", [P, MB, TOK], f32r, Z2)
        brml = sb("brml", [P, MB, TOK], f32r, Z2)
        Z4 = ExitStack()
        mqs = sb("mqs", [P, MC, TOK], f32, Z4)
        mvs = sb("mvs", [P, 2, MEM_DIM], f32, Z4)
        pm = sb("pm", [P, 2, MEM], f32, Z4)
        Z4.close()
        rsh = sb("rsh", [ROT, 4, TOK], f32, Z2)
        Z2.close()
        Z3 = ExitStack()
        mh = sb("mh", [P, KT, TOK], f32r, Z3)
        ml = sb("ml", [P, KT, TOK], f32r, Z3)
        Z3.close()
        padz = sb("padz", [P, 32 * 256], f32, A)
        gt = sb("gt", [P, TOK], f32, A)
        pt = sb("pt", [P, TOK], f32, A)
        pmT = sb("pmT", [P, 2, TOK], f32, A)
        cosT = sb("cosT", [ROT, TOK], f32, A)
        sinT = sb("sinT", [ROT, TOK], f32, A)
        ifr = sb("ifr", [1, ROT], f32, A)
        ifc = sb("ifc", [ROT, 1], f32, A)
        sgn = sb("sgn", [ROT, 1], f32, A)
        lsum = sb("lsum", [P, 2], f32, A)
        lame = sb("lame", [P, 2], f32, A)
        nlam = sb("nlam", [P, 1], f32, A)
        hb = sb("hb", [P, 64], f32, A)
        sp = sb("sp", [P, 32], f32, A)
        nsp = sb("nsp", [P, 32], f32, A)
        spt = sb("spt", [P, 4, 32], f32, A)
        mx = sb("mx", [P, 8], f32, A)
        nmx = sb("nmx", [P, 8], f32, A)
        zs = sb("zs", [P, 8], f32, A)
        rz = sb("rz", [P, 8], f32, A)
        ssq = sb("ssq", [P, 4], f32, A)
        rstd = sb("rstd", [P, 4], f32, A)
        A.close()

        B = ExitStack()
        hbuf = sb("hbuf", [P, GC, TOK], f32, B)
        gbuf = sb("gbuf", [P, GC, TOK], f32, B)
        acc = sb("acc", [P, NT, D], f32, B)
        res = sb("res", [P, NT, D], f32, B)
        x1h = sb("x1h", [P, KT, TOK], f32r, B)
        x1l = sb("x1l", [P, KT, TOK], f32r, B)
        top_v = sb("top_v", [P, PH, 2, NT, TOPK], f32, B)
        top_i = sb("top_i", [P, PH, 2, NT, TOPK], f32, B)
        cand = sb("cand", [P, TOPK, TOPK], f32, B)
        cand2 = sb("cand2", [P, TOPK * TOPK], f32, B)
        best = sb("best", [P, TOPK], f32, B)
        nbest = sb("nbest", [P, 1], f32, B)
        zb = sb("zb", [P, 1], f32, B)
        rzb = sb("rzb", [P, 1], f32, B)
        eb = sb("eb", [P, TOPK], f32, B)
        ci = sb("ci", [P, TOPK], u32, B)
        ca = sb("ca", [P, TOPK], u32, B)
        cb = sb("cb", [P, TOPK], u32, B)
        caf = sb("caf", [P, 2, TOPK], f32, B)
        hit = sb("hit", [P, TOPK, TOPK], f32, B)
        iota16 = sb("iota16", [P, TOPK], f32, B)
        iota = sb("iota", [P, P], f32, B)
        pick = sb("pick", [P, 3, NT, PH * TOPK], f32, B)
        pickT = sb("pickT", [P, 3, TOK], f32, B)
        gate2 = sb("gate2", [P, 2, TOK], f32r, B)
        i2s = [sb(f"i2s{b}", [P, GT], f32, B) for b in range(2)]
        B1 = ExitStack()
        skT = sb("skT", [P, 2 * PH, NK], f32, B1)
        qT = sb("qT", [P, 2, TOK], f32, B1)
        stv = sb("stv", [P, 2, NT, TOPK], f32, B1)
        sti = sb("sti", [P, 2, NT, TOPK], u32, B1)
        left = sb("left", [P, 2, NT, NK], f32, B1)
        B1.close()
        B2 = ExitStack()
        one2 = [sb(f"one2{b}", [P, GT, P], f32r, B2) for b in range(2)]
        mask = sb("mask", [P, GT, GC], f32, B2)
        one1 = [sb(f"one1{b}", [P, GT, 2, GC], f32r, B2) for b in range(2)]
        wt = sb("wt", [P, TOK], f32, B2)
        wh = [sb(f"wh{s}", [P, TOK], f32r, B2) for s in range(2)]
        wl = [sb(f"wl{s}", [P, TOK], f32r, B2) for s in range(2)]
        B2.close()
        B.close()

        ps = [ctx.enter_context(nc.psum_tensor(f"ps{b}", [P, 512], f32)) for b in range(8)]
        psU, psT, psS = ps[0:2], ps[2:6], ps[6:8]

        raw_in = [sem("raw_in0"), sem("raw_in1")]
        hi_made = sem("hi_made")
        lo_made = sem("lo_made")
        units_done = sem("units_done")
        turned = sem("turned")
        bank_read = [sem("bank_read0"), sem("bank_read1")]
        tok_read = sem("tok_read")
        consts = sem("consts")
        small_in = sem("small_in")
        vec_turned, vec_ready, set_dve, set_act = sem("vec_turned"), sem("vec_ready"), sem("set_dve"), sem("set_act")
        lru_in, lru_mm, gates_read = sem("lru_in"), sem("lru_mm"), sem("gates_read")
        xc_made, decays, w_made, root_made = sem("xc_made"), sem("decays"), sem("w_made"), sem("root_made")
        br_made, br_hi, br_lo = sem("br_made"), sem("br_hi"), sem("br_lo")
        in_made = sem("in_made")
        kv_made = sem("kv_made")
        staged = sem("staged")
        mscore, mmax, mexp, mprob, mturned, mpT, mpv, mhi, mlo = (sem("mem_" + n) for n in (
            "score", "max", "exp", "prob", "turned", "probT", "pv", "hi", "lo"))
        gate_made, merge_made, mg_hi, mg_lo = sem("gate_made"), sem("merge_made"), sem("mg_hi"), sem("mg_lo")
        qk_made, rotated, score, smax, sexp, attn, aturned, atT, pv, sqsum, onorm, oturned, ohi, olo, srt = (
            sem("d_" + n) for n in ("qk", "rotated", "score", "max", "exp", "attn", "turned", "attnT", "pv",
                                    "sqsum", "onorm", "oturned", "hi", "lo", "root"))
        res_in, sub_in, ln1_in, ln2_in = sem("res_in"), sem("sub_in"), sem("ln1_in"), sem("ln2_in")
        ln_dve, ln_act, ln_done = sem("ln_dve"), sem("ln_act"), sem("ln_done")
        x1_hi, x1_lo, sub_turned, sk_made = sem("x1_hi"), sem("x1_lo"), sem("sub_turned"), sem("sk_made")
        x1_turned = sem("x1_turned")
        q_made, key_score, top_done = sem("q_made"), sem("key_score"), sem("top_done")
        best_made, best_exp, pick_made, pick_turned, pickT_made, split_gate = (
            sem(n) for n in ("best_made", "best_exp", "pick_made", "pick_turned", "pickT_made", "split_gate"))
        i2_staged, one2_made, one1_made, gate_mm, gate_read = (
            sem(n) for n in ("i2_staged", "one2_made", "one1_made", "gate_mm", "gate_read"))
        h_made, w_ready, w_hi, w_lo, acc_read = sem("h_made"), sem("w_ready"), sem("w_hi"), sem("w_lo"), sem("acc_read")
        out_done = sem("out_done")
        passed = sem("passed")
        dve_link, act_link = sem("dve_link"), sem("act_link")

        def settle(eng):
            eng.sem_inc(passed, 1)

        class Link:

            def __init__(self, eng, s):
                self.eng, self.sem, self.n, self.off = eng, s, 0, 0

            def __call__(self, ins):
                ins.then_inc(self.sem, 1)
                self.n += 1
                self.eng.wait_ge(self.sem, self.off + self.n)

            def loop(self, count, per, first=0):
                return _Loop(self, count, per, first)

        class _Loop:

            def __init__(self, link, count, per, first):
                self.link, self.count, self.per, self.first = link, count, per, first

            def __enter__(self):
                self.fori = self.link.eng.Fori(self.first, self.first + self.count)
                i = self.fori.__enter__()
                self.start = self.link.n
                self.link.off = (i - self.first) * self.per
                return i

            def __exit__(self, *e):
                got = self.link.n - self.start
                assert e[0] or got == self.per, f"{got} steps, not {self.per}"
                self.link.off = 0
                self.link.n = self.start + self.count * self.per
                return self.fori.__exit__(*e)

        def rows(w):
            return w.rearrange("(k p) c -> p k c", p=P)

        win_v, kv_v = rows(w_in[0]), rows(w_mem_kv[0])
        lru_v, diff_v, mem_v, out_v, wq_v = (rows(w[0]) for w in (w_lru, w_diff, w_mem, w_out, w_q))
        u_v = u_tab[0].rearrange("(c p) d -> p c d", p=P)
        v_v = v_tab[0].rearrange("(c p) d -> p c d", p=P)
        k3 = lambda t: t[:, :].rearrange("p (k c) -> p k c", c=BLK)
        w3 = lambda t: t[:, :].rearrange("p (k c) -> p k c", c=WIDE)

        start_free = ((FREE, (lru_mm, mpv, br_made, merge_made, score, key_score, best_exp, w_lo, gates_read, tok_read,
                              mlo, olo, top_done, bank_read[0], bank_read[1])), (FREE2, (gate_mm, gate_read)))

        block = ctx.enter_context(nc.Block())

        @block.sync
        def _(sp_):
            def load(m, s, dst, src, first=False):
                if not first:
                    sp_.wait_ge(lo_made, (m + (PRE - 1)) * 4)
                    settle(sp_)
                sp_.dma_start(dst, src).then_inc(raw_in[s], 16)

            for r, (src, t) in enumerate(((x, 0), (x, 1), (mem, 0), (mem, 1))):
                load(r - PRE, r % 2, raw[r % 2][:, :], src[0, t * P:(t + 1) * P, :], first=r < 2)

            def col(m, s, view, c):
                load(m, s, k3(raw[s]), view[:, :, ds(c, BLK)])

            with sp_.Fori(0, KT) as i:
                col(M_LRU + 2 * i, 0, win_v, COL_AX + i * BLK)
                col(M_LRU + 2 * i + 1, 1, win_v, COL_GATE + i * BLK)
            with sp_.Fori(0, MB // 2) as i:
                for s in range(2):
                    col(M_MK + 2 * i + s, s, kv_v, i * (2 * BLK) + s * BLK)
            with sp_.Fori(0, MEM_W // WIDE) as g:
                for j in range(4):
                    load(M_MV + 4 * g + j, j % 2, w3(raw[j % 2]), kv_v[:, j * KQ:(j + 1) * KQ, ds(MEM_W + g * WIDE, WIDE)])
            with sp_.Fori(0, MB // 2) as i:
                for s in range(2):
                    col(M_MQ + 2 * i + s, s, win_v, COL_MQ + i * (2 * BLK) + s * BLK)
            with sp_.Fori(0, KT) as i:
                col(M_MA + 2 * i, 0, win_v, COL_G + i * BLK)
                col(M_MA + 2 * i + 1, 1, lru_v, i * BLK)
            with sp_.Fori(0, HEADS // 2) as p:
                for j in range(8):
                    c = (COL_Q if j < 4 else COL_K) + (j % 4) * BLK
                    col(M_D + 12 * p + j, j % 2, win_v, c + p * (4 * BLK))
                for j in range(4):
                    load(M_D + 12 * p + 8 + j, j % 2, w3(raw[j % 2]),
                         win_v[:, j * KQ:(j + 1) * KQ, ds(COL_V + p * WIDE, WIDE)])
            with sp_.Fori(0, KT) as i:
                col(M_MM + 2 * i, 0, win_v, COL_G + 2 * D + i * BLK)
                load(M_MM + 2 * i + 1, 1, k3(raw[1])[:, 0:MB, :], mem_v[:, :, ds(i * BLK, BLK)])
            with sp_.Fori(0, KT) as i:
                col(M_MD + 2 * i, 0, win_v, COL_G + D + i * BLK)
                col(M_MD + 2 * i + 1, 1, diff_v, i * BLK)
            with sp_.Fori(0, D // WIDE) as g:
                for j in range(4):
                    load(M_OUT + 4 * g + j, j % 2, w3(raw[j % 2]), out_v[:, j * KQ:(j + 1) * KQ, ds(g * WIDE, WIDE)])
            with sp_.Fori(0, PH) as h:
                for s in range(2):
                    col(M_WQ + 2 * h + s, s, wq_v, h * (2 * BLK) + s * BLK)
            for g in range(GROUPS):
                for n, tab in enumerate((u_v, v_v)):
                    m0 = M_EXP + (2 * g + n) * GC
                    with sp_.Fori(0, GC // 2) as i:
                        for s in range(2):
                            load(m0 + 2 * i + s, s, raw[s][:, :],
                                 tab[:, ds(g * GC + 2 * i + s, 1), :].rearrange("p a d -> p (a d)"))
            sp_.wait_ge(w_ready, GROUPS * GC)
            for n, v in enumerate((ln2_g, ln2_b)):
                sp_.dma_start(gbuf[:, 8 * n:8 * n + 8, :].rearrange("p a b -> p (a b)"),
                              v[0].partition_broadcast(P)).then_inc(ln2_in, 16)
            for t in range(NT):
                sp_.wait_ge(ln_done, NT + t + 1)
                sp_.dma_start(out[0, t * P:(t + 1) * P, :], res[:, t, :]).then_inc(out_done, 16)
            sp_.wait_ge(out_done, 16 * NT)

        @block.gpsimd
        def _(pool):
            for n, sems in start_free:
                for s_ in sems:
                    pool.sem_inc(s_, n)
            pool.memset(ident[:, :], 0.0).then_inc(consts, 1)
            pool.memset(ones1[:, :], 1.0).then_inc(consts, 1)
            pool.memset(axp[:, :], 0.0).then_inc(consts, 1)
            pool.memset(sgn[:, :], 1.0).then_inc(consts, 1)
            for j in range(HALF_ROT):
                pool.memset(ifr[0:1, j:ROT:HALF_ROT], float(THETA ** (-j / HALF_ROT))).then_inc(consts, 1)
            n = 4 + HALF_ROT
            pool.wait_ge(consts, n)
            pool.affine_select(out=ident[:, :], in_=ident[:, :], compare_op=ALU.not_equal, fill=1.0, base=0,
                               pattern=[[-1, P]], channel_multiplier=1).then_inc(consts, 1)
            pool.memset(sgn[0:HALF_ROT, :], -1.0).then_inc(consts, 1)
            v1 = ((conv_w[0].rearrange("j (n p) -> (j n) p", p=P), 0, 64), (conv_b.rearrange("a (n p) -> (a n) p", p=P), 64, 16),
                  (b_gate.rearrange("a (n p) -> (a n) p", p=P), 80, 48))
            v2 = ((lru_b_a[0].rearrange("d (n p) -> (d n) p", p=P), 0, 32), (lru_b_i[0].rearrange("d (n p) -> (d n) p", p=P), 32, 32),
                  (lru_lambda[0].rearrange("d (n p) -> (d n) p", p=P), 64, 32),
                  (diff_subln.rearrange("a (n p) -> (a n) p", p=P), 96, 2))
            for k, vs in enumerate((v1, v2)):
                for src, at0, cnt in vs:
                    pool.dma_start(vrow[at0:at0 + cnt, k, :], src).then_inc(small_in, 16)
            pool.dma_start(lp[:, :, :].rearrange("p a b -> p (a b)"),
                           diff_lambda[0].rearrange("a b -> (a b)").partition_broadcast(P)).then_inc(small_in, 16)
            pool.dma_start(posi[:, :], pos[0].partition_broadcast(ROT)).then_inc(small_in, 16)
            with pool.Fori(0, KT) as i:
                pool.wait_ge(lru_mm, i + FREE)
                for k, w in enumerate((lru_w_a, lru_w_i)):
                    pool.dma_start(lru_w[:, k, :, :], w[0].rearrange("d n i j -> i n d j")[:, ds(i, 1), :, :]
                                   .rearrange("i a d j -> i (a d) j")).then_inc(lru_in, 16)
            with pool.Fori(0, MEM_HEADS) as h:
                pool.wait_ge(kv_made, MB + MEM_W // WIDE + MB)
                pool.wait_ge(mpv, h + FREE)
                pool.tensor_copy(mqs[:, :, :], mq[:, ds(h * MC, MC), :]).then_inc(staged, 1)
                pool.tensor_copy(mvs[:, :, :], mv[:, :, ds(h * MEM_DIM, MEM_DIM)]).then_inc(staged, 1)
            pool.wait_ge(units_done, 2 * M_OUT)
            for t in range(NT):
                pool.dma_start(res[:, t, :], x[0, t * P:(t + 1) * P, :]).then_inc(res_in, 16)
            for v, dst in ((ln1_g, 0), (ln1_b, 8)):
                pool.dma_start(hbuf[:, dst:dst + 8, :].rearrange("p a b -> p (a b)"),
                               v[0].partition_broadcast(P)).then_inc(ln1_in, 16)
            pool.dma_start(gbuf[:, 0:8, :].rearrange("p a b -> p (a b)").rearrange("p (a b) -> p a b", b=P),
                           sub_keys[0].rearrange("h j n c -> n (h j) c")).then_inc(sub_in, 16)
            pool.wait_ge(ln_done, NT)
            pool.iota(iota[:, :], [[1, P]], base=0, channel_multiplier=0,
                      allow_small_or_imprecise_dtypes=True).then_inc(consts, 1)
            pool.iota(iota16[:, :], [[1, TOPK]], base=0, channel_multiplier=0,
                      allow_small_or_imprecise_dtypes=True).then_inc(consts, 1)
            pool.wait_ge(consts, n + 4)
            def one_hot2(n, b, step):
                pool.wait_ge(i2_staged, n + 1)
                pool.wait_ge(gate_mm, step - 1 + FREE2)
                settle(pool)
                for k in range(GT):
                    last = pool.tensor_scalar(one2[b][:, k, :], iota[:, :], i2s[b][:, k:k + 1], None, ALU.is_equal)
                last.then_inc(one2_made, 1)

            with pool.Fori(0, STEPS // 2) as n:
                one_hot2(n, 0, 2 * n)
            with pool.Fori(0, (GROUPS - 1) * STEPS // 2) as n:
                for b in range(2):
                    one_hot2(2 * n + STEPS // 2 + b, b, 2 * n + STEPS + b)

        @block.scalar
        def _(act):
            link = Link(act, act_link)

            def split(m, s, free=True):
                act.wait_ge(raw_in[s], (m + PRE - s) * 8 + 16)
                for q in range(2):
                    if free:
                        act.wait_ge(units_done, 2 * m - 3 + q)
                    act.activation(hi[s][:, q * HALF:(q + 1) * HALF], raw[s][:, q * HALF:(q + 1) * HALF],
                                   ACT.Copy).then_inc(hi_made, 2)

            def split_turned(m, s, j):
                for b in range(4):
                    if b % 2 == 0:
                        act.wait_ge(units_done, 2 * m - 3 + b // 2)
                    act.wait_ge(turned, j * 4 + (b + 1))
                    act.activation(hi[s][:, b * 512:(b + 1) * 512], psT[b][:, :], ACT.Copy).then_inc(hi_made, 1)

            def result(m, b):
                act.wait_ge(units_done, 2 * m + 2)

            act.wait_ge(vec_turned, 1)
            act.activation(vec[:, :, :].rearrange("p a b -> p (a b)")[:, 0:P + 98], psS[0][:, 0:P + 98], ACT.Copy).then_inc(set_act, 1)
            act.activation(ifc[:, :], psS[1][0:ROT, 0:1], ACT.Copy).then_inc(set_act, 1)
            for r in range(PRE):
                dst, t = (xh, r) if r < 2 else (memh, r - 2)
                for b in range(4):
                    act.wait_ge(turned, 4 * r + b + 1)
                    act.activation(dst[:, 4 * b:4 * b + 4, t * P:(t + 1) * P],
                                   psT[b][:, :].rearrange("p (k c) -> p k c", c=P), ACT.Copy).then_inc(hi_made, 1)
            split(0, 0, free=False)
            act.wait_ge(set_dve, 1)
            act.activation(spt[:, 1, :], spt[:, 0, :], ACT.Exp, scale=-1.0).then_inc(set_act, 1)
            act.activation(lame[:, :], lsum[:, :], ACT.Exp).then_inc(set_act, 1)
            act.wait_ge(set_dve, 2)
            act.activation(sinT[:, :], rtmp[:, 2, :], ACT.Sin).then_inc(set_act, 1)
            act.activation(cosT[:, :], rtmp[:, 3, :], ACT.Sin).then_inc(set_act, 1)
            act.wait_ge(set_dve, 3)

            def lru_decays(i):
                act.wait_ge(gates_read, i + 1 + FREE)
                act.wait_ge(br_made, i + FREE)
                for d in range(2):
                    act.activation(dec[:, d, :], t_r[:, d, :], ACT.Exp, bias=nsp[:, ds(i + 16 * d, 1)], scale=nsp[:, ds(i + 16 * d, 1)])
                    last = act.activation(th[:, d, :], t_r[:, d, :], ACT.Tanh, bias=sp[:, ds(i + 16 * d, 1)], scale=sp[:, ds(i + 16 * d, 1)])
                last.then_inc(decays, 1)

            def lru_root(i):
                act.wait_ge(w_made, i + 1)
                act.activation(sq[:, :, :], wsq[:, :, :], ACT.Sqrt).then_inc(root_made, 1)

            def lru_out(i):
                act.wait_ge(br_made, i + 1 + FREE)
                act.activation(brh[:, ds(i, 1), :].rearrange("p a t -> p (a t)"), uin[:, 0, :], ACT.Copy).then_inc(br_hi, 1)

            def lru_gates(i):
                result(M_LRU + 2 * i + 1, 1)
                act.activation(gelu_gate[:, :], psU[1][:, 0:TOK], ACT.Gelu).then_inc(bank_read[1], 1)
                act.wait_ge(lru_mm, i + 1 + FREE)
                for d in range(2):
                    act.activation(t_i[:, d, :], psT[d][:, TOK:2 * TOK], ACT.Tanh, bias=hb[:, ds(i + 32 + 16 * d, 1)], scale=0.5)
                    last = act.activation(t_r[:, d, :], psT[d][:, 0:TOK], ACT.Tanh, bias=hb[:, ds(i + 16 * d, 1)], scale=0.5)
                last.then_inc(gates_read, 1)

            split(M_LRU + 1, 1, free=False)
            split(M_LRU + 2, 0)
            lru_gates(0)
            with act.Fori(1, KT) as i:
                m = M_LRU + 2 * i
                split(m + 1, 1)
                lru_decays(i - 1)
                split(m + 2, 0)
                lru_root(i - 1)
                lru_out(i - 1)
                lru_gates(i)
            lru_decays(KT - 1)
            lru_root(KT - 1)
            lru_out(KT - 1)

            with act.Fori(0, MB // 2) as i:
                m = M_MK + 2 * i
                for s in range(2):
                    split(m + 1 + s, 1 - s)
                    result(m + s, s)
                    act.activation(mk[:, ds(2 * i + s, 1), :].rearrange("p a t -> p (a t)"), psU[s][:, 0:MEM],
                                   ACT.Copy).then_inc(bank_read[s], 1)
            with act.Fori(0, MEM_W // WIDE) as g:
                for j in range(4):
                    split(M_MV + 4 * g + j + 1, (j + 1) % 2)
            with act.Fori(0, MB // 2) as i:
                m = M_MQ + 2 * i
                for s in range(2):
                    split(m + 1 + s, 1 - s)
                    result(m + s, s)
                    act.activation(mq[:, ds(2 * i + s, 1), :].rearrange("p a t -> p (a t)"), psU[s][:, 0:TOK],
                                   ACT.Copy).then_inc(bank_read[s], 1)

            def gate(m, col):
                result(m, 0)
                act.activation(gt[:, :], psU[0][:, 0:TOK], ACT.Sigmoid, bias=vec[:, 0, ds(col + 80, 1)]).then_inc(bank_read[0], 1)

            with act.Fori(0, MEM_HEADS) as h:
                for k in range(4):
                    m = M_MA + 8 * h + 2 * k
                    split(m + 1, 1)
                    act.wait_ge(merge_made, 4 * h + k + FREE)
                    gate(m, 4 * h + k)
                    split(m + 2, 0)
                    if k == 0:
                        act.wait_ge(mmax, h + 1)
                        for t in range(NT):
                            last = act.activation(pm[:, t, :], psS[t][:, 0:MEM], ACT.Exp, bias=nmx[:, t:t + 1],
                                                  scale=MSCALE, accum_out=zs[:, t:t + 1])
                        last.then_inc(mexp, 1)
                    if k == 2:
                        act.wait_ge(mturned, h + 1)
                        act.activation(pmT[:, :, :].rearrange("p a t -> p (a t)"), psT[2][:, :], ACT.Copy).then_inc(mpT, 1)
                    if k == 3:
                        act.wait_ge(mpv, h + 1 + FREE)
                        for c in range(MC):
                            act.activation(brmh[:, ds(h * MC + c, 1), :].rearrange("p a t -> p (a t)"),
                                           psT[(0, 1, 3)[c]][:, 0:TOK], ACT.Copy).then_inc(mhi, 1)

            with act.Fori(0, HEADS // 2) as p:
                m = M_D + 12 * p
                for j in range(8):
                    split(m + j + 1, (j + 1) % 2)
                    result(m + j, j % 2)
                    if j == 0:
                        act.wait_ge(score, 2 * p + FREE)
                    act.activation(qk[:, j, :], psU[j % 2][:, 0:TOK], ACT.Copy).then_inc(bank_read[j % 2], 1)
                split(m + 9, 1)
                split(m + 10, 0)
                for hh in range(2):
                    act.wait_ge(smax, 2 * p + hh + 1)
                    for t in range(NT):
                        for j in range(2):
                            c = 4 * hh + 2 * t + j
                            last = act.activation(ex[:, hh, t, j, :], (psS, psT[2:4])[hh][t][:, j * TOK:(j + 1) * TOK], ACT.Exp,
                                                  bias=nmx[:, c:c + 1], scale=QSCALE, accum_out=zs[:, c:c + 1])
                    last.then_inc(sexp, 1)
                split(m + 11, 1)
                split(m + 12, 0)
                for hh in range(2):
                    act.wait_ge(aturned, 2 * p + hh + 1)
                    act.activation(at[:, hh, :, :].rearrange("p a t -> p (a t)"), psS[hh][:, :], ACT.Copy).then_inc(atT, 1)
                for hh in range(2):
                    act.wait_ge(pv, 2 * p + hh + 1)
                    for t in range(NT):
                        last = act.activation(ex[:, hh, t, 1, :], psT[2 + hh][:, t * VD:(t + 1) * VD], ACT.Square,
                                              accum_out=ssq[:, 2 * hh + t:2 * hh + t + 1])
                last.then_inc(sqsum, 1)
                act.wait_ge(srt, 2 * p + 1)
                act.activation(rstd[:, :], ssq[:, :], ACT.Sqrt).then_inc(sqsum, 1)
                for hh in range(2):
                    act.wait_ge(oturned, 2 * p + hh + 1)
                    for c in range(2):
                        act.activation(brh[:, ds(4 * p + 2 * hh + c, 1), :].rearrange("p a t -> p (a t)"),
                                       psS[hh][:, c * TOK:(c + 1) * TOK], ACT.Copy, scale=vec[:, 1, 98 + c:99 + c]).then_inc(ohi, 1)

            for base_m, col, n0 in ((M_MM, 32, 1), (M_MD, 16, 2)):
                with act.Fori(0, KT) as i:
                    m = base_m + 2 * i
                    split(m + 1, 1)
                    act.wait_ge(merge_made, n0 * KT + i + FREE)
                    gate(m, i + col)
                    split(m + 2, 0)
                    if n0 == 2:
                        act.wait_ge(merge_made, n0 * KT + i + 1 + FREE)
                        act.activation(mh[:, ds(i, 1), :].rearrange("p a t -> p (a t)"),
                                       merged[:, ds(i, 1), :].rearrange("p a t -> p (a t)"), ACT.Copy).then_inc(mg_hi, 1)

            with act.Fori(0, D // WIDE) as g:
                for j in range(4):
                    split(M_OUT + 4 * g + j + 1, (j + 1) % 2)

            def norm_act(k):
                for t in range(NT):
                    act.wait_ge(ln_dve, (k * NT + t) * 2 + 1)
                    act.activation(acc[:, t, :], res[:, t, :], ACT.Square, bias=nmom[:, t:t + 1],
                                   accum_out=mom[:, 1, t:t + 1]).then_inc(ln_act, 1)
                    act.wait_ge(ln_dve, (k * NT + t) * 2 + 2)
                    act.activation(mom[:, 2, t:t + 1], mom[:, 1, t:t + 1], ACT.Sqrt).then_inc(ln_act, 1)

            norm_act(0)
            for b in range(4):
                act.wait_ge(sub_turned, b + 1)
                act.activation(skT[:, 4 * b:4 * b + 4, :].rearrange("p a n -> p (a n)"), psT[b][:, :], ACT.Copy).then_inc(sk_made, 1)
            for t in range(NT):
                for b in range(4):
                    act.wait_ge(x1_turned, 4 * t + b + 1)
                    act.activation(x1h[:, 4 * b:4 * b + 4, t * P:(t + 1) * P],
                                   psT[b][:, :].rearrange("p (k c) -> p k c", c=P), ACT.Copy).then_inc(x1_hi, 1)

            def queries(h, m, after):
                split(m + 1, 1)
                act.wait_ge(key_score, 2 * h + FREE)
                result(m, 0)
                act.activation(qT[:, 0, :], psU[0][:, 0:TOK], ACT.Copy).then_inc(bank_read[0], 1)
                after()
                result(m + 1, 1)
                act.activation(qT[:, 1, :], psU[1][:, 0:TOK], ACT.Copy).then_inc(bank_read[1], 1)

            with act.Fori(0, PH - 1) as h:
                queries(h, M_WQ + 2 * h, lambda: split(M_WQ + 2 * h + 2, 0))
            queries(PH - 1, M_WQ + 2 * PH - 2, lambda: split_turned(M_EXP, 0, PRE))

            def take_h(m, s, c):
                result(m, s)
                act.activation(hbuf[:, ds(c, 1), :].rearrange("p a t -> p (a t)"), psU[s][:, 0:TOK],
                               ACT.Gelu).then_inc(bank_read[s], 1)

            def split_w(m, s, n):
                act.wait_ge(w_ready, n + 1)
                act.wait_ge(units_done, 2 * m - 2)
                act.activation(wh[s][:, :], wt[:, :], ACT.Copy).then_inc(w_hi, 1)

            def best_gates(n):
                act.wait_ge(best_made, n + 1)
                act.activation(eb[:, :], best[:, :], ACT.Exp, bias=nbest[:, 0:1], accum_out=zb[:, 0:1]).then_inc(best_exp, 1)

            for g in range(GROUPS):
                mu, mv_ = M_EXP + 2 * g * GC, M_EXP + (2 * g + 1) * GC
                ju = PRE + g * GC

                def pair(i, last=False, extra=lambda i, s: None):
                    m = mu + 2 * i
                    split_turned(m + 1, 1, ju + 2 * i + 1)
                    take_h(m, 0, 2 * i)
                    extra(i, 0)
                    if last:
                        split(m + 2, 0)
                    else:
                        split_turned(m + 2, 0, ju + 2 * i + 2)
                    take_h(m + 1, 1, 2 * i + 1)
                    extra(i, 1)

                if g > 0:
                    act.wait_ge(w_ready, g * GC)
                    with act.Fori(0, GC // 2 - 1) as i:
                        pair(i)
                else:
                    with act.Fori(0, HALF0) as i:
                        pair(i, extra=lambda i, s: best_gates(2 * i + s))
                    act.wait_ge(pick_turned, 1)
                    act.activation(pickT[:, 0:2, :].rearrange("p a t -> p (a t)"), psS[1][:, :], ACT.Copy).then_inc(pickT_made, 1)
                    act.activation(pickT[:, 2, :], psS[0][:, 0:TOK], ACT.Copy).then_inc(pickT_made, 1)
                    act.wait_ge(pickT_made, 2)
                    act.activation(gate2[:, 0, :], pickT[:, 2, :], ACT.Copy).then_inc(split_gate, 1)
                    with act.Fori(HALF0, GC // 2 - 1) as i:
                        pair(i)
                pair(GC // 2 - 1, last=True)
                split_w(mv_, 0, g * GC)

                def vpair(i, last=False):
                    m = mv_ + 2 * i
                    split(m + 1, 1)
                    split_w(m + 1, 1, g * GC + 2 * i + 1)
                    if not last:
                        split(m + 2, 0)
                        split_w(m + 2, 0, g * GC + 2 * i + 2)
                    elif g + 1 < GROUPS:
                        split_turned(m + 2, 0, ju + GC)

                with act.Fori(0, GC // 2 - 1) as i:
                    vpair(i)
                vpair(GC // 2 - 1, last=True)
            norm_act(1)

        @block.vector
        def _(dve):
            link = Link(dve, dve_link)

            def split(m, s):
                for q in range(2):
                    dve.wait_ge(hi_made, (m + PRE) * 4 + 2 * (q + 1))
                    h = slice(q * HALF, (q + 1) * HALF)
                    dve.tensor_tensor(lo[s][:, h], raw[s][:, h], hi[s][:, h].bitcast(f32), ALU.subtract).then_inc(lo_made, 2)

            def split_turned(m, s):
                for b in range(4):
                    dve.wait_ge(hi_made, (m + PRE) * 4 + (b + 1))
                    h = slice(b * 512, (b + 1) * 512)
                    dve.tensor_tensor(lo[s][:, h], psT[b][:, :], hi[s][:, h].bitcast(f32), ALU.subtract).then_inc(lo_made, 1)

            for r in range(PRE):
                src, dst, t = (xh, xl, r) if r < 2 else (memh, meml, r - 2)
                for b in range(4):
                    dve.wait_ge(hi_made, 4 * r + b + 1)
                    w = (slice(None), slice(4 * b, 4 * b + 4), slice(t * P, (t + 1) * P))
                    dve.tensor_tensor(dst[w], psT[b][:, :].rearrange("p (k c) -> p k c", c=P), src[w].bitcast(f32),
                                      ALU.subtract).then_inc(lo_made, 1)
            split(0, 0)
            dve.wait_ge(set_act, 2)
            dve.wait_ge(small_in, 9 * 16)
            dve.tensor_scalar(hb[:, :], vec[:, 1, 0:64], 0.5, None, ALU.mult)
            dve.scalar_tensor_tensor(spt[:, 0, :], vec[:, 1, 64:96], -1.0, vec[:, 1, 64:96], ALU.mult, ALU.max)
            link(dve.tensor_tensor(lp[:, 0:4:2, :], lp[:, 0:4:2, :], lp[:, 1:4:2, :], ALU.mult))
            dve.tensor_reduce(lsum[:, :], lp[:, 0:4:2, :], AX.X, ALU.add).then_inc(set_dve, 1)
            ang, turns, red, cang = (rtmp[:, k, :] for k in range(4))
            link(dve.tensor_copy(turns, posi[:, :]))
            link(dve.tensor_scalar(ang, turns, ifc[:, 0:1], None, ALU.mult))
            magic = 1.5 * 2.0 ** 23
            link(dve.tensor_scalar(turns, ang, 1.0 / (2 * math.pi), magic, ALU.mult, ALU.add))
            link(dve.tensor_scalar(turns, turns, -magic, None, ALU.add))
            c1 = 6.28125
            c2 = math.floor((2 * math.pi - c1) * 2.0 ** 20) / 2.0 ** 20
            c3 = 2 * math.pi - c1 - c2
            link(dve.scalar_tensor_tensor(red, turns, -c1, ang, ALU.mult, ALU.add))
            link(dve.scalar_tensor_tensor(red, turns, -c2, red, ALU.mult, ALU.add))
            link(dve.scalar_tensor_tensor(red, turns, -c3, red, ALU.mult, ALU.add))
            link(dve.tensor_scalar(red, red, 3.1415925, -3.1415925, ALU.min, ALU.max))
            link(dve.scalar_tensor_tensor(cang, red, -1.0, red, ALU.mult, ALU.min))
            dve.tensor_scalar(cang, cang, math.pi / 2, None, ALU.add).then_inc(set_dve, 1)
            dve.wait_ge(set_act, 4)
            s0, e_, r_, s2 = (spt[:, k, :] for k in range(4))
            link(dve.tensor_scalar(r_, e_, 2.0, None, ALU.add))
            link(dve.reciprocal(r_, r_))
            link(dve.tensor_tensor(r_, r_, e_, ALU.mult))
            link(dve.tensor_tensor(s2, r_, r_, ALU.mult))
            link(dve.tensor_scalar(s0, s2, 1.0 / 17, None, ALU.mult))
            for k in (15, 13, 11, 9, 7, 5, 3):
                link(dve.scalar_tensor_tensor(s0, s0, 1.0 / k, s2, ALU.add, ALU.mult))
            link(dve.scalar_tensor_tensor(s0, s0, 1.0, r_, ALU.add, ALU.mult))
            link(dve.tensor_scalar(e_, vec[:, 1, 64:96], -1.0, 0.0, ALU.mult, ALU.max))
            link(dve.scalar_tensor_tensor(s0, s0, 2.0, e_, ALU.mult, ALU.add))
            link(dve.tensor_scalar(sp[:, :], s0, 4.0, None, ALU.mult))
            link(dve.tensor_scalar(nsp[:, :], sp[:, :], -1.0, None, ALU.mult))
            link(dve.tensor_tensor(nlam[:, :], lame[:, 1:2], lame[:, 0:1], ALU.subtract))
            link(dve.tensor_scalar(nlam[:, :], nlam[:, :], -LAM_INIT, None, ALU.add))
            link(dve.tensor_scalar(vec[:, 1, 98:100], vec[:, 1, 96:98], 1.0 - LAM_INIT, None, ALU.mult))
            dve.wait_ge(set_act, 6)
            dve.tensor_scalar(sinT[:, :], sinT[:, :], sgn[:, 0:1], None, ALU.mult).then_inc(set_dve, 1)

            def conv(i):
                dve.wait_ge(units_done, 2 * (M_LRU + 2 * i) + 2)
                dve.tensor_copy(axp[:, 1:TOK + 1], psU[0][:, 0:TOK]).then_inc(bank_read[0], 1)
                dve.wait_ge(bank_read[0], i + 1 + FREE)
                link(dve.tensor_scalar(xc[:, :], axp[:, 0:TOK], vec[:, 0, ds(i, 1)], vec[:, 0, ds(i + 64, 1)], ALU.mult, ALU.add))
                for j in (1, 2):
                    link(dve.scalar_tensor_tensor(xc[:, :], axp[:, j:TOK + j], vec[:, 0, ds(i + 16 * j, 1)], xc[:, :], ALU.mult, ALU.add))
                dve.scalar_tensor_tensor(xc[:, :], axp[:, 3:TOK + 3], vec[:, 0, ds(i + 48, 1)], xc[:, :], ALU.mult, ALU.add).then_inc(xc_made, 1)

            def lru_in_(i):
                dve.wait_ge(gates_read, i + 1 + FREE)
                dve.scalar_tensor_tensor(uin[:, :, :], t_i[:, :, :], 1.0,
                                         xc[:, :].unsqueeze(1).broadcast_to([P, 2, TOK]), ALU.add, ALU.mult).then_inc(in_made, 1)

            def lru_square(i):
                dve.wait_ge(decays, i + 1)
                link(dve.tensor_tensor(wsq[:, :, :], dec[:, :, :], dec[:, :, :], ALU.mult))
                dve.scalar_tensor_tensor(wsq[:, :, :], wsq[:, :, :], 1.0, th[:, :, :], ALU.add, ALU.mult).then_inc(w_made, 1)

            def lru_scan(i):
                dve.wait_ge(in_made, i + 1)
                dve.wait_ge(root_made, i + 1)
                link(dve.scalar_tensor_tensor(uin[:, :, :], sq[:, :, :], 0.5, uin[:, :, :], ALU.mult, ALU.mult))
                dve.tensor_tensor_scan(hst[:, 0, :], dec[:, 0, :], uin[:, 0, :], 0.0, ALU.mult, ALU.add)
                link(dve.tensor_tensor_scan(hst[:, 1, ::-1], dec[:, 1, ::-1], uin[:, 1, ::-1], 0.0, ALU.mult, ALU.add))
                link(dve.tensor_tensor(hst[:, 0, :], hst[:, 0, :], hst[:, 1, :], ALU.add))
                dve.tensor_tensor(uin[:, 0, :], hst[:, 0, :], gelu_gate[:, :], ALU.mult).then_inc(br_made, 1)
                dve.wait_ge(br_hi, i + 1)
                link(dve.tensor_tensor(brl[:, ds(i, 1), :].rearrange("p a t -> p (a t)"), uin[:, 0, :],
                                       brh[:, ds(i, 1), :].rearrange("p a t -> p (a t)").bitcast(f32), ALU.subtract))

            split(M_LRU + 1, 1)
            conv(0)
            split(M_LRU + 2, 0)
            with link.loop(KT - 1, 8, first=1) as i:
                m = M_LRU + 2 * i
                split(m + 1, 1)
                lru_in_(i - 1)
                conv(i)
                lru_square(i - 1)
                split(m + 2, 0)
                lru_scan(i - 1)
            lru_in_(KT - 1)
            lru_square(KT - 1)
            lru_scan(KT - 1)

            def wide(m, split_, n, take):
                for j in range(4):
                    split_(m + j + 1, (j + 1) % 2)
                dve.wait_ge(units_done, 2 * m + 8)
                take()

            with dve.Fori(0, MB // 2) as i:
                for s in range(2):
                    split(M_MK + 2 * i + s + 1, 1 - s)
            with dve.Fori(0, MEM_W // WIDE) as g:
                def take():
                    for t in range(2):
                        last = dve.tensor_copy(mv[:, t, ds(g * WIDE, WIDE)], psT[t][:, :])
                    last.then_inc(tok_read, 1)
                wide(M_MV + 4 * g, split, g, take)
            with dve.Fori(0, MB // 2) as i:
                for s in range(2):
                    split(M_MQ + 2 * i + s + 1, 1 - s)
            dve.wait_ge(bank_read[1], KT + MB + FREE)
            dve.wait_ge(bank_read[0], KT + MB + FREE)
            dve.tensor_copy(mx[:, 0:1], nsp[:, 0:1]).then_inc(kv_made, MB + MEM_W // WIDE + MB)

            with link.loop(MEM_HEADS, 1) as h:
                for k in range(4):
                    m = M_MA + 8 * h + 2 * k
                    split(m + 1, 1)
                    if k == 0:
                        dve.wait_ge(mscore, h + 1)
                        for t in range(NT):
                            last = dve.tensor_reduce(mx[:, t:t + 1], psS[t][:, 0:MEM], AX.X, ALU.max)
                        link(last)
                        dve.tensor_scalar(nmx[:, 0:2], mx[:, 0:2], -MSCALE, None, ALU.mult).then_inc(mmax, 1)
                    split(m + 2, 0)
                    if k == 1:
                        dve.wait_ge(mexp, h + 1)
                        dve.reciprocal(rz[:, 0:2], zs[:, 0:2]).then_inc(mprob, 1)
                        dve.wait_ge(mprob, 2 * h + 1)
                        for t in range(NT):
                            last = dve.tensor_scalar(pm[:, t, :], pm[:, t, :], rz[:, t:t + 1], None, ALU.mult)
                        last.then_inc(mprob, 1)
                    dve.wait_ge(units_done, 2 * m + 4)
                    dve.wait_ge(bank_read[0], KT + MB + 4 * h + k + 1 + FREE)
                    dve.tensor_tensor(merged[:, ds(4 * h + k, 1), :].rearrange("p a t -> p (a t)"), psU[1][:, 0:TOK],
                                      gt[:, :], ALU.mult).then_inc(merge_made, 1)
                    if k == 3:
                        for c in range(MC):
                            dve.wait_ge(mhi, MC * h + c + 1)
                            w = (slice(None), ds(h * MC + c, 1), slice(None))
                            dve.tensor_tensor(brml[w].rearrange("p a t -> p (a t)"), psT[(0, 1, 3)[c]][:, 0:TOK],
                                              brmh[w].rearrange("p a t -> p (a t)").bitcast(f32), ALU.subtract).then_inc(mlo, 1)

            with link.loop(HEADS // 2, 14) as p:
                m = M_D + 12 * p
                for j in range(8):
                    split(m + j + 1, (j + 1) % 2)
                    if j in (4, 7):
                        b = 0 if j == 4 else 4
                        dve.wait_ge(bank_read[1], KT + MB + 4 * p + (2 if j == 4 else 4) + FREE)
                        dve.wait_ge(bank_read[0], KT + MB + KT + 4 * p + (2 if j == 4 else 4) + FREE)
                        q4 = qk[0:ROT, b:b + 4, :]
                        cos4 = cosT[:, :].unsqueeze(1).broadcast_to([ROT, 4, TOK])
                        sin4 = sinT[:, :].unsqueeze(1).broadcast_to([ROT, 4, TOK])
                        swap = [(k + HALF_ROT) % ROT for k in range(ROT)]
                        settle(dve)
                        link(dve.stream_shuffle(rsh[:, :, :], q4, swap))
                        link(dve.tensor_tensor(rsh[:, :, :], rsh[:, :, :], sin4, ALU.mult))
                        link(dve.tensor_tensor(q4, q4, cos4, ALU.mult))
                        dve.tensor_tensor(q4, q4, rsh[:, :, :], ALU.add).then_inc(rotated, 1)
                split(m + 9, 1)
                split(m + 10, 0)
                for hh in range(2):
                    dve.wait_ge(score, 2 * p + hh + 1 + FREE)
                    for t in range(NT):
                        c = 4 * hh + 2 * t
                        last = dve.tensor_reduce(mx[:, c:c + 2], (psS, psT[2:4])[hh][t][:, :].rearrange("p (j k) -> p j k", j=2), AX.X, ALU.max)
                    link(last)
                    dve.tensor_scalar(nmx[:, 4 * hh:4 * hh + 4], mx[:, 4 * hh:4 * hh + 4], -QSCALE, None, ALU.mult).then_inc(smax, 1)
                split(m + 11, 1)
                split(m + 12, 0)
                for hh in range(2):
                    dve.wait_ge(sexp, 2 * p + hh + 1)
                    z = slice(4 * hh, 4 * hh + 4)
                    zo = slice(4 * hh + 1, 4 * hh + 4, 2)
                    link(dve.reciprocal(rz[:, z], zs[:, z]))
                    link(dve.tensor_scalar(rz[:, zo], rz[:, zo], nlam[:, 0:1], None, ALU.mult))
                    for t in range(NT):
                        c = 4 * hh + 2 * t
                        last = dve.tensor_scalar(ex[:, hh, t, 1, :], ex[:, hh, t, 1, :], rz[:, c + 1:c + 2], None, ALU.mult)
                    link(last)
                    for t in range(NT):
                        c = 4 * hh + 2 * t
                        last = dve.scalar_tensor_tensor(ex[:, hh, t, 0, :], ex[:, hh, t, 0, :], rz[:, c:c + 1],
                                                        ex[:, hh, t, 1, :], ALU.mult, ALU.add)
                    last.then_inc(attn, 1)
                dve.wait_ge(units_done, 2 * m + 24)
                for t in range(2):
                    last = dve.tensor_copy(vv[:, t, :], psT[t][:, :])
                last.then_inc(tok_read, 1)
                dve.wait_ge(sqsum, 2 * p + 1)
                dve.tensor_scalar(ssq[:, :], ssq[:, :], 1.0 / VD, EPS, ALU.mult, ALU.add).then_inc(srt, 1)
                dve.wait_ge(sqsum, 2 * p + 2)
                dve.reciprocal(rstd[:, :], rstd[:, :]).then_inc(srt, 1)
                dve.wait_ge(srt, 2 * p + 2)
                for hh in range(2):
                    for t in range(NT):
                        last = dve.tensor_scalar(ex[:, hh, t, 0, :], psT[2 + hh][:, t * VD:(t + 1) * VD],
                                                 rstd[:, 2 * hh + t:2 * hh + t + 1], None, ALU.mult)
                    last.then_inc(onorm, 1)
                for hh in range(2):
                    dve.wait_ge(ohi, 4 * p + 2 * hh + 2)
                    for c in range(2):
                        w = (slice(None), ds(4 * p + 2 * hh + c, 1), slice(None))
                        dve.scalar_tensor_tensor(brl[w].rearrange("p a t -> p (a t)"), psS[hh][:, c * TOK:(c + 1) * TOK],
                                                 vec[:, 1, 98 + c:99 + c], brh[w].rearrange("p a t -> p (a t)").bitcast(f32),
                                                 ALU.mult, ALU.subtract).then_inc(olo, 1)

            for base_m, n0, reads in ((M_MM, 1, KT + MB + KT + 4 * 4), (M_MD, 2, KT + MB + 2 * KT + 4 * 4)):
                with link.loop(KT, 1) as i:
                    m = base_m + 2 * i
                    split(m + 1, 1)
                    split(m + 2, 0)
                    dve.wait_ge(units_done, 2 * m + 4)
                    dve.wait_ge(bank_read[0], reads + i + 1 + FREE)
                    link(dve.tensor_tensor(pt[:, :], psU[1][:, 0:TOK], gt[:, :], ALU.mult))
                    mg = merged[:, ds(i, 1), :].rearrange("p a t -> p (a t)")
                    dve.tensor_tensor(mg, mg, pt[:, :], ALU.add).then_inc(merge_made, 1)
                    if n0 == 2:
                        dve.wait_ge(mg_hi, i + 1)
                        w = (slice(None), ds(i, 1), slice(None))
                        dve.tensor_tensor(ml[w].rearrange("p a t -> p (a t)"), mg,
                                          mh[w].rearrange("p a t -> p (a t)").bitcast(f32), ALU.subtract).then_inc(mg_lo, 1)

            dve.wait_ge(res_in, 16 * NT)
            with dve.Fori(0, D // WIDE) as g:
                def take():
                    for t in range(2):
                        r = res[:, t, ds(g * WIDE, WIDE)]
                        last = dve.scalar_tensor_tensor(r, r, ALPHA, psT[t][:, :], ALU.mult, ALU.add)
                    last.then_inc(tok_read, 1)
                wide(M_OUT + 4 * g, split, g, take)

            def norm(k, gain, bias):
                dve.wait_ge((ln1_in, ln2_in)[k], 32)
                for t in range(NT):
                    link(dve.tensor_reduce(mom[:, 0, t:t + 1], res[:, t, :], AX.X, ALU.add))
                    dve.tensor_scalar(nmom[:, t:t + 1], mom[:, 0, t:t + 1], -1.0 / D, None, ALU.mult).then_inc(ln_dve, 1)
                    dve.wait_ge(ln_act, (k * NT + t) * 2 + 1)
                    dve.tensor_scalar(mom[:, 1, t:t + 1], mom[:, 1, t:t + 1], 1.0 / D, EPS, ALU.mult, ALU.add).then_inc(ln_dve, 1)
                    dve.wait_ge(ln_act, (k * NT + t) * 2 + 2)
                    link(dve.reciprocal(mom[:, 2, t:t + 1], mom[:, 2, t:t + 1]))
                    link(dve.tensor_scalar(res[:, t, :], res[:, t, :], nmom[:, t:t + 1], mom[:, 2, t:t + 1], ALU.add, ALU.mult))
                    link(dve.tensor_tensor(res[:, t, :], res[:, t, :], gain, ALU.mult))
                    dve.tensor_tensor(res[:, t, :], res[:, t, :], bias, ALU.add).then_inc(ln_done, 1)

            dve.wait_ge(tok_read, MEM_W // WIDE + HEADS // 2 + D // WIDE + FREE)
            norm(0, hbuf[:, 0:8, :].rearrange("p a b -> p (a b)"), hbuf[:, 8:16, :].rearrange("p a b -> p (a b)"))
            for t in range(NT):
                for b in range(4):
                    dve.wait_ge(x1_hi, 4 * t + b + 1)
                    w = (slice(None), slice(4 * b, 4 * b + 4), slice(t * P, (t + 1) * P))
                    dve.tensor_tensor(x1l[w], psT[b][:, :].rearrange("p (k c) -> p k c", c=P), x1h[w].bitcast(f32),
                                      ALU.subtract).then_inc(x1_lo, 1)

            def top16(src, v, i, rest):
                settle(dve)
                link(dve.max(v[:, 0:8], src))
                settle(dve)
                link(dve.match_replace(rest, v[:, 0:8], src, LOWEST))
                settle(dve)
                link(dve.max(v[:, 8:16], rest))
                settle(dve)
                dve.max_index(i[:, 0:8], v[:, 0:8], src)
                link(dve.max_index(i[:, 8:16], v[:, 8:16], rest))

            def keys(h, m, after):
                split(m + 1, 1)
                after()
                for j in range(2):
                    dve.wait_ge(key_score, 2 * h + j + 1 + FREE)
                    for t in range(NT):
                        top16(psS[j][:, t * NK:(t + 1) * NK], stv[:, j, t, :], sti[:, j, t, :], left[:, j, t, :])
                dve.tensor_copy(top_v[:, ds(h, 1), :, :, :].rearrange("p a j t r -> p (a j t r)"),
                                stv[:, :, :, :].rearrange("p j t r -> p (j t r)"))
                dve.tensor_copy(top_i[:, ds(h, 1), :, :, :].rearrange("p a j t r -> p (a j t r)"),
                                sti[:, :, :, :].rearrange("p j t r -> p (j t r)")).then_inc(top_done, 1)
                dve.wait_ge(top_done, h + 1 + FREE)

            with link.loop(PH - 1, 16) as h:
                keys(h, M_WQ + 2 * h, lambda: split(M_WQ + 2 * h + 2, 0))
            keys(PH - 1, M_WQ + 2 * PH - 2, lambda: split_turned(M_EXP, 0))
            dve.wait_ge(consts, 4 + HALF_ROT + 4)

            def choose(h, t, n):
                a_ = top_v[:, ds(h, 1), 0, t, :].rearrange("p a r -> p (a r)")
                b_ = top_v[:, ds(h, 1), 1, t, :].rearrange("p a r -> p (a r)")
                link(dve.tensor_tensor(cand[:, :, :], a_.unsqueeze(2).broadcast_to([P, TOPK, TOPK]),
                                       b_.unsqueeze(1).broadcast_to([P, TOPK, TOPK]), ALU.add))
                flat = cand[:, :, :].rearrange("p a b -> p (a b)")
                dve.wait_ge(best_exp, n + FREE)
                top16(flat, best[:, :], ci[:, :], cand2[:, :])
                dve.tensor_scalar(nbest[:, :], best[:, 0:1], -1.0, None, ALU.mult).then_inc(best_made, 1)
                dve.tensor_single_scalar(ca[:, :], ci[:, :], 4, ALU.logical_shift_right)
                link(dve.tensor_single_scalar(cb[:, :], ci[:, :], TOPK - 1, ALU.bitwise_and))
                dve.tensor_copy(caf[:, 0, :], ca[:, :])
                link(dve.tensor_copy(caf[:, 1, :], cb[:, :]))
                for j in range(2):
                    src = top_i[:, ds(h, 1), j, t, :].rearrange("p a r -> p (a r)")
                    link(dve.tensor_tensor(hit[:, :, :], caf[:, j, :].unsqueeze(2).broadcast_to([P, TOPK, TOPK]),
                                           iota16[:, :].unsqueeze(1).broadcast_to([P, TOPK, TOPK]), ALU.is_equal))
                    link(dve.tensor_tensor(hit[:, :, :], hit[:, :, :], src.unsqueeze(1).broadcast_to([P, TOPK, TOPK]), ALU.mult))
                    link(dve.tensor_reduce(pick[:, j, t, ds(h * TOPK, TOPK)], hit[:, :, :], AX.X, ALU.add))
                dve.wait_ge(best_exp, n + 1 + FREE)
                link(dve.reciprocal(rzb[:, :], zb[:, :]))
                link(dve.tensor_scalar(pick[:, 2, t, ds(h * TOPK, TOPK)], eb[:, :], rzb[:, 0:1], None, ALU.mult))

            def one_hots(step, b, k, own=False):
                tok = ds(k * GT, GT)
                dve.wait_ge(gate_mm, step - 1 + FREE2)
                if own:
                    link(dve.tensor_copy(i2s[b][:, :], pickT[:, 1, tok]))
                else:
                    dve.tensor_copy(i2s[b][:, :], pickT[:, 1, tok]).then_inc(i2_staged, 1)
                link(dve.tensor_tensor(mask[:, :, :], pickT[:, 0, tok].unsqueeze(2).broadcast_to([P, GT, GC]),
                                       iota[:, 0:GC].unsqueeze(1).broadcast_to([P, GT, GC]), ALU.is_equal))
                if own:
                    for q in range(GT):
                        dve.tensor_scalar(one2[b][:, q, :], iota[:, :], i2s[b][:, q:q + 1], None, ALU.is_equal)
                dve.tensor_tensor(one1[b][:, :, :, :], mask[:, :, :].unsqueeze(2).broadcast_to([P, GT, 2, GC]),
                                  gate2[:, :, tok].bitcast(f32).rearrange("p h t -> p t h").unsqueeze(3).broadcast_to([P, GT, 2, GC]),
                                  ALU.mult).then_inc(one1_made, 1)
                dve.wait_ge(one1_made, step + 1)

            def take_gates(step, b, k):
                dve.wait_ge(gate_mm, step + 1 + FREE2)
                dve.tensor_reduce(gbuf[:, :, ds(k * GT, GT)],
                                  psS[b][:, 0:GT * 2 * GC].rearrange("p (k h c) -> p c k h", h=2, c=GC),
                                  AX.X, ALU.add).then_inc(gate_read, 1)

            def weigh(m, s, c, n):
                dve.wait_ge(w_lo, n + FREE)
                cc = (slice(None), ds(c, 1), slice(None))
                dve.tensor_tensor(wt[:, :], hbuf[cc].rearrange("p a t -> p (a t)"), gbuf[cc].rearrange("p a t -> p (a t)"),
                                  ALU.mult).then_inc(w_ready, 1)

            def split_w(s, n):
                dve.wait_ge(w_hi, n + 1)
                dve.tensor_tensor(wl[s][:, :], wt[:, :], wh[s][:, :].bitcast(f32), ALU.subtract).then_inc(w_lo, 1)

            for g in range(GROUPS):
                mu, mv_ = M_EXP + 2 * g * GC, M_EXP + (2 * g + 1) * GC
                if g == 0:
                    with link.loop(PH, 30) as h:
                        for t in range(NT):
                            if t == 0:
                                split_turned(mu + 2 * h + 1, 1)
                            else:
                                split_turned(mu + 2 * h + 2, 0)
                            choose(h, t, 2 * h + t)
                    dve.tensor_copy(best[:, 0:1], zb[:, 0:1]).then_inc(pick_made, 1)
                    dve.wait_ge(split_gate, 1)
                    dve.tensor_tensor(gate2[:, 1, :], pickT[:, 2, :], gate2[:, 0, :].bitcast(f32), ALU.subtract).then_inc(split_gate, 1)
                    dve.wait_ge(split_gate, 2)

                    def round0(i, last=False):
                        for s in range(2):
                            for half in range(2):
                                k0 = (i - HALF0) * 8 + 4 * s + 2 * half
                                for b in range(2):
                                    one_hots(k0 + b, b, k0 + b, own=b == 1)
                                if half == 0:
                                    if last and s == 1:
                                        split(mv_, 0)
                                    else:
                                        split_turned(mu + 2 * i + 1 + s, 1 - s)
                                for b in range(2):
                                    take_gates(k0 + b, b, k0 + b)

                    with link.loop(GC // 2 - 1 - HALF0, 12, first=HALF0) as i:
                        round0(i)
                    round0(GC // 2 - 1, last=True)
                else:
                    link(dve.tensor_scalar(pickT[:, 0, :], pickT[:, 0, :], float(-GC), None, ALU.add))

                    def round_(i, last=False):
                        for s in range(2):
                            k0 = 4 * i + 2 * s
                            for b in range(2):
                                one_hots(g * STEPS + k0 + b, b, k0 + b)
                            if last and s == 1:
                                split(mv_, 0)
                            else:
                                split_turned(mu + 2 * i + 1 + s, 1 - s)
                            for b in range(2):
                                take_gates(g * STEPS + k0 + b, b, k0 + b)

                    with link.loop(GC // 2 - 1, 4) as i:
                        round_(i)
                    round_(GC // 2 - 1, last=True)
                dve.wait_ge(bank_read[1], PAIRS + (g + 1) * (GC // 2) + FREE)
                dve.wait_ge(gate_read, (g + 1) * STEPS + FREE2)
                weigh(mv_, 0, 0, g * GC)
                split_w(0, g * GC)

                def vpair(i, last=False):
                    m, n = mv_ + 2 * i, g * GC + 2 * i
                    weigh(m + 1, 1, 2 * i + 1, n + 1)
                    split(m + 1, 1)
                    split_w(1, n + 1)
                    if not last:
                        weigh(m + 2, 0, 2 * i + 2, n + 2)
                        split(m + 2, 0)
                        split_w(0, n + 2)

                with dve.Fori(0, GC // 2 - 1) as i:
                    vpair(i)
                vpair(GC // 2 - 1, last=True)
                dve.wait_ge(units_done, 2 * (mv_ + GC))
                for t in range(NT):
                    for n in range(4):
                        w = acc[:, t, n * 512:(n + 1) * 512]
                        if g == 0:
                            dve.tensor_copy(w, ps[4 * t + n][:, :]).then_inc(acc_read, 1)
                        else:
                            dve.tensor_tensor(w, w, ps[4 * t + n][:, :], ALU.add).then_inc(acc_read, 1)
                dve.wait_ge(acc_read, 8 * (g + 1))
                if g + 1 < GROUPS:
                    split_turned(mv_ + GC, 0)
            for t in range(NT):
                last = dve.scalar_tensor_tensor(res[:, t, :], res[:, t, :], ALPHA, acc[:, t, :], ALU.mult, ALU.add)
            link(last)
            norm(1, gbuf[:, 0:8, :].rearrange("p a b -> p (a b)"), gbuf[:, 8:16, :].rearrange("p a b -> p (a b)"))

        @block.tensor
        def _(pe):
            def turn(src, bank, q, identity=ident):
                return pe.transpose(psT[bank][:, q * P:(q + 1) * P], src, identity[:, :])

            def unit(m, s, b, ah, al, kt, reads, taken=None, mid=lambda: None):
                pe.wait_ge(lo_made, (m + PRE) * 4 + 2)
                pe.wait_ge(taken or bank_read[b], reads + FREE)
                w_h, w_l = k3(hi[s]), k3(lo[s])
                for k in range(kt):
                    if k == KT // 2:
                        mid()
                        pe.wait_ge(lo_made, (m + PRE) * 4 + 4)
                    o = psU[b][:, 0:TOK]
                    pe.matmul(o, w_h[:, k, :], ah[:, k, :], start=k == 0, stop=False)
                    pe.matmul(o, w_h[:, k, :], al[:, k, :], start=False, stop=False)
                    last = pe.matmul(o, w_l[:, k, :], ah[:, k, :], start=False, stop=k == kt - 1)
                    if k in (KT // 2 - 1, kt - 1):
                        last.then_inc(units_done, 1)

            def wide(m, ah, al, reads):
                for j in range(4):
                    s = j % 2
                    w_h, w_l = w3(hi[s]), w3(lo[s])
                    for half in range(2):
                        pe.wait_ge(lo_made, (m + j + PRE) * 4 + 2 * (half + 1))
                        if j == 0 and half == 0:
                            pe.wait_ge(tok_read, reads + FREE)
                        for t in range(2):
                            for k in (2 * half, 2 * half + 1):
                                a_h = ah[:, KQ * j + k, t * P:(t + 1) * P]
                                a_l = al[:, KQ * j + k, t * P:(t + 1) * P]
                                o = psT[t][:, :]
                                pe.matmul(o, a_h, w_h[:, k, :], start=j == 0 and k == 0, stop=False)
                                pe.matmul(o, a_h, w_l[:, k, :], start=False, stop=False)
                                last = pe.matmul(o, a_l, w_h[:, k, :], start=False, stop=j == 3 and k == KQ - 1)
                        last.then_inc(units_done, 1)

            pe.wait_ge(consts, 6 + HALF_ROT)
            pe.wait_ge(small_in, 9 * 16)
            pe.transpose(psS[0][:, 0:P], vrow[:, 0, :], ident[:, :])
            pe.transpose(psS[0][:, P:P + 98], vrow[0:98, 1, :], ident[0:98, 0:98])
            pe.matmul(psS[1][0:ROT, 0:1], ifr[0:1, :], ones1[0:1, 0:1], start=True, stop=True).then_inc(vec_turned, 1)
            for r in range(PRE):
                pe.wait_ge(raw_in[r % 2], 16 * (r // 2 + 1))
                for b in range(4):
                    if r:
                        pe.wait_ge(lo_made, 4 * (r - 1) + b + 1)
                    for q in range(4):
                        last = turn(raw[r % 2][:, (4 * b + q) * P:(4 * b + q + 1) * P], b, q)
                    last.then_inc(turned, 1)

            with pe.Fori(0, KT) as i:
                m = M_LRU + 2 * i
                unit(m, 0, 0, xh, xl, KT, i)
                unit(m + 1, 1, 1, xh, xl, KT, i)
                pe.wait_ge(xc_made, i + 1)
                pe.wait_ge(lru_in, (i + 1) * 32)
                pe.wait_ge(gates_read, i + FREE)
                for d in range(2):
                    for k in range(2):
                        last = pe.matmul(psT[d][:, k * TOK:(k + 1) * TOK], lru_w[:, k, d, :], xc[:, :], start=True, stop=True)
                last.then_inc(lru_mm, 1)
            with pe.Fori(0, MB // 2) as i:
                for s in range(2):
                    unit(M_MK + 2 * i + s, s, s, memh, meml, KT, KT + i)
            pe.wait_ge(gates_read, KT + FREE)
            with pe.Fori(0, MEM_W // WIDE) as g:
                wide(M_MV + 4 * g, memh, meml, g)
            with pe.Fori(0, MB // 2) as i:
                for s in range(2):
                    unit(M_MQ + 2 * i + s, s, s, xh, xl, KT, KT + MB // 2 + i)
            rd = KT + MB
            pe.wait_ge(kv_made, 1)
            pe.wait_ge(bank_read[1], rd + FREE)
            with pe.Fori(0, MEM_HEADS) as h:
                for k in range(4):
                    m = M_MA + 8 * h + 2 * k
                    unit(m, 0, 0, xh, xl, KT, rd + 4 * h + k)
                    if k == 0:
                        pe.wait_ge(staged, 2 * h + 2)
                        for t in range(NT):
                            for c in range(MC):
                                last = pe.matmul(psS[t][:, 0:MEM], mqs[:, c, t * P:(t + 1) * P],
                                                 mk[:, ds(h * MC + c, 1), :].rearrange("p a m -> p (a m)"),
                                                 start=c == 0, stop=c == MC - 1)
                        last.then_inc(mscore, 1)
                    if k == 2:
                        pe.wait_ge(mprob, 2 * h + 2)
                        for b in range(2):
                            for t in range(NT):
                                last = pe.transpose(psT[2][:, (2 * b + t) * P:(2 * b + t + 1) * P], pm[:, t, b * P:(b + 1) * P], ident[:, :])
                        last.then_inc(mturned, 1)
                    if k == 3:
                        pe.wait_ge(mpT, h + 1)
                        pe.wait_ge(mlo, MC * h + FREE)
                        for c in range(MC):
                            for b in range(2):
                                last = pe.matmul(psT[(0, 1, 3)[c]][:, 0:TOK], mvs[:, b, c * P:(c + 1) * P], pmT[:, b, :],
                                                 start=b == 0, stop=b == 1)
                        last.then_inc(mpv, 1)
                    unit(m + 1, 1, 1, brh, brl, KT, 4 * h + k, merge_made)
            merges = KT
            rd += KT
            pe.wait_ge(merge_made, KT + FREE)
            pe.wait_ge(mlo, MC * MEM_HEADS + FREE)
            with pe.Fori(0, HEADS // 2) as p:
                m = M_D + 12 * p
                for j in range(8):
                    unit(m + j, j % 2, j % 2, xh, xl, KT, rd - merges * (j % 2) + 4 * p + j // 2)
                pe.wait_ge(olo, 4 * p + FREE)
                for hh in range(2):
                    if hh == 0:
                        pe.wait_ge(rotated, 2 * p + 2)
                    for t in range(NT):
                        for j in range(2):
                            last = pe.matmul((psS, psT[2:4])[hh][t][:, j * TOK:(j + 1) * TOK], qk[:, 2 * hh + j, t * P:(t + 1) * P],
                                             qk[:, 4 + 2 * hh + j, :], start=True, stop=True)
                    last.then_inc(score, 1)
                wide(m + 8, xh, xl, MEM_W // WIDE + p)
                for hh in range(2):
                    pe.wait_ge(attn, 2 * p + hh + 1)
                    for b in range(2):
                        for t in range(NT):
                            last = pe.transpose(psS[hh][:, (2 * b + t) * P:(2 * b + t + 1) * P], ex[:, hh, t, 0, b * P:(b + 1) * P], ident[:, :])
                    last.then_inc(aturned, 1)
                pe.wait_ge(tok_read, MEM_W // WIDE + p + 1 + FREE)
                for hh in range(2):
                    pe.wait_ge(atT, 2 * p + hh + 1)
                    for t in range(NT):
                        for b in range(2):
                            last = pe.matmul(psT[2 + hh][:, t * VD:(t + 1) * VD], at[:, hh, b, t * P:(t + 1) * P],
                                             vv[:, b, hh * VD:(hh + 1) * VD], start=b == 0, stop=b == 1)
                    last.then_inc(pv, 1)
                for hh in range(2):
                    pe.wait_ge(onorm, 2 * p + hh + 1)
                    for c in range(2):
                        for t in range(NT):
                            last = pe.transpose(psS[hh][:, (2 * c + t) * P:(2 * c + t + 1) * P], ex[:, hh, t, 0, c * P:(c + 1) * P], ident[:, :])
                    last.then_inc(oturned, 1)
            rd += 4 * (HEADS // 2)
            pe.wait_ge(bank_read[1], rd - merges + FREE)
            with pe.Fori(0, KT) as i:
                unit(M_MM + 2 * i, 0, 0, xh, xl, KT, rd + i)
                unit(M_MM + 2 * i + 1, 1, 1, brmh, brml, MB, KT + i, merge_made)
            rd += KT
            pe.wait_ge(olo, 2 * HEADS + FREE)
            with pe.Fori(0, KT) as i:
                unit(M_MD + 2 * i, 0, 0, xh, xl, KT, rd + i)
                unit(M_MD + 2 * i + 1, 1, 1, brh, brl, KT, 2 * KT + i, merge_made)
            rd += KT
            merges = 3 * KT
            pe.wait_ge(merge_made, merges + FREE)
            pe.wait_ge(mg_lo, KT)
            with pe.Fori(0, D // WIDE) as g:
                wide(M_OUT + 4 * g, mh, ml, MEM_W // WIDE + HEADS // 2 + g)
            pe.wait_ge(sub_in, 16)
            pe.wait_ge(tok_read, MEM_W // WIDE + HEADS // 2 + D // WIDE + FREE)
            keys_raw = gbuf[:, 0:8, :].rearrange("p a b -> p (a b)")
            for b in range(4):
                for q in range(4):
                    last = turn(keys_raw[:, (4 * b + q) * P:(4 * b + q + 1) * P], b, q)
                last.then_inc(sub_turned, 1)
            for t in range(NT):
                pe.wait_ge(ln_done, t + 1)
                for b in range(4):
                    if t == 0:
                        pe.wait_ge(sk_made, b + 1)
                    else:
                        pe.wait_ge(x1_lo, b + 1)
                    for q in range(4):
                        last = turn(res[:, t, (4 * b + q) * P:(4 * b + q + 1) * P], b, q)
                    last.then_inc(x1_turned, 1)
            pe.wait_ge(x1_lo, 4 * NT)

            def turn_unit(m, s, first=False):
                pe.wait_ge(raw_in[s], (m + PRE - s) * 8 + 16)
                for b in range(4):
                    if not first:
                        pe.wait_ge(lo_made, (m + PRE - 1) * 4 + (b + 1))
                    for q in range(4):
                        last = turn(raw[s][:, (4 * b + q) * P:(4 * b + q + 1) * P], b, q)
                    last.then_inc(turned, 1)

            def queries(h, m, after):
                unit(m, 0, 0, x1h, x1l, KT, rd + h)
                after()
                unit(m + 1, 1, 1, x1h, x1l, KT, rd - merges + h)
                pe.wait_ge(top_done, h + FREE)
                for j in range(2):
                    pe.wait_ge(bank_read[j], rd - merges * j + h + 1 + FREE)
                    for t in range(NT):
                        last = pe.matmul(psS[j][:, t * NK:(t + 1) * NK], qT[:, j, t * P:(t + 1) * P],
                                         skT[:, ds(2 * h + j, 1), :].rearrange("p a n -> p (a n)"), start=True, stop=True)
                    last.then_inc(key_score, 1)

            with pe.Fori(0, PH - 1) as h:
                queries(h, M_WQ + 2 * h, lambda: None)
            queries(PH - 1, M_WQ + 2 * PH - 2, lambda: turn_unit(M_EXP, 0, first=True))
            rd += PH

            for g in range(GROUPS):
                mu, mv_ = M_EXP + 2 * g * GC, M_EXP + (2 * g + 1) * GC
                r0 = rd + g * (GC // 2)

                def pair(i, last=False, mid=lambda i, s: None, extra=lambda i, s: None):
                    m = mu + 2 * i
                    turn_unit(m + 1, 1)
                    unit(m, 0, 0, x1h, x1l, KT, r0 + i, mid=lambda: mid(i, 0))
                    extra(i, 0)
                    if not last:
                        turn_unit(m + 2, 0)
                    unit(m + 1, 1, 1, x1h, x1l, KT, r0 - merges + i, mid=lambda: mid(i, 1))
                    extra(i, 1)

                def gate_step(step, b, made2):
                    if made2 is not None:
                        pe.wait_ge(one2_made, made2)
                    pe.wait_ge(one1_made, step + 1)
                    pe.wait_ge(gate_read, step - 1 + FREE2)
                    for k in range(GT):
                        last = pe.matmul(psS[b][:, k * 2 * GC:(k + 1) * 2 * GC], one2[b][:, k, :],
                                         one1[b][:, k, :, :].rearrange("p h c -> p (h c)"), start=True, stop=True)
                    last.then_inc(gate_mm, 1)

                def first_steps(qs):
                    def build(i, s):
                        for q in qs:
                            k = (i - HALF0) * 8 + 4 * s + q
                            gate_step(k, q % 2, (i - HALF0) * 4 + 2 * s + q // 2 + 1 if q % 2 == 0 else None)
                    return build

                def steps(q):
                    def build(i, s):
                        k = 4 * i + 2 * s + q
                        gate_step(g * STEPS + k, q, (g - 1) * STEPS + STEPS // 2 + k + 1)
                    return build

                if g == 0:
                    with pe.Fori(0, HALF0) as i:
                        pair(i)
                    pe.wait_ge(pick_made, 1)
                    for k in range(3):
                        dst = psS[1] if k < 2 else psS[0]
                        for t in range(NT):
                            c = ((k % 2) * NT + t) * P
                            last = pe.transpose(dst[:, c:c + P], pick[:, k, t, :], ident[:, :])
                    last.then_inc(pick_turned, 1)
                    pe.wait_ge(split_gate, 1)
                    with pe.Fori(HALF0, GC // 2 - 1) as i:
                        pair(i, mid=first_steps((0, 1)), extra=first_steps((2, 3)))
                    pair(GC // 2 - 1, last=True, mid=first_steps((0, 1)), extra=first_steps((2, 3)))
                else:
                    with pe.Fori(0, GC // 2 - 1) as i:
                        pair(i, mid=steps(0), extra=steps(1))
                    pair(GC // 2 - 1, last=True, mid=steps(0), extra=steps(1))

                def v_unit(m, s, n, first=False, final=False):
                    for half in range(2):
                        pe.wait_ge(lo_made, (m + PRE) * 4 + 2 * (half + 1))
                        if half == 0:
                            pe.wait_ge(w_lo, n + 1 + FREE)
                        for t in range(NT):
                            for part, (w, v) in enumerate(((wh[s], hi[s]), (wh[s], lo[s]), (wl[s], hi[s]))):
                                for c in (2 * half, 2 * half + 1):
                                    last = pe.matmul(ps[4 * t + c][:, :], w[:, t * P:(t + 1) * P], v[:, c * 512:(c + 1) * 512],
                                                     start=first and part == 0, stop=final and part == 2)
                        last.then_inc(units_done, 1)

                pe.wait_ge(gate_read, (g + 1) * STEPS + FREE2)
                pe.wait_ge(bank_read[0], r0 + GC // 2 + FREE)
                pe.wait_ge(bank_read[1], r0 - merges + GC // 2 + FREE)
                v_unit(mv_, 0, g * GC, first=True)
                v_unit(mv_ + 1, 1, g * GC + 1)
                with pe.Fori(1, GC // 2 - 1) as i:
                    for s in range(2):
                        v_unit(mv_ + 2 * i + s, s, g * GC + 2 * i + s)
                v_unit(mv_ + GC - 2, 0, g * GC + GC - 2)
                v_unit(mv_ + GC - 1, 1, g * GC + GC - 1, final=True)
                if g + 1 < GROUPS:
                    pe.wait_ge(acc_read, 8 * (g + 1))
                    turn_unit(mv_ + GC, 0, first=True)


_INS = ['x', 'mem', 'positions', 'w_in', 'b_gate', 'conv_w', 'conv_b', 'lru_w_a', 'lru_b_a', 'lru_w_i', 'lru_b_i',
        'lru_lambda', 'diff_lambda', 'diff_subln', 'w_mem_kv', 'w_branch_lru', 'w_branch_diff', 'w_branch_mem',
        'w_out', 'ln1_g', 'ln1_b', 'peer_w_q', 'peer_sub_keys', 'peer_u', 'peer_v', 'ln2_g', 'ln2_b']


def kernel(**inputs):
    import numpy as _np
    import concourse.bacc as _bacc
    from concourse import mybir as _mybir
    from concourse.bass_utils import run_bass_kernel_spmd as _run

    nc = _bacc.Bacc("TRN2", target_bir_lowering=False, num_devices=1)
    arrays, args = {}, []
    for name in _INS:
        a = _np.ascontiguousarray(inputs[name])
        arrays[f"in_{name}"] = a
        args.append(nc.dram_tensor(f"in_{name}", a.shape, _mybir.dt.from_np(a.dtype), kind="ExternalInput").ap())
    o = nc.dram_tensor("out_x", (1, TOK, D), _mybir.dt.float32, kind="ExternalOutput").ap()
    layer(nc, *args, o)
    r = _run(nc, [arrays], core_ids=[0])
    return r.results[0]["out_x"]
```

```python
import math
from contextlib import ExitStack

import concourse.bass as bass
from concourse import mybir

f32, f32r, bf16 = mybir.dt.float32, mybir.dt.float32r, mybir.dt.bfloat16
i32, u32 = mybir.dt.int32, mybir.dt.uint32
ALU = mybir.AluOpType
ACT = mybir.ActivationFunctionType
AX = mybir.AxisListType
ds = bass.ds

P = 128
D = 2048
TOK = 256
NT = TOK // P
KT = D // P
BLK = 128
WIDE = 512
KQ = 4
UNIT = KT * BLK
HALF = UNIT // 2
MEM = 256
MEM_HEADS, MEM_DIM = 4, 384
MEM_W = MEM_HEADS * MEM_DIM
MB = MEM_W // P
MC = MEM_DIM // P
HEADS, HD = 8, 128
VD = 2 * HD
ROT, HALF_ROT, THETA = 32, 16, 500000.0
QSCALE, MSCALE = HD ** -0.5, MEM_DIM ** -0.5
LAM_INIT = 0.8 - 0.6 * math.exp(0.0)
ALPHA = 2.0 ** 0.25
EPS = 1e-5
PH, NK, TOPK = 8, 128, 16
GROUPS, GC = 4, 32
GT = 8
GH = GT // 2
STEPS = TOK // GT
HALF0 = GC // 4
LOWEST = -3.0e38
FREE, FREE2 = 1, 2

COL_GATE, COL_AX, COL_Q, COL_K, COL_V = 0, 2048, 4096, 6144, 8192
COL_MQ, COL_G = 10240, 11776
PRE = 2
TURNS = 4
M_LRU = 0
M_MQ = M_LRU + 2 * KT
M_MEM = M_MQ + MB - 2
M_MK = M_MQ + MB + 2
M_MV = M_MK + MB
M_MA = M_MV + MEM_W // WIDE * 4
M_D = M_MA + 2 * KT
M_MM = M_D + HEADS // 2 * 12
M_MD = M_MM + 2 * KT
M_OUT = M_MD + 2 * KT
M_WQ = M_OUT + D // WIDE * 4
M_EXP = M_WQ + 2 * PH
PAIRS = KT + MB + 2 * HEADS + PH


def layer(nc, x, mem, pos, w_in, b_gate, conv_w, conv_b, lru_w_a, lru_b_a, lru_w_i, lru_b_i, lru_lambda,
          diff_lambda, diff_subln, w_mem_kv, w_lru, w_diff, w_mem, w_out, ln1_g, ln1_b, w_q, sub_keys,
          u_tab, v_tab, ln2_g, ln2_b, out):
    ctx = ExitStack()
    with ctx:
        def sb(name, shape, dt=f32, stack=ctx):
            return stack.enter_context(nc.sbuf_tensor(name, shape, dt))

        def sem(name):
            return ctx.enter_context(nc.semaphore(name))

        raw = [sb(f"raw{s}", [P, UNIT]) for s in range(2)]
        hi = [sb(f"hi{s}", [P, UNIT], f32r) for s in range(2)]
        lo = [sb(f"lo{s}", [P, UNIT], f32r) for s in range(2)]
        ident = sb("ident", [P, P])
        ones1 = sb("ones1", [1, 1])
        vrow = sb("vrow", [P, 2, P])
        vec = sb("vec", [P, 2, P])
        mom = sb("mom", [P, 4, 2])
        nmom = sb("nmom", [P, 2])
        rowsum = sb("rowsum", [P, NT, 4])
        base = ExitStack()

        A = ExitStack()
        S0 = ExitStack()
        rtmp = sb("rtmp", [ROT, 4, TOK], f32, S0)
        posi = sb("posi", [ROT, TOK], i32, S0)
        lp = sb("lp", [P, 4, P], f32, S0)
        S0.close()
        brh = sb("brh", [P, KT, TOK], f32r, A)
        brl = sb("brl", [P, KT, TOK], f32r, A)
        L = ExitStack()
        axp = sb("axp", [P, 2, TOK + 4], f32, L)
        xc = sb("xc", [P, 2, TOK], f32, L)
        xkept = sb("xkept", [P, 2, TOK], f32, L)
        gelu_gate = sb("gelu_gate", [P, 2, TOK], f32, L)
        gkept = sb("gkept", [P, 2, TOK], f32, L)
        lru_w = sb("lru_w", [P, 2, 2, P], f32, L)
        t_r = sb("t_r", [P, 2, 2, TOK], f32, L)
        t_i = sb("t_i", [P, 2, 2, TOK], f32, L)
        dec = sb("dec", [P, 2, 2, TOK], f32, L)
        wsq = sb("wsq", [P, 2, 2, TOK], f32, L)
        uin = sb("uin", [P, 2, 2, TOK], f32, L)
        hst = sb("hst", [P, 2, 2, TOK], f32, L)
        L.close()
        merged = sb("merged", [P, KT, TOK], f32, A)
        M = ExitStack()
        mv = sb("mv", [P, 2, MEM_W], f32, M)
        mk = sb("mk", [P, MB, MEM], f32, M)
        M.close()
        S = ExitStack()
        qk = sb("qk", [P, 8, TOK], f32, S)
        vv = sb("vv", [P, 2, WIDE], f32, S)
        ex = sb("ex", [P, 2, 2, 2, TOK], f32, S)
        at = sb("at", [P, 2, 2, TOK], f32, S)
        S.close()
        sb("held_a", [P, 24, TOK], f32, A)
        mq = sb("mq", [P, MB, TOK], f32, A)
        xh = sb("xh", [P, KT, TOK], f32r, A)
        xl = sb("xl", [P, KT, TOK], f32r, A)
        Z1 = ExitStack()
        memh = sb("memh", [P, KT, MEM], f32r, Z1)
        meml = sb("meml", [P, KT, MEM], f32r, Z1)
        Z1.close()
        Z2 = ExitStack()
        brmh = sb("brmh", [P, MB, TOK], f32r, Z2)
        brml = sb("brml", [P, MB, TOK], f32r, Z2)
        Z4 = ExitStack()
        mqs = sb("mqs", [P, MC, TOK], f32, Z4)
        mvs = sb("mvs", [P, 2, MEM_DIM], f32, Z4)
        pm = sb("pm", [P, 2, MEM], f32, Z4)
        Z4.close()
        rsh = sb("rsh", [ROT, 4, TOK], f32, Z2)
        Z2.close()
        Z3 = ExitStack()
        mh = sb("mh", [P, KT, TOK], f32r, Z3)
        ml = sb("ml", [P, KT, TOK], f32r, Z3)
        Z3.close()
        sb("held_b", [P, 32, TOK], f32, A)
        gt = sb("gt", [P, TOK], f32, A)
        pt = sb("pt", [P, TOK], f32, A)
        pmT = sb("pmT", [P, 2, TOK], f32, A)
        cosT = sb("cosT", [ROT, TOK], f32, A)
        sinT = sb("sinT", [ROT, TOK], f32, A)
        ifr = sb("ifr", [1, ROT], f32, A)
        ifc = sb("ifc", [ROT, 1], f32, A)
        sgn = sb("sgn", [ROT, 1], f32, A)
        lsum = sb("lsum", [P, 2], f32, A)
        lame = sb("lame", [P, 2], f32, A)
        nlam = sb("nlam", [P, 1], f32, A)
        hb = sb("hb", [P, 64], f32, A)
        sp = sb("sp", [P, 32], f32, A)
        nsp = sb("nsp", [P, 32], f32, A)
        spt = sb("spt", [P, 4, 32], f32, A)
        mx = sb("mx", [P, 8], f32, A)
        nmx = sb("nmx", [P, 8], f32, A)
        zs = sb("zs", [P, 8], f32, A)
        rz = sb("rz", [P, 8], f32, A)
        ssq = sb("ssq", [P, 4], f32, A)
        rstd = sb("rstd", [P, 4], f32, A)
        A.close()

        B = ExitStack()
        hbuf = sb("hbuf", [P, GC, TOK], f32, B)
        gbuf = sb("gbuf", [P, GC, TOK], f32, B)
        acc = sb("acc", [P, NT, D], f32, B)
        res = sb("res", [P, NT, D], f32, B)
        x1h = sb("x1h", [P, KT, TOK], f32r, B)
        x1l = sb("x1l", [P, KT, TOK], f32r, B)
        best = sb("best", [P, NT, TOPK], f32, B)
        nbest = sb("nbest", [P, NT], f32, B)
        zb = sb("zb", [P, NT], f32, B)
        rzb = sb("rzb", [P, NT], f32, B)
        eb = sb("eb", [P, NT, TOPK], f32, B)
        ci = sb("ci", [P, NT, TOPK], u32, B)
        ca = sb("ca", [P, NT, TOPK], u32, B)
        cb = sb("cb", [P, NT, TOPK], u32, B)
        caf = sb("caf", [P, 2, NT, TOPK], f32, B)
        iota16 = sb("iota16", [P, TOPK], f32, B)
        iota = sb("iota", [P, P], f32, B)
        keys = sb("keys", [P, P], bf16, B)
        i1 = sb("i1", [P, TOK], bf16, B)
        pickT = sb("pickT", [P, 3, TOK], f32, B)
        gate3 = sb("gate3", [P, 3, TOK], bf16, B)
        neg_i2 = sb("neg_i2", [P, GT], f32, B)
        i2s = [sb(f"i2s{b}", [P, GT], f32, B) for b in range(2)]
        cand, cand2, hit = gbuf[:, 0:2, :], gbuf[:, 2:4, :], gbuf[:, 4:8, :].rearrange("p n (a b) -> p n a b", b=TOPK)
        top_v, top_i = (gbuf[:, c:c + 2, :].rearrange("p n (a t r) -> p (n a) t r", t=NT, r=TOPK)
                        .rearrange("p (h j) t r -> p h j t r", j=2) for c in (8, 10))
        pick = gbuf[:, 12:15, :].rearrange("p k (t c) -> p k t c", t=NT)
        B1 = ExitStack()
        skT = sb("skT", [P, 2 * PH, NK], f32, B1)
        qT = sb("qT", [P, 2, TOK], f32, B1)
        stv = sb("stv", [P, 2, NT, TOPK], f32, B1)
        sti = sb("sti", [P, 2, NT, TOPK], u32, B1)
        left = sb("left", [P, 2, NT, NK], f32, B1)
        B1.close()
        B2 = ExitStack()
        one2 = [sb(f"one2{b}", [P, GT, P], bf16, B2) for b in range(2)]
        dist = sb("dist", [P, GT, P], f32, B2)
        mask = sb("mask", [P, GT, GC], bf16, B2)
        one1 = [sb(f"one1{b}", [P, GT, 3, GC], bf16, B2) for b in range(2)]
        wt = sb("wt", [P, TOK], f32, B2)
        wh = [sb(f"wh{s}", [P, TOK], f32r, B2) for s in range(2)]
        wl = [sb(f"wl{s}", [P, TOK], f32r, B2) for s in range(2)]
        B2.close()
        B.close()

        ps = [ctx.enter_context(nc.psum_tensor(f"ps{b}", [P, 512], f32)) for b in range(8)]
        psU, psT, psS = ps[0:2], ps[2:6], ps[6:8]

        raw_in = [sem("raw_in0"), sem("raw_in1")]
        hi_made = sem("hi_made")
        lo_made = sem("lo_made")
        units_done = sem("units_done")
        turned = sem("turned")
        bank_read = [sem("bank_read0"), sem("bank_read1")]
        tok_read = sem("tok_read")
        consts = sem("consts")
        small_in = sem("small_in")
        vec_turned, vec_ready, set_dve, set_act = sem("vec_turned"), sem("vec_ready"), sem("set_dve"), sem("set_act")
        lru_in, lru_mm, gates_read, xc_kept, in_made = (sem(n) for n in ("lru_in", "lru_mm", "gates_read", "xc_kept", "in_made"))
        exponents, gelu_kept = sem("exponents"), sem("gelu_kept")
        dec_squared, scanned, summed = sem("dec_squared"), sem("scanned"), sem("summed")
        xc_made, decays, w_made, root_made = sem("xc_made"), sem("decays"), sem("w_made"), sem("root_made")
        br_made, br_hi, br_lo = sem("br_made"), sem("br_hi"), sem("br_lo")
        kv_made = sem("kv_made")
        staged = sem("staged")
        mscore, mmax, mexp, mprob, mturned, mpT, mpv, mhi, mlo = (sem("mem_" + n) for n in (
            "score", "max", "exp", "prob", "turned", "probT", "pv", "hi", "lo"))
        gate_made, merge_made, mg_hi, mg_lo = sem("gate_made"), sem("merge_made"), sem("mg_hi"), sem("mg_lo")
        qk_made, rotated, score, smax, sexp, attn, aturned, atT, pv, sqsum, onorm, oturned, ohi, olo, srt = (
            sem("d_" + n) for n in ("qk", "rotated", "score", "max", "exp", "attn", "turned", "attnT", "pv",
                                    "sqsum", "onorm", "oturned", "hi", "lo", "root"))
        res_in, sub_in, ln1_in, ln2_in = sem("res_in"), sem("sub_in"), sem("ln1_in"), sem("ln2_in")
        ln_mean, ln_dve, ln_act, ln_done = sem("ln_mean"), sem("ln_dve"), sem("ln_act"), sem("ln_done")
        x1_hi, x1_lo, sub_turned, sk_made = sem("x1_hi"), sem("x1_lo"), sem("sub_turned"), sem("sk_made")
        x1_turned = sem("x1_turned")
        q_made, key_score, top_done = sem("q_made"), sem("key_score"), sem("top_done")
        best_made, best_exp, pick_made, pick_turned, pickT_made = (
            sem(n) for n in ("best_made", "best_exp", "pick_made", "pick_turned", "pickT_made"))
        hit_made, hit_keys = sem("hit_made"), sem("hit_keys")
        neg_staged, dist_made, act_one2 = sem("neg_staged"), sem("dist_made"), sem("act_one2")
        i2_staged, one2_made, one1_made, gate_mm, gate_read = (
            sem(n) for n in ("i2_staged", "one2_made", "one1_made", "gate_mm", "gate_read"))
        h_made, w_ready, w_hi, w_lo, acc_read = sem("h_made"), sem("w_ready"), sem("w_hi"), sem("w_lo"), sem("acc_read")
        sum_made, res_scaled, res_added = sem("sum_made"), sem("res_scaled"), sem("res_added")
        out_done = sem("out_done")
        passed = sem("passed")
        dve_link, act_link = sem("dve_link"), sem("act_link")

        def settle(eng):
            eng.sem_inc(passed, 1)

        class Link:

            def __init__(self, eng, s):
                self.eng, self.sem, self.n, self.off = eng, s, 0, 0

            def __call__(self, ins):
                ins.then_inc(self.sem, 1)
                self.n += 1
                self.eng.wait_ge(self.sem, self.off + self.n)

            def mark(self, ins):
                ins.then_inc(self.sem, 1)
                self.n += 1

            def wait(self, n):
                self.eng.wait_ge(self.sem, self.off + n)

            def loop(self, count, per, first=0):
                return _Loop(self, count, per, first)

        class _Loop:

            def __init__(self, link, count, per, first):
                self.link, self.count, self.per, self.first = link, count, per, first

            def __enter__(self):
                self.fori = self.link.eng.Fori(self.first, self.first + self.count)
                i = self.fori.__enter__()
                self.start = self.link.n
                self.link.off = (i - self.first) * self.per
                return i

            def __exit__(self, *e):
                got = self.link.n - self.start
                assert e[0] or got == self.per, f"{got} steps, not {self.per}"
                self.link.off = 0
                self.link.n = self.start + self.count * self.per
                return self.fori.__exit__(*e)

        def rows(w):
            return w.rearrange("(k p) c -> p k c", p=P)

        win_v, kv_v = rows(w_in[0]), rows(w_mem_kv[0])
        lru_v, diff_v, mem_v, out_v, wq_v = (rows(w[0]) for w in (w_lru, w_diff, w_mem, w_out, w_q))
        u_v = u_tab[0].rearrange("(c p) d -> p c d", p=P)
        v_v = v_tab[0].rearrange("(c p) d -> p c d", p=P)
        k3 = lambda t: t[:, :].rearrange("p (k c) -> p k c", c=BLK)
        w3 = lambda t: t[:, :].rearrange("p (k c) -> p k c", c=WIDE)

        start_free = ((FREE, (lru_mm, mpv, br_made, merge_made, score, best_exp, w_lo, gates_read, tok_read,
                              mlo, olo, gate_read, act_one2, bank_read[0], bank_read[1])), (FREE2, (gate_mm, key_score, top_done)))

        block = ctx.enter_context(nc.Block())

        @block.sync
        def _(sp_):
            def load(m, s, dst, src, first=False):
                if not first:
                    sp_.wait_ge(lo_made, (m + (PRE - 1)) * 4)
                    settle(sp_)
                sp_.dma_start(dst, src).then_inc(raw_in[s], 16)

            for t in range(NT):
                load(t - PRE, t, raw[t][:, :], x[0, t * P:(t + 1) * P, :], first=True)

            def col(m, s, view, c):
                load(m, s, k3(raw[s]), view[:, :, ds(c, BLK)])

            with sp_.Fori(0, KT) as i:
                col(M_LRU + 2 * i, 0, win_v, COL_AX + i * BLK)
                col(M_LRU + 2 * i + 1, 1, win_v, COL_GATE + i * BLK)
            def mq_col(n, m, s):
                col(m, s, win_v, COL_MQ + n * BLK)

            with sp_.Fori(0, MB // 2 - 1) as i:
                for s in range(2):
                    mq_col(2 * i + s, M_MQ + 2 * i + s, s)
            for t in range(NT):
                load(M_MEM + 2 * t, 0, raw[0][:, :], mem[0, t * P:(t + 1) * P, :])
                mq_col(MB - 2 + t, M_MEM + 2 * t + 1, 1)
            with sp_.Fori(0, MB // 2) as i:
                for s in range(2):
                    col(M_MK + 2 * i + s, s, kv_v, i * (2 * BLK) + s * BLK)
            with sp_.Fori(0, MEM_W // WIDE) as g:
                for j in range(4):
                    load(M_MV + 4 * g + j, j % 2, w3(raw[j % 2]), kv_v[:, j * KQ:(j + 1) * KQ, ds(MEM_W + g * WIDE, WIDE)])
            with sp_.Fori(0, KT) as i:
                col(M_MA + 2 * i, 0, win_v, COL_G + i * BLK)
                col(M_MA + 2 * i + 1, 1, lru_v, i * BLK)
            with sp_.Fori(0, HEADS // 2) as p:
                for j in range(8):
                    c = (COL_K if j % 4 >= 2 else COL_Q) + (2 * (j // 4) + j % 2) * BLK
                    col(M_D + 12 * p + j, j % 2, win_v, c + p * (4 * BLK))
                for j in range(4):
                    load(M_D + 12 * p + 8 + j, j % 2, w3(raw[j % 2]),
                         win_v[:, j * KQ:(j + 1) * KQ, ds(COL_V + p * WIDE, WIDE)])
            with sp_.Fori(0, KT) as i:
                col(M_MM + 2 * i, 0, win_v, COL_G + 2 * D + i * BLK)
                load(M_MM + 2 * i + 1, 1, k3(raw[1])[:, 0:MB, :], mem_v[:, :, ds(i * BLK, BLK)])
            with sp_.Fori(0, KT) as i:
                col(M_MD + 2 * i, 0, win_v, COL_G + D + i * BLK)
                col(M_MD + 2 * i + 1, 1, diff_v, i * BLK)
            with sp_.Fori(0, D // WIDE) as g:
                for j in range(4):
                    load(M_OUT + 4 * g + j, j % 2, w3(raw[j % 2]), out_v[:, j * KQ:(j + 1) * KQ, ds(g * WIDE, WIDE)])
            with sp_.Fori(0, PH) as h:
                for s in range(2):
                    col(M_WQ + 2 * h + s, s, wq_v, h * (2 * BLK) + s * BLK)
            for g in range(GROUPS):
                for n, tab in enumerate((u_v, v_v)):
                    m0 = M_EXP + (2 * g + n) * GC
                    with sp_.Fori(0, GC // 2) as i:
                        for s in range(2):
                            load(m0 + 2 * i + s, s, raw[s][:, :],
                                 tab[:, ds(g * GC + 2 * i + s, 1), :].rearrange("p a d -> p (a d)"))
            sp_.wait_ge(w_ready, GROUPS * GC)
            for n, v in enumerate((ln2_g, ln2_b)):
                sp_.dma_start(gbuf[:, 8 * n:8 * n + 8, :].rearrange("p a b -> p (a b)"),
                              v[0].partition_broadcast(P)).then_inc(ln2_in, 16)
            for t in range(NT):
                for half in range(2):
                    sp_.wait_ge(ln_done, 2 * NT + 2 * t + half + 1)
                    h = slice(half * D // 2, (half + 1) * D // 2)
                    sp_.dma_start(out[0, t * P:(t + 1) * P, h], res[:, t, h]).then_inc(out_done, 16)
            sp_.wait_ge(out_done, 16 * 2 * NT)

        @block.gpsimd
        def _(pool):
            for n, sems in start_free:
                for s_ in sems:
                    pool.sem_inc(s_, n)
            pool.memset(ident[:, :], 0.0).then_inc(consts, 1)
            pool.memset(ones1[:, :], 1.0).then_inc(consts, 1)
            pool.memset(axp[:, :, :], 0.0).then_inc(consts, 1)
            pool.memset(sgn[:, :], 1.0).then_inc(consts, 1)
            for j in range(HALF_ROT):
                pool.memset(ifr[0:1, j:ROT:HALF_ROT], float(THETA ** (-j / HALF_ROT))).then_inc(consts, 1)
            n = 4 + HALF_ROT
            pool.wait_ge(consts, n)
            pool.affine_select(out=ident[:, :], in_=ident[:, :], compare_op=ALU.not_equal, fill=1.0, base=0,
                               pattern=[[-1, P]], channel_multiplier=1).then_inc(consts, 1)
            pool.memset(sgn[0:HALF_ROT, :], -1.0).then_inc(consts, 1)
            v1 = ((conv_w[0].rearrange("j (n p) -> (j n) p", p=P), 0, 64), (conv_b.rearrange("a (n p) -> (a n) p", p=P), 64, 16),
                  (b_gate.rearrange("a (n p) -> (a n) p", p=P), 80, 48))
            v2 = ((lru_b_a[0].rearrange("d (n p) -> (d n) p", p=P), 0, 32), (lru_b_i[0].rearrange("d (n p) -> (d n) p", p=P), 32, 32),
                  (lru_lambda[0].rearrange("d (n p) -> (d n) p", p=P), 64, 32),
                  (diff_subln.rearrange("a (n p) -> (a n) p", p=P), 96, 2))
            for k, vs in enumerate((v1, v2)):
                for src, at0, cnt in vs:
                    pool.dma_start(vrow[at0:at0 + cnt, k, :], src).then_inc(small_in, 16)
            pool.dma_start(lp[:, :, :].rearrange("p a b -> p (a b)"),
                           diff_lambda[0].rearrange("a b -> (a b)").partition_broadcast(P)).then_inc(small_in, 16)
            pool.dma_start(posi[:, :], pos[0].partition_broadcast(ROT)).then_inc(small_in, 16)
            def load_lru(i):
                pool.wait_ge(lru_mm, i + FREE)
                for k, w in enumerate((lru_w_a, lru_w_i)):
                    pool.dma_start(lru_w[:, k, :, :], w[0].rearrange("d n i j -> i n d j")[:, ds(i, 1), :, :]
                                   .rearrange("i a d j -> i (a d) j")).then_inc(lru_in, 16)

            def lru_finish(q):
                pool.wait_ge(scanned, q + 1)
                pool.tensor_tensor(hst[:, :, 0, :], hst[:, :, 0, :], hst[:, :, 1, :], ALU.add).then_inc(summed, 1)
                pool.wait_ge(summed, 2 * q + 1)
                pool.wait_ge(gelu_kept, q + 1)
                pool.tensor_tensor(hst[:, :, 0, :], hst[:, :, 0, :], gkept[:, :, :], ALU.mult).then_inc(br_made, 1)
                pool.wait_ge(br_hi, q + 1)
                pool.tensor_tensor(brl[:, ds(2 * q, 2), :], hst[:, :, 0, :], brh[:, ds(2 * q, 2), :].bitcast(f32),
                                   ALU.subtract).then_inc(summed, 1)

            def lru_square(q):
                pool.wait_ge(bank_read[1], 2 * q + 2 + FREE)
                pool.wait_ge(br_made, q + FREE)
                settle(pool)
                pool.tensor_copy(gkept[:, :, :], gelu_gate[:, :, :]).then_inc(gelu_kept, 1)
                pool.wait_ge(decays, q + 1)
                pool.tensor_tensor(wsq[:, :, :, :], dec[:, :, :, :], dec[:, :, :, :], ALU.mult).then_inc(dec_squared, 1)

            def lru_keep(r, first=False):
                pool.wait_ge(xc_made, 2 * r + 2)
                if not first:
                    pool.wait_ge(in_made, r)
                settle(pool)
                pool.tensor_copy(xkept[:, :, :], xc[:, :, :]).then_inc(xc_kept, 1)

            def lru_round(r, stage=2):
                load_lru(2 * r)
                if stage > 1:
                    lru_finish(r - 2)
                load_lru(2 * r + 1)
                if stage > 0:
                    lru_square(r - 1)
                lru_keep(r, first=stage == 0)

            lru_round(0, 0)
            lru_round(1, 1)
            with pool.Fori(2, KT // 2) as r:
                lru_round(r)
            lru_finish(KT // 2 - 2)
            lru_square(KT // 2 - 1)
            lru_finish(KT // 2 - 1)
            with pool.Fori(0, MEM_HEADS) as h:
                pool.wait_ge(kv_made, MB + MEM_W // WIDE + MB)
                pool.wait_ge(mpv, h + FREE)
                pool.tensor_copy(mqs[:, :, :], mq[:, ds(h * MC, MC), :]).then_inc(staged, 1)
                pool.tensor_copy(mvs[:, :, :], mv[:, :, ds(h * MEM_DIM, MEM_DIM)]).then_inc(staged, 1)
            pool.wait_ge(units_done, 2 * M_OUT)
            for t in range(NT):
                pool.dma_start(res[:, t, :], x[0, t * P:(t + 1) * P, :]).then_inc(res_in, 16)
                pool.wait_ge(units_done, 2 * (M_OUT + 2 * t + 2))
            pool.dma_start(gbuf[:, 0:8, :].rearrange("p a b -> p (a b)").rearrange("p (a b) -> p a b", b=P),
                           sub_keys[0].rearrange("h j n c -> n (h j) c")).then_inc(sub_in, 16)
            for n_, (v, dst) in enumerate(((ln1_g, 0), (ln1_b, 8))):
                pool.wait_ge(units_done, 2 * (M_OUT + 2 * n_ + 6))
                pool.dma_start(hbuf[:, dst:dst + 8, :].rearrange("p a b -> p (a b)"),
                               v[0].partition_broadcast(P)).then_inc(ln1_in, 16)
            pool.wait_ge(ln_done, 2 * NT)
            pool.iota(iota[:, :], [[1, P]], base=0, channel_multiplier=0,
                      allow_small_or_imprecise_dtypes=True).then_inc(consts, 1)
            pool.iota(iota16[:, :], [[1, TOPK]], base=0, channel_multiplier=0,
                      allow_small_or_imprecise_dtypes=True).then_inc(consts, 1)
            pool.wait_ge(consts, n + 4)
            with pool.Fori(0, PH) as h:
                pool.wait_ge(hit_made, h + 1)
                pool.tensor_tensor(hit, hit, top_i[:, ds(h, 1), :, :, :].rearrange("p a j t r -> p (a j t) r").unsqueeze(2)
                                   .broadcast_to([P, 2 * NT, TOPK, TOPK]), ALU.mult).then_inc(hit_keys, 1)

            def one_hot2(n, b, step):
                pool.wait_ge(i2_staged, n + 1)
                pool.wait_ge(gate_mm, step - 1 + FREE2)
                settle(pool)
                for k in range(GT):
                    last = pool.tensor_scalar(one2[b][:, k, :], keys[:, :], i2s[b][:, k:k + 1], None, ALU.is_equal)
                last.then_inc(one2_made, 1)

            with pool.Fori(0, STEPS // 2) as n:
                one_hot2(n, 0, 2 * n)
            with pool.Fori(0, (GROUPS - 1) * STEPS // 2) as n:
                for b in range(2):
                    one_hot2(2 * n + STEPS // 2 + b, b, 2 * n + STEPS + b)
            pool.tensor_scalar(res[:, :, :], res[:, :, :], ALPHA, None, ALU.mult).then_inc(res_scaled, 1)
            pool.wait_ge(acc_read, 8 * (GROUPS - 1))
            pool.wait_ge(res_scaled, 1)
            pool.tensor_tensor(acc[:, :, :], acc[:, :, :], res[:, :, :], ALU.add).then_inc(res_added, 1)

        @block.scalar
        def _(act):
            link = Link(act, act_link)

            def split(m, s, kt=KT, free=True, into=None, after=None):
                d = s if into is None else into
                u = m - 2 if after is None else after
                act.wait_ge(raw_in[s], (m + PRE - s) * 8 + 16)
                for q in range(2):
                    if free:
                        act.wait_ge(units_done, 2 * u + 1 + q)
                    h = slice(q * HALF, min((q + 1) * HALF, kt * BLK))
                    act.activation(hi[d][:, h], raw[s][:, h], ACT.Copy).then_inc(hi_made, 2)

            def split_turned(m, s, j):
                for b in range(4):
                    if b % 2 == 0:
                        act.wait_ge(units_done, 2 * m - 3 + b // 2)
                    act.wait_ge(turned, j * 4 + (b + 1))
                    act.activation(hi[s][:, b * 512:(b + 1) * 512], psT[b][:, :], ACT.Copy).then_inc(hi_made, 1)

            def result(m, b):
                act.wait_ge(units_done, 2 * m + 2)

            def take_rows(r, m, dst, t):
                for b in range(4):
                    act.wait_ge(turned, 4 * r + b + 1)
                    act.activation(dst[:, 4 * b:4 * b + 4, t * P:(t + 1) * P],
                                   psT[b][:, :].rearrange("p (k c) -> p k c", c=P), ACT.Copy).then_inc(hi_made, 1)

            for t in range(NT):
                take_rows(t, t - PRE, xh, t)
            split(0, 0, free=False)

            def setup_vectors():
                act.wait_ge(vec_turned, 1)
                act.activation(vec[:, :, :].rearrange("p a b -> p (a b)")[:, 0:P + 98], psS[0][:, 0:P + 98], ACT.Copy).then_inc(set_act, 1)
                act.activation(ifc[:, :], psS[1][0:ROT, 0:1], ACT.Copy).then_inc(set_act, 1)

            def setup_exp():
                act.wait_ge(set_dve, 1)
                act.activation(spt[:, 1, :], spt[:, 0, :], ACT.Exp, scale=-1.0).then_inc(set_act, 1)
                act.activation(lame[:, :], lsum[:, :], ACT.Exp).then_inc(set_act, 1)

            def setup_sin():
                act.wait_ge(set_dve, 3)
                act.activation(sinT[:, :], rtmp[:, 2, :], ACT.Sin).then_inc(set_act, 1)
                act.activation(cosT[:, :], rtmp[:, 3, :], ACT.Sin).then_inc(set_act, 1)

            def lru_gates(q, first=False):
                result(M_LRU + 4 * q + 3, 1)
                if not first:
                    act.wait_ge(gelu_kept, q)
                for b in range(2):
                    act.activation(gelu_gate[:, b, :], (psU, psS)[b][1][:, 0:TOK], ACT.Gelu).then_inc(bank_read[1], 1)
                act.wait_ge(lru_mm, 2 * q + 2 + FREE)
                for b in range(2):
                    for d in range(2):
                        o = psT[2 * b + d]
                        act.activation(t_i[:, b, d, :], o[:, TOK:2 * TOK], ACT.Tanh, bias=hb[:, ds(2 * q + b + 32 + 16 * d, 1)], scale=0.5)
                        last = act.activation(t_r[:, b, d, :], o[:, 0:TOK], ACT.Tanh, bias=hb[:, ds(2 * q + b + 16 * d, 1)], scale=0.5)
                last.then_inc(gates_read, 1)

            def lru_decays(q):
                act.wait_ge(gates_read, q + 1 + FREE)
                for d in range(2):
                    for b in range(2):
                        last = act.activation(dec[:, b, d, :], t_r[:, b, d, :], ACT.Exp, bias=nsp[:, ds(2 * q + b + 16 * d, 1)],
                                              scale=nsp[:, ds(2 * q + b + 16 * d, 1)])
                last.then_inc(decays, 1)
                for d in range(2):
                    for b in range(2):
                        last = act.activation(t_r[:, b, d, :], t_r[:, b, d, :], ACT.Tanh, bias=sp[:, ds(2 * q + b + 16 * d, 1)],
                                              scale=sp[:, ds(2 * q + b + 16 * d, 1)])
                last.then_inc(exponents, 1)

            def lru_root(q):
                act.wait_ge(w_made, q + 1)
                act.activation(wsq[:, :, :, :], wsq[:, :, :, :], ACT.Sqrt).then_inc(root_made, 1)

            def lru_out(q):
                act.wait_ge(br_made, q + 1 + FREE)
                act.activation(brh[:, ds(2 * q, 2), :], hst[:, :, 0, :], ACT.Copy).then_inc(br_hi, 1)

            def lru_round(r, stage=2):
                m = M_LRU + 4 * r
                split(m + 1, 1, free=stage > 0)
                if stage == 0:
                    setup_vectors()
                if stage == 1:
                    act.wait_ge(set_dve, 2)
                if stage > 0:
                    lru_gates(r - 1, first=stage == 1)
                if stage > 1:
                    lru_out(r - 2)
                split(m + 2, 0)
                if stage == 0:
                    setup_exp()
                if stage > 0:
                    lru_decays(r - 1)
                split(m + 3, 1)
                if stage > 0:
                    lru_root(r - 1)
                split(m + 4, 0)

            lru_round(0, 0)
            lru_round(1, 1)
            setup_sin()
            with act.Fori(2, KT // 2) as r:
                lru_round(r)

            def take_block(m, dst, n, s, b):
                result(m, s)
                act.activation(dst[:, ds(n, 1), :].rearrange("p a t -> p (a t)"), psU[b][:, 0:TOK],
                               ACT.Copy).then_inc(bank_read[b], 1)

            last_pair = KT // 2 - 1
            split(M_MQ + 1, 1)
            lru_gates(last_pair)
            lru_out(last_pair - 1)
            take_block(M_MQ, mq, 0, 0, 0)
            split(M_MQ + 2, 0)
            lru_decays(last_pair)
            take_block(M_MQ + 1, mq, 1, 1, 1)
            split(M_MQ + 3, 1)
            lru_root(last_pair)
            take_block(M_MQ + 2, mq, 2, 0, 0)
            split(M_MQ + 4, 0)
            lru_out(last_pair)
            take_block(M_MQ + 3, mq, 3, 1, 1)
            with act.Fori(2, MB // 2 - 2) as i:
                m = M_MQ + 2 * i
                for s in range(2):
                    split(m + 1 + s, 1 - s)
                    take_block(m + s, mq, 2 * i + s, s, s)
            split(M_MEM - 1, 1)
            take_block(M_MEM - 2, mq, MB - 4, 0, 0)
            take_rows(2, M_MEM, memh, 0)
            split(M_MEM + 1, 1, into=0, after=M_MEM - 2)
            take_block(M_MEM - 1, mq, MB - 3, 1, 1)
            take_rows(3, M_MEM + 2, memh, 1)
            split(M_MEM + 3, 1, after=M_MEM - 1)
            take_block(M_MEM + 1, mq, MB - 2, 1, 0)
            split(M_MK, 0, after=M_MEM + 1)
            take_block(M_MEM + 3, mq, MB - 1, 1, 1)
            act.wait_ge(summed, KT)
            with act.Fori(0, MB // 2) as i:
                m = M_MK + 2 * i
                for s in range(2):
                    split(m + 1 + s, 1 - s)
                    take_block(m + s, mk, 2 * i + s, s, s)
            with act.Fori(0, MEM_W // WIDE) as g:
                for j in range(4):
                    split(M_MV + 4 * g + j + 1, (j + 1) % 2)

            def gate(m, col):
                result(m, 0)
                act.activation(gt[:, :], psU[0][:, 0:TOK], ACT.Sigmoid, bias=vec[:, 0, ds(col + 80, 1)]).then_inc(bank_read[0], 1)

            with act.Fori(0, MEM_HEADS) as h:
                for k in range(4):
                    m = M_MA + 8 * h + 2 * k
                    split(m + 1, 1)
                    act.wait_ge(merge_made, 4 * h + k + FREE)
                    gate(m, 4 * h + k)
                    split(m + 2, 0)
                    if k == 0:
                        act.wait_ge(mmax, h + 1)
                        for t in range(NT):
                            last = act.activation(pm[:, t, :], psS[t][:, 0:MEM], ACT.Exp, bias=nmx[:, t:t + 1],
                                                  scale=MSCALE, accum_out=zs[:, t:t + 1])
                        last.then_inc(mexp, 1)
                    if k == 2:
                        act.wait_ge(mturned, h + 1)
                        act.activation(pmT[:, :, :].rearrange("p a t -> p (a t)"), psT[2][:, :], ACT.Copy).then_inc(mpT, 1)
                    if k == 3:
                        act.wait_ge(mpv, h + 1 + FREE)
                        for c in range(MC):
                            act.activation(brmh[:, ds(h * MC + c, 1), :].rearrange("p a t -> p (a t)"),
                                           psT[(0, 1, 3)[c]][:, 0:TOK], ACT.Copy).then_inc(mhi, 1)

            def softmax_exp(p, hh):
                act.wait_ge(smax, 2 * p + hh + 1)
                for t in range(NT):
                    for j in range(2):
                        c = 4 * hh + 2 * t + j
                        last = act.activation(ex[:, hh, t, j, :], (psS, psT[2:4])[hh][t][:, j * TOK:(j + 1) * TOK], ACT.Exp,
                                              bias=nmx[:, c:c + 1], scale=QSCALE, accum_out=zs[:, c:c + 1])
                last.then_inc(sexp, 1)

            def take_turned_attn(p, hh):
                act.wait_ge(aturned, 2 * p + hh + 1)
                act.activation(at[:, hh, :, :].rearrange("p a t -> p (a t)"), psS[hh][:, :], ACT.Copy).then_inc(atT, 1)

            def head_norm(p):
                for hh in range(2):
                    act.wait_ge(pv, 2 * p + hh + 1)
                    for t in range(NT):
                        last = act.activation(ex[:, hh, t, 1, :], psT[2 + hh][:, t * VD:(t + 1) * VD], ACT.Square,
                                              accum_out=ssq[:, 2 * hh + t:2 * hh + t + 1])
                last.then_inc(sqsum, 1)
                act.wait_ge(srt, 2 * p + 1)
                act.activation(rstd[:, :], ssq[:, :], ACT.Sqrt).then_inc(sqsum, 1)

            def take_heads(p):
                for hh in range(2):
                    act.wait_ge(oturned, 2 * p + hh + 1)
                    for c in range(2):
                        act.activation(brh[:, ds(4 * p + 2 * hh + c, 1), :].rearrange("p a t -> p (a t)"),
                                       psS[hh][:, c * TOK:(c + 1) * TOK], ACT.Copy, scale=vec[:, 1, 98 + c:99 + c]).then_inc(ohi, 1)

            def attention(p, before=None):
                m = M_D + 12 * p
                for j in range(8):
                    split(m + j + 1, (j + 1) % 2)
                    if j == 0:
                        act.wait_ge(score, 2 * p + FREE)
                    if j == 1 and before is not None:
                        head_norm(before)
                    if j == 4 and before is not None:
                        take_heads(before)
                    if j == 7:
                        softmax_exp(p, 0)
                    result(m + j, j % 2)
                    act.activation(qk[:, j, :], psU[j % 2][:, 0:TOK], ACT.Copy).then_inc(bank_read[j % 2], 1)
                split(m + 9, 1)
                split(m + 10, 0)
                take_turned_attn(p, 0)
                split(m + 11, 1)
                softmax_exp(p, 1)
                split(m + 12, 0)
                take_turned_attn(p, 1)

            attention(0)
            with act.Fori(1, HEADS // 2) as p:
                attention(p, before=p - 1)

            def merge(i, base_m, col, n0):
                m = base_m + 2 * i
                split(m + 1, 1, MB if n0 == 1 else KT)
                act.wait_ge(merge_made, n0 * KT + i + FREE)
                gate(m, i + col)
                split(m + 2, 0)
                if n0 == 2:
                    act.wait_ge(merge_made, n0 * KT + i + 1 + FREE)
                    act.activation(mh[:, ds(i, 1), :].rearrange("p a t -> p (a t)"),
                                   merged[:, ds(i, 1), :].rearrange("p a t -> p (a t)"), ACT.Copy).then_inc(mg_hi, 1)

            merge(0, M_MM, 32, 1)
            head_norm(HEADS // 2 - 1)
            merge(1, M_MM, 32, 1)
            take_heads(HEADS // 2 - 1)
            with act.Fori(2, KT) as i:
                merge(i, M_MM, 32, 1)
            with act.Fori(0, KT) as i:
                merge(i, M_MD, 16, 2)

            with act.Fori(0, D // WIDE) as g:
                for j in range(4):
                    split(M_OUT + 4 * g + j + 1, (j + 1) % 2)

            def norm_act(k, scratch, between=lambda: None):
                for t in range(NT):
                    act.wait_ge(ln_mean, NT * k + t + 1)
                    act.activation(scratch, res[:, t, :], ACT.Square, bias=nmom[:, t:t + 1],
                                   accum_out=mom[:, 1, t:t + 1]).then_inc(ln_act, 1)
                    if t == 0:
                        between()
                    act.wait_ge(ln_dve, NT * k + t + 1)
                    act.activation(mom[:, 2, t:t + 1], mom[:, 1, t:t + 1], ACT.Sqrt).then_inc(ln_act, 1)

            act.activation(mom[:, 3, :], ident[:, 0:2], ACT.Sqrt)
            def take_sub_keys():
                for b in range(4):
                    act.wait_ge(sub_turned, b + 1)
                    act.activation(skT[:, 4 * b:4 * b + 4, :].rearrange("p a n -> p (a n)"), psT[b][:, :], ACT.Copy).then_inc(sk_made, 1)

            norm_act(0, hbuf[:, 16:24, :].rearrange("p a b -> p (a b)"), take_sub_keys)
            for t in range(NT):
                for b in range(4):
                    act.wait_ge(x1_turned, 4 * t + b + 1)
                    act.activation(x1h[:, 4 * b:4 * b + 4, t * P:(t + 1) * P],
                                   psT[b][:, :].rearrange("p (k c) -> p k c", c=P), ACT.Copy).then_inc(x1_hi, 1)

            def query(h, m, j):
                act.wait_ge(key_score, 2 * h + j - 1 + FREE2)
                result(m + j, j)
                act.activation(qT[:, j, :], psU[j][:, 0:TOK], ACT.Copy).then_inc(bank_read[j], 1)

            with act.Fori(0, PH - 1) as h:
                m = M_WQ + 2 * h
                split(m + 1, 1)
                query(h, m, 0)
                split(m + 2, 0)
                query(h, m, 1)
            split(M_EXP - 1, 1)
            query(PH - 1, M_EXP - 2, 0)
            split_turned(M_EXP, 0, TURNS)
            query(PH - 1, M_EXP - 2, 1)

            def take_h(m, s, c):
                result(m, s)
                act.activation(hbuf[:, ds(c, 1), :].rearrange("p a t -> p (a t)"), psU[s][:, 0:TOK],
                               ACT.Gelu).then_inc(bank_read[s], 1)

            def split_w(m, s, n):
                act.wait_ge(w_ready, n + 1)
                act.wait_ge(units_done, 2 * m - 2)
                act.activation(wh[s][:, :], wt[:, :], ACT.Copy).then_inc(w_hi, 1)

            def best_gates(n):
                act.wait_ge(best_made, n + 1)
                for t in range(NT):
                    last = act.activation(eb[:, t, :], best[:, t, :], ACT.Exp, bias=nbest[:, t:t + 1], accum_out=zb[:, t:t + 1])
                last.then_inc(best_exp, 1)

            def one_hot2(n):
                act.wait_ge(neg_staged, n + 1)
                act.wait_ge(act_one2, n + FREE)
                for k in range(GT):
                    last = act.activation(dist[:, k, :], keys[:, :], ACT.Square, bias=neg_i2[:, k:k + 1])
                last.then_inc(dist_made, 1)
                act.wait_ge(dist_made, n + 1)
                act.activation(one2[1][:, :, :], dist[:, :, :], ACT.Relu, bias=1.0, scale=-1.0).then_inc(act_one2, 1)

            for g in range(GROUPS):
                mu, mv_ = M_EXP + 2 * g * GC, M_EXP + (2 * g + 1) * GC
                ju = TURNS + g * GC

                def pair(i, last=False, extra=lambda i: None, first_step=None):
                    m = mu + 2 * i
                    split_turned(m + 1, 1, ju + 2 * i + 1)
                    if first_step is not None:
                        one_hot2(2 * first_step)
                    take_h(m, 0, 2 * i)
                    if last:
                        split(m + 2, 0)
                    else:
                        split_turned(m + 2, 0, ju + 2 * i + 2)
                    extra(i)
                    if first_step is not None:
                        one_hot2(2 * first_step + 1)
                    take_h(m + 1, 1, 2 * i + 1)

                if g > 0:
                    act.wait_ge(w_ready, g * GC)
                    with act.Fori(0, GC // 2 - 1) as i:
                        pair(i)
                else:
                    with act.Fori(0, HALF0) as i:
                        pair(i, extra=best_gates)
                    act.wait_ge(pick_turned, 1)
                    act.activation(pickT[:, 0:2, :].rearrange("p a t -> p (a t)"), psS[1][:, :], ACT.Copy).then_inc(pickT_made, 1)
                    act.activation(pickT[:, 2, :], psS[0][:, 0:TOK], ACT.Copy).then_inc(pickT_made, 1)
                    with act.Fori(HALF0, GC // 2 - 1) as i:
                        pair(i, first_step=i - HALF0)
                pair(GC // 2 - 1, last=True, first_step=GC // 2 - 1 - HALF0 if g == 0 else None)
                split_w(mv_, 0, g * GC)

                def vpair(i, last=False):
                    m = mv_ + 2 * i
                    split(m + 1, 1)
                    split_w(m + 1, 1, g * GC + 2 * i + 1)
                    if not last:
                        split(m + 2, 0)
                        split_w(m + 2, 0, g * GC + 2 * i + 2)
                    elif g + 1 < GROUPS:
                        split_turned(m + 2, 0, ju + GC)

                with act.Fori(0, GC // 2 - 1) as i:
                    vpair(i)
                vpair(GC // 2 - 1, last=True)
            norm_act(1, gbuf[:, 16:24, :].rearrange("p a b -> p (a b)"))

        @block.vector
        def _(dve):
            link = Link(dve, dve_link)

            def split(m, s, kt=KT, into=None):
                d = s if into is None else into
                for q in range(2):
                    dve.wait_ge(hi_made, (m + PRE) * 4 + 2 * (q + 1))
                    h = slice(q * HALF, min((q + 1) * HALF, kt * BLK))
                    dve.tensor_tensor(lo[d][:, h], raw[s][:, h], hi[d][:, h].bitcast(f32), ALU.subtract).then_inc(lo_made, 2)

            def split_turned(m, s):
                for b in range(4):
                    dve.wait_ge(hi_made, (m + PRE) * 4 + (b + 1))
                    h = slice(b * 512, (b + 1) * 512)
                    dve.tensor_tensor(lo[s][:, h], psT[b][:, :], hi[s][:, h].bitcast(f32), ALU.subtract).then_inc(lo_made, 1)

            def split_rows(m, hi_, lo_, t):
                for b in range(4):
                    dve.wait_ge(hi_made, (m + PRE) * 4 + b + 1)
                    w = (slice(None), slice(4 * b, 4 * b + 4), slice(t * P, (t + 1) * P))
                    dve.tensor_tensor(lo_[w], psT[b][:, :].rearrange("p (k c) -> p k c", c=P), hi_[w].bitcast(f32),
                                      ALU.subtract).then_inc(lo_made, 1)

            for t in range(NT):
                split_rows(t - PRE, xh, xl, t)
            split(0, 0)

            def setup_sums():
                dve.wait_ge(set_act, 2)
                dve.wait_ge(small_in, 9 * 16)
                dve.tensor_scalar(hb[:, :], vec[:, 1, 0:64], 0.5, None, ALU.mult)
                dve.scalar_tensor_tensor(spt[:, 0, :], vec[:, 1, 64:96], -1.0, vec[:, 1, 64:96], ALU.mult, ALU.max)
                link(dve.tensor_tensor(lp[:, 0:4:2, :], lp[:, 0:4:2, :], lp[:, 1:4:2, :], ALU.mult))
                dve.tensor_reduce(lsum[:, :], lp[:, 0:4:2, :], AX.X, ALU.add).then_inc(set_dve, 1)

            def setup_softplus():
                dve.wait_ge(set_act, 4)
                s0, e_, r_, s2 = (spt[:, k, :] for k in range(4))
                link(dve.tensor_scalar(r_, e_, 2.0, None, ALU.add))
                link(dve.reciprocal(r_, r_))
                link(dve.tensor_tensor(r_, r_, e_, ALU.mult))
                link(dve.tensor_tensor(s2, r_, r_, ALU.mult))
                link(dve.tensor_scalar(s0, s2, 1.0 / 17, None, ALU.mult))
                for k in (15, 13, 11, 9, 7, 5, 3):
                    link(dve.scalar_tensor_tensor(s0, s0, 1.0 / k, s2, ALU.add, ALU.mult))
                link(dve.scalar_tensor_tensor(s0, s0, 1.0, r_, ALU.add, ALU.mult))
                link(dve.tensor_scalar(e_, vec[:, 1, 64:96], -1.0, 0.0, ALU.mult, ALU.max))
                link(dve.scalar_tensor_tensor(s0, s0, 2.0, e_, ALU.mult, ALU.add))
                link(dve.tensor_scalar(sp[:, :], s0, 4.0, None, ALU.mult))
                link(dve.tensor_scalar(nsp[:, :], sp[:, :], -1.0, None, ALU.mult))
                link(dve.tensor_tensor(nlam[:, :], lame[:, 1:2], lame[:, 0:1], ALU.subtract))
                link(dve.tensor_scalar(nlam[:, :], nlam[:, :], -LAM_INIT, None, ALU.add))
                dve.tensor_scalar(vec[:, 1, 98:100], vec[:, 1, 96:98], 1.0 - LAM_INIT, None, ALU.mult).then_inc(set_dve, 1)

            def setup_angles():
                ang, turns, red, cang = (rtmp[:, k, :] for k in range(4))
                link(dve.tensor_copy(turns, posi[:, :]))
                link(dve.tensor_scalar(ang, turns, ifc[:, 0:1], None, ALU.mult))
                magic = 1.5 * 2.0 ** 23
                link(dve.tensor_scalar(turns, ang, 1.0 / (2 * math.pi), magic, ALU.mult, ALU.add))
                link(dve.tensor_scalar(turns, turns, -magic, None, ALU.add))
                c1 = 6.28125
                c2 = math.floor((2 * math.pi - c1) * 2.0 ** 20) / 2.0 ** 20
                c3 = 2 * math.pi - c1 - c2
                link(dve.scalar_tensor_tensor(red, turns, -c1, ang, ALU.mult, ALU.add))
                link(dve.scalar_tensor_tensor(red, turns, -c2, red, ALU.mult, ALU.add))
                link(dve.scalar_tensor_tensor(red, turns, -c3, red, ALU.mult, ALU.add))
                link(dve.tensor_scalar(red, red, 3.1415925, -3.1415925, ALU.min, ALU.max))
                link(dve.scalar_tensor_tensor(cang, red, -1.0, red, ALU.mult, ALU.min))
                dve.tensor_scalar(cang, cang, math.pi / 2, None, ALU.add).then_inc(set_dve, 1)

            def conv(r, b, first=False):
                n = 2 * r + b
                x_, ax = xc[:, b, :], axp[:, b, :]
                dve.wait_ge(units_done, 2 * (M_LRU + 2 * n) + 2)
                dve.tensor_copy(ax[:, 1:TOK + 1], (psU, psS)[b][0][:, 0:TOK]).then_inc(bank_read[0], 1)
                if not first and b == 0:
                    dve.wait_ge(xc_kept, r)
                dve.wait_ge(bank_read[0], n + 1 + FREE)
                link(dve.tensor_scalar(x_, ax[:, 0:TOK], vec[:, 0, ds(n, 1)], vec[:, 0, ds(n + 64, 1)], ALU.mult, ALU.add))
                for j in (1, 2):
                    link(dve.scalar_tensor_tensor(x_, ax[:, j:TOK + j], vec[:, 0, ds(n + 16 * j, 1)], x_, ALU.mult, ALU.add))
                dve.scalar_tensor_tensor(x_, ax[:, 3:TOK + 3], vec[:, 0, ds(n + 48, 1)], x_, ALU.mult, ALU.add).then_inc(xc_made, 1)

            def lru_input(q, first=False):
                if not first:
                    dve.wait_ge(scanned, q)
                dve.wait_ge(gates_read, q + 1 + FREE)
                dve.wait_ge(xc_kept, q + 1)
                for b in range(2):
                    last = dve.scalar_tensor_tensor(uin[:, b, :, :], t_i[:, b, :, :], 1.0,
                                                    xkept[:, b, :].unsqueeze(1).broadcast_to([P, 2, TOK]), ALU.add, ALU.mult)
                last.then_inc(in_made, 1)

            def lru_weight(q):
                dve.wait_ge(dec_squared, q + 1)
                dve.wait_ge(exponents, q + 1)
                dve.scalar_tensor_tensor(wsq[:, :, :, :], wsq[:, :, :, :], 1.0, t_r[:, :, :, :], ALU.add, ALU.mult).then_inc(w_made, 1)

            def lru_scan(q):
                dve.wait_ge(in_made, q + 1)
                dve.wait_ge(root_made, q + 1)
                link(dve.scalar_tensor_tensor(uin[:, :, :, :], wsq[:, :, :, :], 0.5, uin[:, :, :, :], ALU.mult, ALU.mult))
                for b in range(2):
                    dve.tensor_tensor_scan(hst[:, b, 0, :], dec[:, b, 0, :], uin[:, b, 0, :], 0.0, ALU.mult, ALU.add)
                    last = dve.tensor_tensor_scan(hst[:, b, 1, ::-1], dec[:, b, 1, ::-1], uin[:, b, 1, ::-1], 0.0, ALU.mult, ALU.add)
                last.then_inc(scanned, 1)

            def lru_round(r, stage=2):
                m = M_LRU + 4 * r
                split(m + 1, 1)
                if stage == 0:
                    dve.wait_ge(set_act, 2)
                    dve.wait_ge(consts, 6 + HALF_ROT)
                conv(r, 0, first=stage == 0)
                split(m + 2, 0)
                if stage == 0:
                    setup_sums()
                if stage > 0:
                    lru_input(r - 1, first=stage == 1)
                split(m + 3, 1)
                if stage > 0:
                    lru_weight(r - 1)
                conv(r, 1)
                split(m + 4, 0)
                if stage == 0:
                    setup_softplus()
                    setup_angles()
                if stage > 1:
                    dve.wait_ge(summed, 2 * r - 2)
                if stage > 0:
                    lru_scan(r - 1)

            lru_round(0, 0)
            lru_round(1, 1)
            dve.wait_ge(set_act, 6)
            dve.tensor_scalar(sinT[:, :], sinT[:, :], sgn[:, 0:1], None, ALU.mult).then_inc(set_dve, 1)
            with link.loop(KT // 2 - 2, 7, first=2) as r:
                lru_round(r)
            last_pair = KT // 2 - 1
            split(M_MQ + 1, 1)
            lru_input(last_pair)
            split(M_MQ + 2, 0)
            lru_weight(last_pair)
            split(M_MQ + 3, 1)
            dve.wait_ge(summed, 2 * last_pair)
            lru_scan(last_pair)
            split(M_MQ + 4, 0)

            def wide(m, split_, n, take):
                for j in range(4):
                    split_(m + j + 1, (j + 1) % 2)
                dve.wait_ge(units_done, 2 * m + 8)
                take()

            with dve.Fori(2, MB // 2 - 2) as i:
                for s in range(2):
                    split(M_MQ + 2 * i + s + 1, 1 - s)
            split(M_MEM - 1, 1)
            for t in range(NT):
                split_rows(M_MEM + 2 * t, memh, meml, t)
                split(M_MEM + 2 * t + 1, 1, into=t)
            split(M_MK, 0)
            with dve.Fori(0, MB // 2) as i:
                for s in range(2):
                    split(M_MK + 2 * i + s + 1, 1 - s)
            dve.wait_ge(summed, KT)
            for g in range(MEM_W // WIDE):
                def take():
                    for t in range(2):
                        last = dve.tensor_copy(mv[:, t, g * WIDE:(g + 1) * WIDE], psT[g % 2 * 2 + t][:, :])
                    last.then_inc(tok_read, 1)
                wide(M_MV + 4 * g, split, g, take)
            dve.wait_ge(bank_read[1], KT + MB + FREE)
            dve.wait_ge(bank_read[0], KT + MB + FREE)
            dve.tensor_copy(mx[:, 0:1], nsp[:, 0:1]).then_inc(kv_made, MB + MEM_W // WIDE + MB)

            with link.loop(MEM_HEADS, 1) as h:
                for k in range(4):
                    m = M_MA + 8 * h + 2 * k
                    split(m + 1, 1)
                    if k == 0:
                        dve.wait_ge(mscore, h + 1)
                        for t in range(NT):
                            last = dve.tensor_reduce(mx[:, t:t + 1], psS[t][:, 0:MEM], AX.X, ALU.max)
                        link(last)
                        dve.tensor_scalar(nmx[:, 0:2], mx[:, 0:2], -MSCALE, None, ALU.mult).then_inc(mmax, 1)
                    split(m + 2, 0)
                    if k == 1:
                        dve.wait_ge(mexp, h + 1)
                        dve.reciprocal(rz[:, 0:2], zs[:, 0:2]).then_inc(mprob, 1)
                        dve.wait_ge(mprob, 2 * h + 1)
                        for t in range(NT):
                            last = dve.tensor_scalar(pm[:, t, :], pm[:, t, :], rz[:, t:t + 1], None, ALU.mult)
                        last.then_inc(mprob, 1)
                    dve.wait_ge(units_done, 2 * m + 4)
                    dve.wait_ge(bank_read[0], KT + MB + 4 * h + k + 1 + FREE)
                    dve.tensor_tensor(merged[:, ds(4 * h + k, 1), :].rearrange("p a t -> p (a t)"), psU[1][:, 0:TOK],
                                      gt[:, :], ALU.mult).then_inc(merge_made, 1)
                    if k == 3:
                        for c in range(MC):
                            dve.wait_ge(mhi, MC * h + c + 1)
                            w = (slice(None), ds(h * MC + c, 1), slice(None))
                            dve.tensor_tensor(brml[w].rearrange("p a t -> p (a t)"), psT[(0, 1, 3)[c]][:, 0:TOK],
                                              brmh[w].rearrange("p a t -> p (a t)").bitcast(f32), ALU.subtract).then_inc(mlo, 1)

            def rotary(p, hh):
                dve.wait_ge(bank_read[1], KT + MB + 4 * p + 2 * hh + 2 + FREE)
                dve.wait_ge(bank_read[0], KT + MB + KT + 4 * p + 2 * hh + 2 + FREE)
                rows4 = qk[0:ROT, 4 * hh:4 * hh + 4, :]
                cos4 = cosT[:, :].unsqueeze(1).broadcast_to([ROT, 4, TOK])
                sin4 = sinT[:, :].unsqueeze(1).broadcast_to([ROT, 4, TOK])
                settle(dve)
                link(dve.stream_shuffle(rsh[:, :, :], rows4, [(k + HALF_ROT) % ROT for k in range(ROT)]))
                link(dve.tensor_tensor(rsh[:, :, :], rsh[:, :, :], sin4, ALU.mult))
                link(dve.tensor_tensor(rows4, rows4, cos4, ALU.mult))
                dve.tensor_tensor(rows4, rows4, rsh[:, :, :], ALU.add).then_inc(rotated, 1)

            def softmax_max(p, hh):
                dve.wait_ge(score, 2 * p + hh + 1 + FREE)
                for t in range(NT):
                    c = 4 * hh + 2 * t
                    last = dve.tensor_reduce(mx[:, c:c + 2], (psS, psT[2:4])[hh][t][:, :].rearrange("p (j k) -> p j k", j=2), AX.X, ALU.max)
                link(last)
                dve.tensor_scalar(nmx[:, 4 * hh:4 * hh + 4], mx[:, 4 * hh:4 * hh + 4], -QSCALE, None, ALU.mult).then_inc(smax, 1)

            def attn_weights(p, hh):
                dve.wait_ge(sexp, 2 * p + hh + 1)
                z = slice(4 * hh, 4 * hh + 4)
                zo = slice(4 * hh + 1, 4 * hh + 4, 2)
                link(dve.reciprocal(rz[:, z], zs[:, z]))
                link(dve.tensor_scalar(rz[:, zo], rz[:, zo], nlam[:, 0:1], None, ALU.mult))
                for t in range(NT):
                    c = 4 * hh + 2 * t
                    last = dve.tensor_scalar(ex[:, hh, t, 1, :], ex[:, hh, t, 1, :], rz[:, c + 1:c + 2], None, ALU.mult)
                link(last)
                for t in range(NT):
                    c = 4 * hh + 2 * t
                    last = dve.scalar_tensor_tensor(ex[:, hh, t, 0, :], ex[:, hh, t, 0, :], rz[:, c:c + 1],
                                                    ex[:, hh, t, 1, :], ALU.mult, ALU.add)
                last.then_inc(attn, 1)

            def head_norm(p):
                dve.wait_ge(sqsum, 2 * p + 1)
                dve.tensor_scalar(ssq[:, :], ssq[:, :], 1.0 / VD, EPS, ALU.mult, ALU.add).then_inc(srt, 1)
                dve.wait_ge(sqsum, 2 * p + 2)
                dve.reciprocal(rstd[:, :], rstd[:, :]).then_inc(srt, 1)
                dve.wait_ge(srt, 2 * p + 2)
                for hh in range(2):
                    for t in range(NT):
                        last = dve.tensor_scalar(ex[:, hh, t, 0, :], psT[2 + hh][:, t * VD:(t + 1) * VD],
                                                 rstd[:, 2 * hh + t:2 * hh + t + 1], None, ALU.mult)
                    last.then_inc(onorm, 1)

            def take_heads(p):
                for hh in range(2):
                    dve.wait_ge(ohi, 4 * p + 2 * hh + 2)
                    for c in range(2):
                        w = (slice(None), ds(4 * p + 2 * hh + c, 1), slice(None))
                        dve.scalar_tensor_tensor(brl[w].rearrange("p a t -> p (a t)"), psS[hh][:, c * TOK:(c + 1) * TOK],
                                                 vec[:, 1, 98 + c:99 + c], brh[w].rearrange("p a t -> p (a t)").bitcast(f32),
                                                 ALU.mult, ALU.subtract).then_inc(olo, 1)

            def attention(p, before=None):
                m = M_D + 12 * p
                for j in range(7):
                    split(m + j + 1, (j + 1) % 2)
                    if j == 1 and before is not None:
                        head_norm(before)
                    if j == 4:
                        rotary(p, 0)
                        if before is not None:
                            take_heads(before)
                softmax_max(p, 0)
                split(m + 8, 0)
                attn_weights(p, 0)
                split(m + 9, 1)
                rotary(p, 1)
                split(m + 10, 0)
                split(m + 11, 1)
                softmax_max(p, 1)
                attn_weights(p, 1)
                split(m + 12, 0)
                dve.wait_ge(units_done, 2 * m + 24)
                for t in range(2):
                    last = dve.tensor_copy(vv[:, t, :], psT[t][:, :])
                last.then_inc(tok_read, 1)

            attention(0)
            with link.loop(HEADS // 2 - 1, 14, first=1) as p:
                attention(p, before=p - 1)

            def merge(i, base_m, n0, between=lambda: None):
                m = base_m + 2 * i
                split(m + 1, 1, MB if n0 == 1 else KT)
                split(m + 2, 0)
                between()
                dve.wait_ge(units_done, 2 * m + 4)
                dve.wait_ge(bank_read[0], n0 * KT + MB + KT + 4 * 4 + i + 1 + FREE)
                link(dve.tensor_tensor(pt[:, :], psU[1][:, 0:TOK], gt[:, :], ALU.mult))
                mg = merged[:, ds(i, 1), :].rearrange("p a t -> p (a t)")
                dve.tensor_tensor(mg, mg, pt[:, :], ALU.add).then_inc(merge_made, 1)
                if n0 == 2:
                    dve.wait_ge(mg_hi, i + 1)
                    w = (slice(None), ds(i, 1), slice(None))
                    dve.tensor_tensor(ml[w].rearrange("p a t -> p (a t)"), mg,
                                      mh[w].rearrange("p a t -> p (a t)").bitcast(f32), ALU.subtract).then_inc(mg_lo, 1)

            merge(0, M_MM, 1, lambda: head_norm(HEADS // 2 - 1))
            merge(1, M_MM, 1)
            take_heads(HEADS // 2 - 1)
            with link.loop(KT - 2, 1, first=2) as i:
                merge(i, M_MM, 1)
            with link.loop(KT, 1) as i:
                merge(i, M_MD, 2)

            with dve.Fori(0, D // WIDE // 2) as g2:
                for k in range(2):
                    g = 2 * g2 + k

                    def take():
                        dve.wait_ge(res_in, 16 * NT)
                        for t in range(2):
                            r = res[:, t, ds(g * WIDE, WIDE)]
                            last = dve.scalar_tensor_tensor(r, r, ALPHA, psT[2 * k + t][:, :], ALU.mult, ALU.add,
                                                            accum_out=rowsum[:, t, ds(g, 1)])
                        last.then_inc(tok_read, 1)
                    wide(M_OUT + 4 * g, split, g, take)

            class Norm:

                def __init__(self, k, gain, bias):
                    self.k, self.gain, self.bias = k, gain, bias
                    dve.wait_ge((ln1_in, ln2_in)[k], 32)

                def mean(self, t):
                    link(dve.tensor_reduce(mom[:, 0, t:t + 1], rowsum[:, t, :], AX.X, ALU.add))
                    dve.tensor_scalar(nmom[:, t:t + 1], mom[:, 0, t:t + 1], -1.0 / D, None, ALU.mult).then_inc(ln_mean, 1)
                    dve.wait_ge(ln_mean, NT * self.k + t + 1)

                def centre(self, t):
                    dve.scalar_tensor_tensor(acc[:, t, :], res[:, t, :], nmom[:, t:t + 1], self.gain, ALU.add, ALU.mult)

                def variance(self, t):
                    dve.wait_ge(ln_act, 4 * self.k + 2 * t + 1)
                    dve.tensor_scalar(mom[:, 1, t:t + 1], mom[:, 1, t:t + 1], 1.0 / D, EPS, ALU.mult, ALU.add).then_inc(ln_dve, 1)

                def rstd(self, t):
                    dve.wait_ge(ln_act, 4 * self.k + 2 * t + 2)
                    link(dve.reciprocal(mom[:, 2, t:t + 1], mom[:, 2, t:t + 1]))

                def scale(self, t, half):
                    h = slice(half * D // 2, (half + 1) * D // 2)
                    dve.scalar_tensor_tensor(res[:, t, h], acc[:, t, h], mom[:, 2, t:t + 1], self.bias[:, h],
                                             ALU.mult, ALU.add).then_inc(ln_done, 1)

                def last_tile(self):
                    self.centre(1)
                    self.rstd(0)
                    self.scale(0, 0)
                    self.variance(1)
                    self.scale(0, 1)
                    self.rstd(1)
                    self.scale(1, 0)
                    self.scale(1, 1)

            dve.wait_ge(tok_read, MEM_W // WIDE + HEADS // 2 + D // WIDE + FREE)
            norm = Norm(0, hbuf[:, 0:8, :].rearrange("p a b -> p (a b)"), hbuf[:, 8:16, :].rearrange("p a b -> p (a b)"))
            norm.mean(0)
            norm.mean(1)
            norm.centre(0)
            norm.variance(0)
            norm.last_tile()
            for t in range(NT):
                for b in range(4):
                    dve.wait_ge(x1_hi, 4 * t + b + 1)
                    w = (slice(None), slice(4 * b, 4 * b + 4), slice(t * P, (t + 1) * P))
                    dve.tensor_tensor(x1l[w], psT[b][:, :].rearrange("p (k c) -> p k c", c=P), x1h[w].bitcast(f32),
                                      ALU.subtract).then_inc(x1_lo, 1)

            def top16(*rows):
                n = link.n
                for src, v, i, rest in rows:
                    settle(dve)
                    link.mark(dve.max(v[:, 0:8], src))
                for src, v, i, rest in rows:
                    n += 1
                    link.wait(n)
                    settle(dve)
                    link.mark(dve.match_replace(rest, v[:, 0:8], src, LOWEST))
                for src, v, i, rest in rows:
                    n += 1
                    link.wait(n)
                    settle(dve)
                    link.mark(dve.max(v[:, 8:16], rest))
                for src, v, i, rest in rows:
                    n += 1
                    link.wait(n)
                    settle(dve)
                    dve.max_index(i[:, 0:8], v[:, 0:8], src)
                    link.mark(dve.max_index(i[:, 8:16], v[:, 8:16], rest))
                link.wait(link.n)

            def best_keys(h, j):
                dve.wait_ge(top_done, 2 * h + j - 1 + FREE2)
                dve.wait_ge(key_score, 2 * h + j + 1 + FREE2)
                top16(*((psS[j][:, t * NK:(t + 1) * NK], stv[:, j, t, :], sti[:, j, t, :], left[:, j, t, :])
                        for t in range(NT)))
                for top, st in ((top_v, stv), (top_i, sti)):
                    last = dve.tensor_copy(top[:, ds(h, 1), j, :, :].rearrange("p a t r -> p (a t r)"),
                                           st[:, j, :, :].rearrange("p t r -> p (t r)"))
                last.then_inc(top_done, 1)

            split(M_WQ + 1, 1)
            split(M_WQ + 2, 0)
            best_keys(0, 0)
            with link.loop(PH - 2, 16, first=1) as h:
                m = M_WQ + 2 * h
                split(m + 1, 1)
                best_keys(h - 1, 1)
                split(m + 2, 0)
                best_keys(h, 0)
            split(M_EXP - 1, 1)
            best_keys(PH - 2, 1)
            split_turned(M_EXP, 0)
            best_keys(PH - 1, 0)
            best_keys(PH - 1, 1)
            dve.wait_ge(top_done, 2 * PH + FREE2)
            dve.wait_ge(consts, 4 + HALF_ROT + 4)

            def best_pairs(h):
                a_, b_ = (top_v[:, ds(h, 1), j, :, :].rearrange("p a t r -> p (a t) r") for j in range(2))
                link(dve.tensor_tensor(cand.rearrange("p t (a b) -> p t a b", b=TOPK),
                                       a_.unsqueeze(3).broadcast_to([P, NT, TOPK, TOPK]),
                                       b_.unsqueeze(2).broadcast_to([P, NT, TOPK, TOPK]), ALU.add))
                dve.wait_ge(best_exp, h + FREE)
                top16(*((cand[:, t, :], best[:, t, :], ci[:, t, :], cand2[:, t, :]) for t in range(NT)))
                dve.tensor_scalar(nbest[:, :], best[:, :, 0:1].rearrange("p t a -> p (t a)"), -1.0, None,
                                  ALU.mult).then_inc(best_made, 1)

            def picks(h):
                dve.tensor_single_scalar(ca[:, :, :], ci[:, :, :], 4, ALU.logical_shift_right)
                link(dve.tensor_single_scalar(cb[:, :, :], ci[:, :, :], TOPK - 1, ALU.bitwise_and))
                dve.tensor_copy(caf[:, 0, :, :], ca[:, :, :])
                link(dve.tensor_copy(caf[:, 1, :, :], cb[:, :, :]))
                dve.tensor_tensor(hit, caf[:, :, :, :].rearrange("p j t r -> p (j t) r").unsqueeze(3)
                                  .broadcast_to([P, 2 * NT, TOPK, TOPK]),
                                  iota16[:, :].unsqueeze(1).unsqueeze(1).broadcast_to([P, 2 * NT, TOPK, TOPK]),
                                  ALU.is_equal).then_inc(hit_made, 1)
                dve.wait_ge(best_exp, h + 1 + FREE)
                link(dve.reciprocal(rzb[:, :], zb[:, :]))
                for t in range(NT):
                    last = dve.tensor_scalar(pick[:, 2, t, ds(h * TOPK, TOPK)], eb[:, t, :], rzb[:, t:t + 1], None, ALU.mult)
                link(last)

            def pick_keys(h):
                dve.wait_ge(hit_keys, h + 1)
                link(dve.tensor_reduce(pick[:, 0:2, :, ds(h * TOPK, TOPK)].rearrange("p j t r -> p (j t) r"), hit, AX.X, ALU.add))

            def one_hots(step, b, k, for_act=False):
                tok = ds(k * GT, GT)
                dve.wait_ge(gate_mm, step - 1 + FREE2)
                if for_act:
                    dve.tensor_scalar(neg_i2[:, :], pickT[:, 1, tok], -1.0, None, ALU.mult).then_inc(neg_staged, 1)
                else:
                    dve.tensor_copy(i2s[b][:, :], pickT[:, 1, tok]).then_inc(i2_staged, 1)
                link(dve.tensor_tensor(mask[:, :, :], i1[:, tok].unsqueeze(2).broadcast_to([P, GT, GC]),
                                       keys[:, 0:GC].unsqueeze(1).broadcast_to([P, GT, GC]), ALU.is_equal))
                dve.tensor_tensor(one1[b][:, :, :, :], mask[:, :, :].unsqueeze(2).broadcast_to([P, GT, 3, GC]),
                                  gate3[:, :, tok].rearrange("p h t -> p t h").unsqueeze(3).broadcast_to([P, GT, 3, GC]),
                                  ALU.mult).then_inc(one1_made, 1)
                dve.wait_ge(one1_made, step + 1)

            def take_gates(step, b, k):
                dve.wait_ge(gate_mm, step + 1 + FREE2)
                for half in range(2):
                    last = dve.tensor_reduce(gbuf[:, :, ds(k * GT + half * GH, GH)],
                                             psS[half][:, 0:GH * 3 * GC].rearrange("p (k h c) -> p c k h", h=3, c=GC),
                                             AX.X, ALU.add)
                last.then_inc(gate_read, 1)

            def weigh(m, s, c, n):
                dve.wait_ge(w_lo, n + FREE)
                cc = (slice(None), ds(c, 1), slice(None))
                dve.tensor_tensor(wt[:, :], hbuf[cc].rearrange("p a t -> p (a t)"), gbuf[cc].rearrange("p a t -> p (a t)"),
                                  ALU.mult).then_inc(w_ready, 1)

            def split_w(s, n):
                dve.wait_ge(w_hi, n + 1)
                dve.tensor_tensor(wl[s][:, :], wt[:, :], wh[s][:, :].bitcast(f32), ALU.subtract).then_inc(w_lo, 1)

            for g in range(GROUPS):
                mu, mv_ = M_EXP + 2 * g * GC, M_EXP + (2 * g + 1) * GC
                if g == 0:
                    def choose(h, before=None):
                        split_turned(mu + 2 * h + 1, 1)
                        if before is not None:
                            pick_keys(before)
                        best_pairs(h)
                        split_turned(mu + 2 * h + 2, 0)
                        picks(h)

                    choose(0)
                    with link.loop(PH - 1, 14, first=1) as h:
                        choose(h, before=h - 1)
                    pick_keys(PH - 1)
                    dve.tensor_copy(rzb[:, 0:1], zb[:, 0:1]).then_inc(pick_made, 1)
                    dve.wait_ge(pickT_made, 2)
                    dve.tensor_copy(keys[:, :], iota[:, :])
                    dve.tensor_copy(i1[:, :], pickT[:, 0, :])
                    for n in range(3):
                        link(dve.tensor_copy(gate3[:, n, :], pickT[:, 2, :]))
                        if n < 2:
                            link(dve.tensor_tensor(pickT[:, 2, :], pickT[:, 2, :], gate3[:, n, :], ALU.subtract))

                    def round0(i, last=False):
                        for s in range(2):
                            k = (i - HALF0) * 4 + 2 * s
                            one_hots(k + 1, 1, k + 1, for_act=True)
                            if last and s == 1:
                                split(mv_, 0)
                                take_gates(k, 0, k)
                            else:
                                split_turned(mu + 2 * i + 1 + s, 1 - s)
                                take_gates(k, 0, k)
                                one_hots(k + 2, 0, k + 2)
                            take_gates(k + 1, 1, k + 1)

                    one_hots(0, 0, 0)
                    with link.loop(GC // 2 - 1 - HALF0, 4, first=HALF0) as i:
                        round0(i)
                    round0(GC // 2 - 1, last=True)
                else:
                    def round_(i, last=False):
                        for s in range(2):
                            k = 2 * i + s
                            if last and s == 1:
                                split(mv_, 0)
                            else:
                                one_hots(g * STEPS + k + 1, 1 - s, k + 1)
                                split_turned(mu + 2 * i + 1 + s, 1 - s)
                            take_gates(g * STEPS + k, s, k)

                    with link.loop(GC // 2 - 1, 2) as i:
                        round_(i)
                    round_(GC // 2 - 1, last=True)
                dve.wait_ge(bank_read[1], PAIRS + (g + 1) * (GC // 2) + FREE)
                dve.wait_ge(gate_read, (g + 1) * STEPS + FREE)
                weigh(mv_, 0, 0, g * GC)
                split_w(0, g * GC)

                def vpair(i, last=False):
                    m, n = mv_ + 2 * i, g * GC + 2 * i
                    weigh(m + 1, 1, 2 * i + 1, n + 1)
                    split(m + 1, 1)
                    split_w(1, n + 1)
                    if not last:
                        weigh(m + 2, 0, 2 * i + 2, n + 2)
                        split(m + 2, 0)
                        split_w(0, n + 2)

                with dve.Fori(0, GC // 2 - 1) as i:
                    vpair(i)
                if g + 1 < GROUPS:
                    link(dve.tensor_scalar(i1[:, :], i1[:, :], float(-GC), None, ALU.add))
                    one_hots((g + 1) * STEPS, 0, 0)
                vpair(GC // 2 - 1, last=True)
                for t in range(NT):
                    if t == 0:
                        dve.wait_ge(sum_made, g + 1)
                    else:
                        dve.wait_ge(units_done, 2 * (mv_ + GC))
                    for n in range(4):
                        w = (slice(None), t, slice(n * 512, (n + 1) * 512))
                        bank = ps[4 * t + n][:, :]
                        if g == 0:
                            dve.tensor_copy(acc[w], bank).then_inc(acc_read, 1)
                        elif g + 1 < GROUPS:
                            dve.tensor_tensor(acc[w], acc[w], bank, ALU.add).then_inc(acc_read, 1)
                        else:
                            if t == 0 and n == 0:
                                dve.wait_ge(res_added, 1)
                                norm = Norm(1, gbuf[:, 0:8, :].rearrange("p a b -> p (a b)"),
                                            gbuf[:, 8:16, :].rearrange("p a b -> p (a b)"))
                            dve.scalar_tensor_tensor(res[w], bank, 1.0, acc[w], ALU.mult, ALU.add,
                                                     accum_out=rowsum[:, t, n:n + 1]).then_inc(acc_read, 1)
                    if g + 1 == GROUPS:
                        dve.wait_ge(acc_read, 8 * g + 4 * (t + 1))
                        norm.mean(t)
                        if t == 0:
                            norm.centre(0)
                            norm.variance(0)
                dve.wait_ge(acc_read, 8 * (g + 1))
                if g + 1 < GROUPS:
                    split_turned(mv_ + GC, 0)
            norm.last_tile()

        @block.tensor
        def _(pe):
            def turn(src, bank, q, identity=ident):
                return pe.transpose(psT[bank][:, q * P:(q + 1) * P], src, identity[:, :])

            def unit(m, s, b, ah, al, kt, reads, taken=None, mid=lambda: None, mid_at=KT // 2, mem_before=False):
                pe.wait_ge(lo_made, (m + PRE) * 4 + 2)
                pe.wait_ge(taken or bank_read[b % 2], reads + FREE)
                w_h, w_l = k3(hi[s]), k3(lo[s])
                for k in range(kt):
                    if k == mid_at:
                        mid()
                    if k == KT // 2:
                        pe.wait_ge(lo_made, (m + PRE) * 4 + 4)
                    o = ps[b][:, 0:TOK]
                    one = pe.matmul(o, w_h[:, k, :], ah[:, k, :], start=k == 0, stop=False)
                    if mem_before and k == 0:
                        one.then_inc(units_done, 2)
                    pe.matmul(o, w_h[:, k, :], al[:, k, :], start=False, stop=False)
                    last = pe.matmul(o, w_l[:, k, :], ah[:, k, :], start=False, stop=k == kt - 1)
                    if k in (KT // 2 - 1, kt - 1):
                        last.then_inc(units_done, 1)

            def wide(m, ah, al, reads, after=lambda j: None, b=0):
                for j in range(4):
                    s = j % 2
                    w_h, w_l = w3(hi[s]), w3(lo[s])
                    for half in range(2):
                        pe.wait_ge(lo_made, (m + j + PRE) * 4 + 2 * (half + 1))
                        if j == 0 and half == 0:
                            pe.wait_ge(tok_read, reads + FREE)
                        for t in range(2):
                            for k in (2 * half, 2 * half + 1):
                                a_h = ah[:, KQ * j + k, t * P:(t + 1) * P]
                                a_l = al[:, KQ * j + k, t * P:(t + 1) * P]
                                o = psT[b + t][:, :]
                                pe.matmul(o, a_h, w_h[:, k, :], start=j == 0 and k == 0, stop=False)
                                pe.matmul(o, a_h, w_l[:, k, :], start=False, stop=False)
                                last = pe.matmul(o, a_l, w_h[:, k, :], start=False, stop=j == 3 and k == KQ - 1)
                        last.then_inc(units_done, 1)
                    after(j)

            def turn_rows(m, s, ready):
                pe.wait_ge(raw_in[s], (m + PRE - s) * 8 + 16)
                for b in range(4):
                    ready(b)
                    for q in range(4):
                        last = turn(raw[s][:, (4 * b + q) * P:(4 * b + q + 1) * P], b, q)
                    last.then_inc(turned, 1)

            def turn_vectors():
                pe.wait_ge(small_in, 9 * 16)
                pe.transpose(psS[0][:, 0:P], vrow[:, 0, :], ident[:, :])
                pe.transpose(psS[0][:, P:P + 98], vrow[0:98, 1, :], ident[0:98, 0:98])
                pe.matmul(psS[1][0:ROT, 0:1], ifr[0:1, :], ones1[0:1, 0:1], start=True, stop=True).then_inc(vec_turned, 1)

            pe.wait_ge(consts, 6 + HALF_ROT)
            turn_rows(-PRE, 0, lambda b: None)
            turn_rows(1 - PRE, 1, lambda b: pe.wait_ge(lo_made, b + 1))
            pe.wait_ge(lo_made, 8)
            def lru_products(r, b):
                pe.wait_ge(xc_made, 2 * r + b + 1)
                pe.wait_ge(lru_in, (2 * r + b + 1) * 32)
                pe.wait_ge(gates_read, r + FREE)
                for d in range(2):
                    for k in range(2):
                        last = pe.matmul(psT[2 * b + d][:, k * TOK:(k + 1) * TOK], lru_w[:, k, d, :], xc[:, b, :], start=True, stop=True)
                last.then_inc(lru_mm, 1)

            def lru_round(r, first=False):
                for b in range(2):
                    m = M_LRU + 4 * r + 2 * b
                    read = 0 if first else 2 * r + b - 1
                    if first and b == 1:
                        pe.wait_ge(set_act, 2)
                    unit(m, 0, 6 * b, xh, xl, KT, read)
                    if first and b == 0:
                        turn_vectors()
                    unit(m + 1, 1, 6 * b + 1, xh, xl, KT, read, mid=lambda: lru_products(r, b), mid_at=3 * KT // 4)

            lru_round(0, first=True)
            with pe.Fori(1, KT // 2) as r:
                lru_round(r)
            with pe.Fori(0, MB // 2 - 2) as i:
                for s in range(2):
                    unit(M_MQ + 2 * i + s, s, s, xh, xl, KT, KT + i)
            unit(M_MEM - 2, 0, 0, xh, xl, KT, KT + MB // 2 - 2)
            pe.wait_ge(gates_read, KT // 2 + FREE)
            turn_rows(M_MEM, 0, lambda b: None)
            unit(M_MEM - 1, 1, 1, xh, xl, KT, KT + MB // 2 - 2)
            unit(M_MEM + 1, 0, 0, xh, xl, KT, KT + MB // 2 - 1, mem_before=True,
                 mid=lambda: turn_rows(M_MEM + 2, 0, lambda b: pe.wait_ge(lo_made, (M_MEM + PRE) * 4 + b + 1)))
            unit(M_MEM + 3, 1, 1, xh, xl, KT, KT + MB // 2 - 1, mem_before=True)
            with pe.Fori(0, MB // 2) as i:
                for s in range(2):
                    unit(M_MK + 2 * i + s, s, s, memh, meml, KT, KT + MB // 2 + i)
            for g in range(MEM_W // WIDE):
                wide(M_MV + 4 * g, memh, meml, max(g - 1, 0), b=g % 2 * 2)
            rd = KT + MB
            pe.wait_ge(kv_made, 1)
            pe.wait_ge(summed, KT)
            pe.wait_ge(bank_read[1], rd + FREE)
            with pe.Fori(0, MEM_HEADS) as h:
                for k in range(4):
                    m = M_MA + 8 * h + 2 * k
                    unit(m, 0, 0, xh, xl, KT, rd + 4 * h + k)
                    if k == 0:
                        pe.wait_ge(staged, 2 * h + 2)
                        for t in range(NT):
                            for c in range(MC):
                                last = pe.matmul(psS[t][:, 0:MEM], mqs[:, c, t * P:(t + 1) * P],
                                                 mk[:, ds(h * MC + c, 1), :].rearrange("p a m -> p (a m)"),
                                                 start=c == 0, stop=c == MC - 1)
                        last.then_inc(mscore, 1)
                    if k == 2:
                        pe.wait_ge(mprob, 2 * h + 2)
                        for b in range(2):
                            for t in range(NT):
                                last = pe.transpose(psT[2][:, (2 * b + t) * P:(2 * b + t + 1) * P], pm[:, t, b * P:(b + 1) * P], ident[:, :])
                        last.then_inc(mturned, 1)
                    if k == 3:
                        pe.wait_ge(mpT, h + 1)
                        pe.wait_ge(mlo, MC * h + FREE)
                        for c in range(MC):
                            for b in range(2):
                                last = pe.matmul(psT[(0, 1, 3)[c]][:, 0:TOK], mvs[:, b, c * P:(c + 1) * P], pmT[:, b, :],
                                                 start=b == 0, stop=b == 1)
                        last.then_inc(mpv, 1)
                    unit(m + 1, 1, 1, brh, brl, KT, 4 * h + k, merge_made)
            merges = KT
            rd += KT
            pe.wait_ge(merge_made, KT + FREE)
            pe.wait_ge(mlo, MC * MEM_HEADS + FREE)

            def scores(p, hh):
                pe.wait_ge(rotated, 2 * p + hh + 1)
                if hh == 0:
                    pe.wait_ge(olo, 4 * p + FREE)
                for t in range(NT):
                    for j in range(2):
                        last = pe.matmul((psS, psT[2:4])[hh][t][:, j * TOK:(j + 1) * TOK], qk[:, 4 * hh + j, t * P:(t + 1) * P],
                                         qk[:, 4 * hh + 2 + j, :], start=True, stop=True)
                last.then_inc(score, 1)

            def turn_attn(p, hh):
                pe.wait_ge(attn, 2 * p + hh + 1)
                for b in range(2):
                    for t in range(NT):
                        last = pe.transpose(psS[hh][:, (2 * b + t) * P:(2 * b + t + 1) * P], ex[:, hh, t, 0, b * P:(b + 1) * P], ident[:, :])
                last.then_inc(aturned, 1)

            def values(p):
                pe.wait_ge(tok_read, MEM_W // WIDE + p + 1 + FREE)
                for hh in range(2):
                    pe.wait_ge(atT, 2 * p + hh + 1)
                    for t in range(NT):
                        for b in range(2):
                            last = pe.matmul(psT[2 + hh][:, t * VD:(t + 1) * VD], at[:, hh, b, t * P:(t + 1) * P],
                                             vv[:, b, hh * VD:(hh + 1) * VD], start=b == 0, stop=b == 1)
                    last.then_inc(pv, 1)

            def turn_heads(p):
                for hh in range(2):
                    pe.wait_ge(onorm, 2 * p + hh + 1)
                    for c in range(2):
                        for t in range(NT):
                            last = pe.transpose(psS[hh][:, (2 * c + t) * P:(2 * c + t + 1) * P], ex[:, hh, t, 0, c * P:(c + 1) * P], ident[:, :])
                    last.then_inc(oturned, 1)

            def attention(p, before=None):
                m = M_D + 12 * p
                for j in range(8):
                    unit(m + j, j % 2, j % 2, xh, xl, KT, rd - merges * (j % 2) + 4 * p + j // 2,
                         mid=(lambda: scores(p, 0)) if j == 6 else lambda: None)
                    if j == 0 and before is not None:
                        values(before)
                    if j == 3 and before is not None:
                        turn_heads(before)
                wide(m + 8, xh, xl, MEM_W // WIDE + p,
                     after=lambda j: (lambda: turn_attn(p, 0), lambda: scores(p, 1), lambda: None, lambda: turn_attn(p, 1))[j]())

            attention(0)
            with pe.Fori(1, HEADS // 2) as p:
                attention(p, before=p - 1)
            rd += 4 * (HEADS // 2)
            pe.wait_ge(bank_read[1], rd - merges + FREE)

            def merge_mem(i, between=lambda: None):
                unit(M_MM + 2 * i, 0, 0, xh, xl, KT, rd + i)
                between()
                unit(M_MM + 2 * i + 1, 1, 1, brmh, brml, MB, KT + i, merge_made)

            merge_mem(0, lambda: values(HEADS // 2 - 1))
            merge_mem(1)
            turn_heads(HEADS // 2 - 1)
            with pe.Fori(2, KT) as i:
                merge_mem(i)
            rd += KT
            pe.wait_ge(olo, 2 * HEADS + FREE)
            with pe.Fori(0, KT) as i:
                unit(M_MD + 2 * i, 0, 0, xh, xl, KT, rd + i)
                unit(M_MD + 2 * i + 1, 1, 1, brh, brl, KT, 2 * KT + i, merge_made)
            rd += KT
            merges = 3 * KT
            pe.wait_ge(merge_made, merges + FREE)
            pe.wait_ge(mg_lo, KT)
            with pe.Fori(0, D // WIDE // 2) as g2:
                for k in range(2):
                    g = 2 * g2 + k
                    wide(M_OUT + 4 * g, mh, ml, MEM_W // WIDE + HEADS // 2 - 1 + g, b=2 * k)
            pe.wait_ge(sub_in, 16)
            pe.wait_ge(tok_read, MEM_W // WIDE + HEADS // 2 + D // WIDE + FREE)
            keys_raw = gbuf[:, 0:8, :].rearrange("p a b -> p (a b)")
            for b in range(4):
                for q in range(4):
                    last = turn(keys_raw[:, (4 * b + q) * P:(4 * b + q + 1) * P], b, q)
                last.then_inc(sub_turned, 1)
            for t in range(NT):
                for b in range(4):
                    pe.wait_ge(ln_done, 2 * t + b // 2 + 1)
                    if t == 0:
                        pe.wait_ge(sk_made, b + 1)
                    else:
                        pe.wait_ge(x1_lo, b + 1)
                    for q in range(4):
                        last = turn(res[:, t, (4 * b + q) * P:(4 * b + q + 1) * P], b, q)
                    last.then_inc(x1_turned, 1)
            pe.wait_ge(x1_lo, 4 * NT)

            def turn_unit(m, s, first=False, taken=lambda b: None):
                pe.wait_ge(raw_in[s], (m + PRE - s) * 8 + 16)
                for b in range(4):
                    taken(b)
                    if not first:
                        pe.wait_ge(lo_made, (m + PRE - 1) * 4 + (b + 1))
                    for q in range(4):
                        last = turn(raw[s][:, (4 * b + q) * P:(4 * b + q + 1) * P], b, q)
                    last.then_inc(turned, 1)

            def score_keys(h, j):
                pe.wait_ge(top_done, 2 * h + j - 1 + FREE2)
                pe.wait_ge(bank_read[j], rd - merges * j + h + 1 + FREE)
                for t in range(NT):
                    last = pe.matmul(psS[j][:, t * NK:(t + 1) * NK], qT[:, j, t * P:(t + 1) * P],
                                     skT[:, ds(2 * h + j, 1), :].rearrange("p a n -> p (a n)"), start=True, stop=True)
                last.then_inc(key_score, 1)

            def queries(h, before=None, after=lambda: None):
                m = M_WQ + 2 * h
                unit(m, 0, 0, x1h, x1l, KT, rd + h, mid=lambda: before is not None and score_keys(before, 1))
                after()
                unit(m + 1, 1, 1, x1h, x1l, KT, rd - merges + h, mid=lambda: score_keys(h, 0))

            queries(0)
            with pe.Fori(1, PH - 1) as h:
                queries(h, h - 1)
            queries(PH - 1, PH - 2, lambda: turn_unit(M_EXP, 0, first=True))
            score_keys(PH - 1, 1)
            rd += PH

            for g in range(GROUPS):
                mu, mv_ = M_EXP + 2 * g * GC, M_EXP + (2 * g + 1) * GC
                r0 = rd + g * (GC // 2)

                def pair(i, last=False, mid=lambda i, s: None, extra=lambda i, s: None):
                    m = mu + 2 * i
                    turn_unit(m + 1, 1)
                    unit(m, 0, 0, x1h, x1l, KT, r0 + i, mid=lambda: mid(i, 0))
                    extra(i, 0)
                    if not last:
                        turn_unit(m + 2, 0)
                    unit(m + 1, 1, 1, x1h, x1l, KT, r0 - merges + i, mid=lambda: mid(i, 1))
                    extra(i, 1)

                def gate_step(step, b, made, made2):
                    pe.wait_ge(made, made2)
                    pe.wait_ge(one1_made, step + 1)
                    pe.wait_ge(gate_read, step + FREE)
                    for k in range(GT):
                        c = k % GH * 3 * GC
                        last = pe.matmul(psS[k // GH][:, c:c + 3 * GC], one2[b][:, k, :],
                                         one1[b][:, k, :, :].rearrange("p h c -> p (h c)"), start=True, stop=True)
                    last.then_inc(gate_mm, 1)

                def first_step(b):
                    def build(i, s):
                        k = (i - HALF0) * 4 + 2 * s + b
                        n = (i - HALF0) * 2 + s + 1
                        gate_step(k, b, *((one2_made, n), (act_one2, n + FREE))[b])
                    return build

                def one_step(i, s):
                    k = 2 * i + s
                    gate_step(g * STEPS + k, s, one2_made, (g - 1) * STEPS + STEPS // 2 + k + 1)

                if g == 0:
                    with pe.Fori(0, HALF0) as i:
                        pair(i)
                    pe.wait_ge(pick_made, 1)
                    for k in range(3):
                        dst = psS[1] if k < 2 else psS[0]
                        for t in range(NT):
                            c = ((k % 2) * NT + t) * P
                            last = pe.transpose(dst[:, c:c + P], pick[:, k, t, :], ident[:, :])
                    last.then_inc(pick_turned, 1)
                    pe.wait_ge(pickT_made, 2)
                    with pe.Fori(HALF0, GC // 2 - 1) as i:
                        pair(i, mid=first_step(0), extra=first_step(1))
                    pair(GC // 2 - 1, last=True, mid=first_step(0), extra=first_step(1))
                else:
                    with pe.Fori(0, GC // 2 - 1) as i:
                        pair(i, mid=one_step)
                    pair(GC // 2 - 1, last=True, mid=one_step)

                def v_products(s, t, half, first=False, final=False):
                    for part, (w, v) in enumerate(((wh[s], hi[s]), (wh[s], lo[s]), (wl[s], hi[s]))):
                        for c in (2 * half, 2 * half + 1):
                            last = pe.matmul(ps[4 * t + c][:, :], w[:, t * P:(t + 1) * P], v[:, c * 512:(c + 1) * 512],
                                             start=first and part == 0, stop=final and part == 2)
                    return last

                def v_unit(m, s, n, first=False):
                    for half in range(2):
                        pe.wait_ge(lo_made, (m + PRE) * 4 + 2 * (half + 1))
                        if half == 0:
                            pe.wait_ge(w_lo, n + 1 + FREE)
                        for t in range(NT):
                            last = v_products(s, t, half, first)
                        last.then_inc(units_done, 1)

                pe.wait_ge(gate_read, (g + 1) * STEPS + FREE)
                pe.wait_ge(bank_read[0], r0 + GC // 2 + FREE)
                pe.wait_ge(bank_read[1], r0 - merges + GC // 2 + FREE)
                v_unit(mv_, 0, g * GC, first=True)
                v_unit(mv_ + 1, 1, g * GC + 1)
                with pe.Fori(1, GC // 2 - 1) as i:
                    for s in range(2):
                        v_unit(mv_ + 2 * i + s, s, g * GC + 2 * i + s)
                for t in range(NT):
                    for s in range(2):
                        for half in range(2):
                            if t == 0:
                                pe.wait_ge(lo_made, (mv_ + GC - 2 + s + PRE) * 4 + 2 * (half + 1))
                                pe.wait_ge(w_lo, g * GC + GC - 1 + s + FREE)
                            last = v_products(s, t, half, final=s == 1)
                        if t == 1:
                            last.then_inc(units_done, 2)
                    if t == 0:
                        last.then_inc(sum_made, 1)
                if g + 1 < GROUPS:
                    turn_unit(mv_ + GC, 0, first=True, taken=lambda b: pe.wait_ge(acc_read, 8 * g + (3, 4, 5, 6)[b]))
                    pe.wait_ge(acc_read, 8 * (g + 1))


_INS = ['x', 'mem', 'positions', 'w_in', 'b_gate', 'conv_w', 'conv_b', 'lru_w_a', 'lru_b_a', 'lru_w_i', 'lru_b_i',
        'lru_lambda', 'diff_lambda', 'diff_subln', 'w_mem_kv', 'w_branch_lru', 'w_branch_diff', 'w_branch_mem',
        'w_out', 'ln1_g', 'ln1_b', 'peer_w_q', 'peer_sub_keys', 'peer_u', 'peer_v', 'ln2_g', 'ln2_b']


def kernel(**inputs):
    import numpy as _np
    import concourse.bacc as _bacc
    from concourse import mybir as _mybir
    from concourse.bass_utils import run_bass_kernel_spmd as _run

    nc = _bacc.Bacc("TRN2", target_bir_lowering=False, num_devices=1)
    arrays, args = {}, []
    for name in _INS:
        a = _np.ascontiguousarray(inputs[name])
        arrays[f"in_{name}"] = a
        args.append(nc.dram_tensor(f"in_{name}", a.shape, _mybir.dt.from_np(a.dtype), kind="ExternalInput").ap())
    o = nc.dram_tensor("out_x", (1, TOK, D), _mybir.dt.float32, kind="ExternalOutput").ap()
    layer(nc, *args, o)
    r = _run(nc, [arrays], core_ids=[0])
    return r.results[0]["out_x"]
```
